# Optimizing a Trainium2 kernel written in Bass

```python
import jax, jax.numpy as jnp
from jax import lax
import numpy as np
import math

D_MODEL = 1024
BATCH = 1
SEQ = 256
DEPTH = 1

HEAD_DIM = 64
GRID_W = 64
NA_HEADS = 8
NA_KH = 8
NA_KW = 16
DIL_CONFIGS = ((128, 1), (512, 4), (2048, 16))
DIL_HEADS_PER_GROUP = 4
DIL_HEADS = DIL_HEADS_PER_GROUP * len(DIL_CONFIGS)
DIL_QBLOCK = 64
ROT_DIM = HEAD_DIM // 4
ROPE_THETA = 500000.0
D_FF = -(-8 * D_MODEL // (3 * 256)) * 256
EPS = 1e-6
NEG_INF = -1e30
WA = NA_HEADS * HEAD_DIM
WB = DIL_HEADS * HEAD_DIM
WB_OUT = DIL_HEADS_PER_GROUP * HEAD_DIM
W_IN = 3 * WA + 3 * WB + 2 * D_MODEL


f32 = jnp.float32

def rms_norm(x, g):
    x32 = x.astype(f32)
    y = x32 * lax.rsqrt(jnp.mean(x32 * x32, axis=-1, keepdims=True) + EPS)
    return (y * g.astype(f32)).astype(x.dtype)

def partial_rotary(t, pos):
    half = ROT_DIM // 2
    inv_freq = ROPE_THETA ** (-(jnp.arange(half, dtype=f32) * 2.0) / ROT_DIM)
    ang = pos.astype(f32)[:, None] * inv_freq[None, :]
    cos = jnp.cos(ang)[None, :, None, :]
    sin = jnp.sin(ang)[None, :, None, :]
    x1 = t[..., :half].astype(f32)
    x2 = t[..., half:ROT_DIM].astype(f32)
    rot = jnp.concatenate([x1 * cos - x2 * sin, x2 * cos + x1 * sin], axis=-1).astype(t.dtype)
    return jnp.concatenate([rot, t[..., ROT_DIM:]], axis=-1)

def neighbourhood_attention(q, k, v, rpb):
    b, s, h, dh = q.shape
    rows = s // GRID_W
    kh = min(NA_KH, rows)
    qg = q.reshape(b, rows, GRID_W, h, dh)
    kg = k.reshape(b, rows, GRID_W, h, dh)
    vg = v.reshape(b, rows, GRID_W, h, dh)
    r = jnp.arange(rows)
    row_start = jnp.clip(r - kh // 2, 0, rows - kh)
    row_idx = row_start[:, None] + jnp.arange(kh)[None, :]
    kn = kg[:, row_idx].reshape(b, rows, kh * GRID_W, h, dh)
    vn = vg[:, row_idx].reshape(b, rows, kh * GRID_W, h, dh)
    col = jnp.arange(GRID_W)
    col_start = jnp.clip(col - NA_KW // 2, 0, GRID_W - NA_KW)
    col_mask = (col[None, :] >= col_start[:, None]) & (col[None, :] < col_start[:, None] + NA_KW)
    mask = jnp.broadcast_to(col_mask[:, None, :], (GRID_W, kh, GRID_W)).reshape(GRID_W, kh * GRID_W)
    row_off = row_idx - r[:, None] + (NA_KH - 1)
    col_off = jnp.clip(col[None, :] - col[:, None] + (NA_KW - 1), 0, 2 * NA_KW - 2)
    bias = rpb[:, row_off[:, None, :, None], col_off[None, :, None, :]]
    bias = bias.reshape(h, rows, GRID_W, kh * GRID_W).astype(f32)
    scores = jnp.einsum('brqhd,brkhd->bhrqk', qg, kn).astype(f32) * (dh ** -0.5) + bias[None]
    scores = jnp.where(mask, scores, NEG_INF)
    p = jax.nn.softmax(scores, axis=-1).astype(v.dtype)
    o = jnp.einsum('bhrqk,brkhd->brqhd', p, vn)
    return o.reshape(b, s, h * dh)

def dilated_window_attention(q, k, v, window, dilation):
    b, s, h, dh = q.shape
    half = (window // 2) // dilation
    seg = s // dilation

    def split(t):
        return t.reshape(b, seg, dilation, h, dh).transpose(0, 2, 1, 3, 4).reshape(b * dilation, seg, h, dh)

    qs, ks, vs = split(q), split(k), split(v)
    nb = -(-seg // DIL_QBLOCK)
    lp = nb * DIL_QBLOCK
    qs = jnp.pad(qs, ((0, 0), (0, lp - seg), (0, 0), (0, 0)))
    pad_k = ((0, 0), (half, lp - seg + half), (0, 0), (0, 0))
    kp, vp = jnp.pad(ks, pad_k), jnp.pad(vs, pad_k)
    span = DIL_QBLOCK + 2 * half
    key_idx = jnp.arange(nb)[:, None] * DIL_QBLOCK + jnp.arange(span)[None, :]
    kb = kp[:, key_idx]
    vb = vp[:, key_idx]
    qb = qs.reshape(-1, nb, DIL_QBLOCK, h, dh)
    qpos = jnp.arange(nb)[:, None] * DIL_QBLOCK + jnp.arange(DIL_QBLOCK)[None, :]
    kpos = key_idx - half
    rel = kpos[:, None, :] - qpos[:, :, None]
    mask = (jnp.abs(rel) <= half) & (kpos[:, None, :] >= 0) & (kpos[:, None, :] < seg)
    scores = jnp.einsum('nbqhd,nbkhd->nhbqk', qb, kb).astype(f32) * (dh ** -0.5)
    scores = jnp.where(mask[None, None], scores, NEG_INF)
    lse = jax.nn.logsumexp(scores, axis=-1)
    p = jnp.exp(scores - lse[..., None]).astype(v.dtype)
    o = jnp.einsum('nhbqk,nbkhd->nbqhd', p, vb).reshape(-1, lp, h, dh)[:, :seg]
    lse = lse.transpose(0, 2, 3, 1).reshape(-1, lp, h)[:, :seg]
    o = o.reshape(b, dilation, seg, h, dh).transpose(0, 2, 1, 3, 4).reshape(b, s, h, dh)
    lse = lse.reshape(b, dilation, seg, h).transpose(0, 2, 1, 3).reshape(b, s, h)
    return o, lse

def first_inputs(seed: int = 0) -> dict:
    key = jax.random.key(seed)
    ks = jax.random.split(key, 20)
    nrm = lambda k, shape, scale: jax.random.normal(k, shape, f32) * scale
    d = D_MODEL
    return {
        "x": nrm(ks[0], (BATCH, SEQ, d), 1.0),
        "c": nrm(ks[1], (BATCH, d), 1.0),
        "w_ada": nrm(ks[2], (DEPTH, d, 6 * d), 0.5 * d ** -0.5),
        "b_ada": nrm(ks[3], (DEPTH, 6 * d), 0.02),
        "g_norm1": 1.0 + nrm(ks[4], (DEPTH, d), 0.05),
        "g_norm2": 1.0 + nrm(ks[5], (DEPTH, d), 0.05),
        "w_in": nrm(ks[6], (DEPTH, d, W_IN), d ** -0.5),
        "b_gate": nrm(ks[7], (DEPTH, 2 * d), 0.02),
        "g_qa": 1.0 + nrm(ks[8], (DEPTH, HEAD_DIM), 0.05),
        "g_ka": 1.0 + nrm(ks[9], (DEPTH, HEAD_DIM), 0.05),
        "g_qb": 1.0 + nrm(ks[10], (DEPTH, HEAD_DIM), 0.05),
        "g_kb": 1.0 + nrm(ks[11], (DEPTH, HEAD_DIM), 0.05),
        "rpb": nrm(ks[12], (DEPTH, NA_HEADS, 2 * NA_KH - 1, 2 * NA_KW - 1), 0.1),
        "w_proj_a": nrm(ks[13], (DEPTH, WA, d), WA ** -0.5),
        "w_proj_b": nrm(ks[14], (DEPTH, WB_OUT, d), WB_OUT ** -0.5),
        "w_o": nrm(ks[15], (DEPTH, d, d), d ** -0.5),
        "w_ffn_in": nrm(ks[16], (DEPTH, d, 2 * D_FF), d ** -0.5),
        "w_ffn_out": nrm(ks[17], (DEPTH, D_FF, d), D_FF ** -0.5),
    }

def first_block(x, c, w_ada, b_ada, g_norm1, g_norm2, w_in, b_gate, g_qa, g_ka, g_qb, g_kb,
              rpb, w_proj_a, w_proj_b, w_o, w_ffn_in, w_ffn_out):
    b, s, _ = x.shape
    pos = jnp.arange(s)
    c_act = jax.nn.silu(c)
    split_at = [WA, 2 * WA, 3 * WA, 3 * WA + WB, 3 * WA + 2 * WB, 3 * WA + 3 * WB]
    for l in range(DEPTH):
        mod = c_act @ w_ada[l] + b_ada[l]
        sh1, sc1, gt1, sh2, sc2, gt2 = [m[:, None, :] for m in jnp.split(mod, 6, axis=-1)]

        h = rms_norm(x, g_norm1[l]) * (1.0 + sc1) + sh1
        proj = h @ w_in[l]
        qa, ka, va, qb, kb, vb, gates = jnp.split(proj, split_at, axis=-1)

        qa = rms_norm(qa.reshape(b, s, NA_HEADS, HEAD_DIM), g_qa[l])
        ka = rms_norm(ka.reshape(b, s, NA_HEADS, HEAD_DIM), g_ka[l])
        va = va.reshape(b, s, NA_HEADS, HEAD_DIM)
        o_a = neighbourhood_attention(qa, ka, va, rpb[l])

        qb = partial_rotary(rms_norm(qb.reshape(b, s, DIL_HEADS, HEAD_DIM), g_qb[l]), pos)
        kb = partial_rotary(rms_norm(kb.reshape(b, s, DIL_HEADS, HEAD_DIM), g_kb[l]), pos)
        vb = vb.reshape(b, s, DIL_HEADS, HEAD_DIM)
        outs, lses = [], []
        for g, (win, dil) in enumerate(DIL_CONFIGS):
            sl = slice(g * DIL_HEADS_PER_GROUP, (g + 1) * DIL_HEADS_PER_GROUP)
            o_g, lse_g = dilated_window_attention(qb[:, :, sl], kb[:, :, sl], vb[:, :, sl], win, dil)
            outs.append(o_g)
            lses.append(lse_g)
        wts = jax.nn.softmax(jnp.stack(lses, axis=0), axis=0)
        o_b = jnp.einsum('gbsh,gbshd->bshd', wts.astype(vb.dtype), jnp.stack(outs, axis=0))
        o_b = o_b.reshape(b, s, WB_OUT)

        gate_a, gate_b = jnp.split(jax.nn.sigmoid(gates + b_gate[l]), 2, axis=-1)
        merged = gate_a * (o_a @ w_proj_a[l]) + gate_b * (o_b @ w_proj_b[l])
        x = x + gt1 * (merged @ w_o[l])

        h2 = rms_norm(x, g_norm2[l]) * (1.0 + sc2) + sh2
        a, up = jnp.split(h2 @ w_ffn_in[l], 2, axis=-1)
        x = x + gt2 * ((jax.nn.silu(a) * up) @ w_ffn_out[l])
    return x


DEPTH_2 = 2

D_FF_2 = 2816
CONV_K = 4
SSM_EXPAND = 2
SSM_INNER = SSM_EXPAND * D_MODEL
SSM_HEAD_DIM = 64
SSM_HEADS = SSM_INNER // SSM_HEAD_DIM
SSM_GROUPS = 4
SSM_STATE = 128
SSM_CONV_DIM = SSM_INNER + 2 * SSM_GROUPS * SSM_STATE
SSM_CHUNK = 128
DN_HEADS = 8
DN_HEAD_K = 128
DN_HEAD_V = 128
DN_K_DIM = DN_HEADS * DN_HEAD_K
DN_V_DIM = DN_HEADS * DN_HEAD_V
DN_CONV_DIM = 2 * DN_K_DIM + DN_V_DIM
DN_CHUNK = 64
IN_SPLIT_SIZES = (SSM_INNER, SSM_CONV_DIM, SSM_HEADS,
                  DN_CONV_DIM, DN_V_DIM, DN_HEADS, DN_HEADS,
                  D_MODEL, D_MODEL)
IN_DIM = sum(IN_SPLIT_SIZES)


def rms_norm_2(x, w):
    xf = x.astype(jnp.float32)
    y = xf * lax.rsqrt(jnp.mean(xf * xf, axis=-1, keepdims=True) + EPS)
    return (y * w.astype(jnp.float32)).astype(x.dtype)

def l2_norm(x):
    xf = x.astype(jnp.float32)
    return xf * lax.rsqrt(jnp.sum(xf * xf, axis=-1, keepdims=True) + EPS)

def swiglu(x, w_in, w_out):
    gate, up = jnp.split(x @ w_in, 2, axis=-1)
    return (jax.nn.silu(gate) * up) @ w_out

def causal_depthwise_conv(x, w, bias=None):
    K, C = w.shape
    y = lax.conv_general_dilated(
        x, w[:, None, :].astype(x.dtype), window_strides=(1,), padding=[(K - 1, 0)],
        dimension_numbers=("NWC", "WIO", "NWC"), feature_group_count=C)
    if bias is not None:
        y = y + bias.astype(x.dtype)
    return y

def ssd_chunked(x, dt, a, Bm, Cm):
    b, S, H, P = x.shape
    G, N = Bm.shape[2], Bm.shape[3]
    hg = H // G
    L = SSM_CHUNK
    nc = S // L
    f32 = jnp.float32
    xdt = (x.astype(f32) * dt[..., None]).reshape(b, nc, L, G, hg, P)
    log_a = (dt * a).reshape(b, nc, L, G, hg)
    Bc = Bm.astype(f32).reshape(b, nc, L, G, N)
    Cc = Cm.astype(f32).reshape(b, nc, L, G, N)
    a_cum = jnp.cumsum(log_a, axis=2)
    causal = jnp.tril(jnp.ones((L, L), dtype=bool))[None, None, :, :, None, None]
    seg = a_cum[:, :, :, None] - a_cum[:, :, None, :]
    decay = jnp.where(causal, jnp.exp(jnp.where(causal, seg, 0.0)), 0.0)
    cb = jnp.einsum("bclgn,bcsgn->bclsg", Cc, Bc)
    y_diag = jnp.einsum("bclsg,bclsgh,bcsghp->bclghp", cb, decay, xdt)
    decay_to_end = jnp.exp(a_cum[:, :, -1:] - a_cum)
    chunk_states = jnp.einsum("bclgn,bclgh,bclghp->bcghpn", Bc, decay_to_end, xdt)
    chunk_decay = jnp.exp(a_cum[:, :, -1])

    def step(state, inp):
        cs, cd = inp
        return state * cd[..., None, None] + cs, state

    s0 = jnp.zeros((b, G, hg, P, N), f32)
    _, states_in = lax.scan(step, s0, (jnp.moveaxis(chunk_states, 1, 0), jnp.moveaxis(chunk_decay, 1, 0)))
    states_in = jnp.moveaxis(states_in, 0, 1)
    y_off = jnp.einsum("bclgn,bcghpn,bclgh->bclghp", Cc, states_in, jnp.exp(a_cum))
    return (y_diag + y_off).reshape(b, S, H, P)

def gated_delta_rule_chunked(q, k, v, g, beta):
    b, S, H, dk = q.shape
    dv = v.shape[-1]
    C = DN_CHUNK
    n = S // C
    f32 = jnp.float32

    def chunks(t):
        return jnp.moveaxis(t.astype(f32).reshape(b, n, C, *t.shape[2:]), 2, 3)

    q, k, v, g, beta = (chunks(t) for t in (q, k, v, g, beta))
    G = jnp.cumsum(g, axis=-1)
    incl = jnp.tril(jnp.ones((C, C), dtype=bool))
    strict = jnp.tril(jnp.ones((C, C), dtype=bool), -1)
    diff = G[..., :, None] - G[..., None, :]
    decay = jnp.where(incl, jnp.exp(jnp.where(incl, diff, 0.0)), 0.0)
    kb = k * beta[..., None]
    M = jnp.where(strict, jnp.einsum("bnhid,bnhjd->bnhij", kb, k) * decay, 0.0)
    eye = jnp.eye(C, dtype=f32)
    rhs = jnp.concatenate([v * beta[..., None], kb * jnp.exp(G)[..., None]], axis=-1)
    sol = lax.linalg.triangular_solve(eye + M, rhs, left_side=True, lower=True, unit_diagonal=True)
    u, w = sol[..., :dv], sol[..., dv:]
    a_qk = jnp.einsum("bnhid,bnhjd->bnhij", q, k) * decay
    q_dec = q * jnp.exp(G)[..., None]
    g_last = G[..., -1]
    k_dec = k * jnp.exp(g_last[..., None] - G)[..., None]

    def step(state, inp):
        q_c, a_c, u_c, w_c, k_c, gl = inp
        v_new = u_c - jnp.einsum("bhck,bhkv->bhcv", w_c, state)
        o = jnp.einsum("bhck,bhkv->bhcv", q_c, state) + jnp.einsum("bhij,bhjv->bhiv", a_c, v_new)
        state = state * jnp.exp(gl)[..., None, None] + jnp.einsum("bhck,bhcv->bhkv", k_c, v_new)
        return state, o

    xs = tuple(jnp.moveaxis(t, 1, 0) for t in (q_dec, a_qk, u, w, k_dec, g_last))
    s0 = jnp.zeros((b, H, dk, dv), f32)
    _, o = lax.scan(step, s0, xs)
    o = jnp.moveaxis(jnp.moveaxis(o, 0, 1), 2, 3)
    return o.reshape(b, S, H, dv)

def mamba2_branch(z, xbc, dt_raw, conv_w, conv_b, dt_bias, a_log, d_skip, norm_w):
    b, S, _ = xbc.shape
    f32 = jnp.float32
    xbc = jax.nn.silu(causal_depthwise_conv(xbc, conv_w, conv_b))
    xs, Bm, Cm = jnp.split(xbc, [SSM_INNER, SSM_INNER + SSM_GROUPS * SSM_STATE], axis=-1)
    xs = xs.reshape(b, S, SSM_HEADS, SSM_HEAD_DIM)
    Bm = Bm.reshape(b, S, SSM_GROUPS, SSM_STATE)
    Cm = Cm.reshape(b, S, SSM_GROUPS, SSM_STATE)
    dt = jax.nn.softplus(dt_raw.astype(f32) + dt_bias.astype(f32))
    a = -jnp.exp(a_log.astype(f32))
    y = ssd_chunked(xs, dt, a, Bm, Cm) + xs.astype(f32) * d_skip.astype(f32)[:, None]
    yg = (y.reshape(b, S, SSM_INNER) * jax.nn.silu(z.astype(f32))).reshape(b, S, SSM_GROUPS, -1)
    yg = yg * lax.rsqrt(jnp.mean(yg * yg, axis=-1, keepdims=True) + EPS)
    return (yg.reshape(b, S, SSM_INNER) * norm_w.astype(f32)).astype(z.dtype)

def deltanet_branch(qkv, z, b_raw, a_raw, conv_w, dt_bias, a_log, norm_w):
    b, S, _ = qkv.shape
    f32 = jnp.float32
    qkv = jax.nn.silu(causal_depthwise_conv(qkv, conv_w))
    q, k, v = jnp.split(qkv, [DN_K_DIM, 2 * DN_K_DIM], axis=-1)
    q = l2_norm(q.reshape(b, S, DN_HEADS, DN_HEAD_K)) * (DN_HEAD_K ** -0.5)
    k = l2_norm(k.reshape(b, S, DN_HEADS, DN_HEAD_K))
    v = v.reshape(b, S, DN_HEADS, DN_HEAD_V)
    beta = jax.nn.sigmoid(b_raw.astype(f32))
    g = -jnp.exp(a_log.astype(f32)) * jax.nn.softplus(a_raw.astype(f32) + dt_bias.astype(f32))
    o = gated_delta_rule_chunked(q, k, v, g, beta)
    o = o * lax.rsqrt(jnp.mean(o * o, axis=-1, keepdims=True) + EPS) * norm_w.astype(f32)
    o = o * jax.nn.silu(z.astype(f32).reshape(b, S, DN_HEADS, DN_HEAD_V))
    return o.reshape(b, S, DN_V_DIM).astype(z.dtype)

def second_inputs(seed: int = 0) -> dict:
    key = jax.random.key(seed)
    k = jax.random.split(key, 23)
    f32 = jnp.float32

    def dense(kk, shape, fan_in):
        return jax.random.normal(kk, shape, f32) * fan_in ** -0.5

    def gain(kk, shape):
        return 1.0 + 0.02 * jax.random.normal(kk, shape, f32)

    def dt_bias(kk, shape):
        u = jax.random.uniform(kk, shape, f32)
        dt = jnp.exp(u * (math.log(0.1) - math.log(1e-3)) + math.log(1e-3))
        return dt + jnp.log(-jnp.expm1(-dt))

    def a_log(kk, shape):
        return jnp.log(jax.random.uniform(kk, shape, f32, 1.0, 16.0))

    L = DEPTH_2
    return {
        "x": jax.random.normal(k[0], (BATCH, SEQ, D_MODEL), f32),
        "ffn1_norm": gain(k[1], (L, D_MODEL)),
        "ffn1_w_in": dense(k[2], (L, D_MODEL, 2 * D_FF_2), D_MODEL),
        "ffn1_w_out": dense(k[3], (L, D_FF_2, D_MODEL), D_FF_2),
        "mix_norm": gain(k[4], (L, D_MODEL)),
        "w_in": dense(k[5], (L, D_MODEL, IN_DIM), D_MODEL),
        "ssm_conv_w": dense(k[6], (L, CONV_K, SSM_CONV_DIM), CONV_K),
        "ssm_conv_b": 0.02 * jax.random.normal(k[7], (L, SSM_CONV_DIM), f32),
        "ssm_dt_bias": dt_bias(k[8], (L, SSM_HEADS)),
        "ssm_a_log": a_log(k[9], (L, SSM_HEADS)),
        "ssm_d": 1.0 + 0.1 * jax.random.normal(k[10], (L, SSM_HEADS), f32),
        "ssm_norm": gain(k[11], (L, SSM_INNER)),
        "ssm_w_branch": dense(k[12], (L, SSM_INNER, D_MODEL), SSM_INNER),
        "dn_conv_w": dense(k[13], (L, CONV_K, DN_CONV_DIM), CONV_K),
        "dn_dt_bias": dt_bias(k[14], (L, DN_HEADS)),
        "dn_a_log": a_log(k[15], (L, DN_HEADS)),
        "dn_norm": gain(k[16], (L, DN_HEAD_V)),
        "dn_w_branch": dense(k[17], (L, DN_V_DIM, D_MODEL), DN_V_DIM),
        "w_out": dense(k[18], (L, D_MODEL, D_MODEL), D_MODEL),
        "ffn2_norm": gain(k[19], (L, D_MODEL)),
        "ffn2_w_in": dense(k[20], (L, D_MODEL, 2 * D_FF_2), D_MODEL),
        "ffn2_w_out": dense(k[21], (L, D_FF_2, D_MODEL), D_FF_2),
        "final_norm": gain(k[22], (D_MODEL,)),
    }

def second_block(x, ffn1_norm, ffn1_w_in, ffn1_w_out, mix_norm, w_in, ssm_conv_w, ssm_conv_b,
              ssm_dt_bias, ssm_a_log, ssm_d, ssm_norm, ssm_w_branch, dn_conv_w, dn_dt_bias,
              dn_a_log, dn_norm, dn_w_branch, w_out, ffn2_norm, ffn2_w_in, ffn2_w_out, final_norm):
    split_points = [int(p) for p in np.cumsum(IN_SPLIT_SIZES)[:-1]]
    h = x
    for l in range(DEPTH_2):
        h = h + 0.5 * swiglu(rms_norm_2(h, ffn1_norm[l]), ffn1_w_in[l], ffn1_w_out[l])
        u = rms_norm_2(h, mix_norm[l])
        (z_s, xbc, dt_s, qkv, z_d, b_d, a_d, gate_s, gate_d) = jnp.split(u @ w_in[l], split_points, axis=-1)
        y_s = mamba2_branch(z_s, xbc, dt_s, ssm_conv_w[l], ssm_conv_b[l], ssm_dt_bias[l],
                            ssm_a_log[l], ssm_d[l], ssm_norm[l])
        y_d = deltanet_branch(qkv, z_d, b_d, a_d, dn_conv_w[l], dn_dt_bias[l],
                              dn_a_log[l], dn_norm[l])
        merged = (jax.nn.sigmoid(gate_s) * (y_s @ ssm_w_branch[l])
                  + jax.nn.sigmoid(gate_d) * (y_d @ dn_w_branch[l]))
        h = h + merged @ w_out[l]
        h = h + 0.5 * swiglu(rms_norm_2(h, ffn2_norm[l]), ffn2_w_in[l], ffn2_w_out[l])
    return rms_norm_2(h, final_norm)


def setup_inputs(seed=0):
    out = dict(first_inputs(seed))
    for name, value in second_inputs(seed + 1).items():
        if name != "x":
            out[name + "_2"] = value
    return out


def reference(
    x, c, w_ada, b_ada, g_norm1, g_norm2, w_in, b_gate, g_qa, g_ka, g_qb, g_kb, rpb, w_proj_a,
    w_proj_b, w_o, w_ffn_in, w_ffn_out, ffn1_norm_2, ffn1_w_in_2, ffn1_w_out_2, mix_norm_2,
    w_in_2, ssm_conv_w_2, ssm_conv_b_2, ssm_dt_bias_2, ssm_a_log_2, ssm_d_2, ssm_norm_2,
    ssm_w_branch_2, dn_conv_w_2, dn_dt_bias_2, dn_a_log_2, dn_norm_2, dn_w_branch_2, w_out_2,
    ffn2_norm_2, ffn2_w_in_2, ffn2_w_out_2, final_norm_2,
):
    x = first_block(
        x, c, w_ada, b_ada, g_norm1, g_norm2, w_in, b_gate, g_qa, g_ka, g_qb, g_kb, rpb,
        w_proj_a, w_proj_b, w_o, w_ffn_in, w_ffn_out,
    )
    return second_block(
        x, ffn1_norm_2, ffn1_w_in_2, ffn1_w_out_2, mix_norm_2, w_in_2, ssm_conv_w_2,
        ssm_conv_b_2, ssm_dt_bias_2, ssm_a_log_2, ssm_d_2, ssm_norm_2, ssm_w_branch_2,
        dn_conv_w_2, dn_dt_bias_2, dn_a_log_2, dn_norm_2, dn_w_branch_2, w_out_2, ffn2_norm_2,
        ffn2_w_in_2, ffn2_w_out_2, final_norm_2,
    )


_drawn_inputs = setup_inputs


def setup_inputs(seed=0):
    import zlib

    import numpy as np

    out = dict(_drawn_inputs(seed))
    spreads = {}
    factors = {'g_norm1': 8.0,
     'b_gate': 8.0,
     'g_qa': 8.0,
     'g_ka': 8.0,
     'g_qb': 8.0,
     'g_kb': 8.0,
     'rpb': 8.0,
     'ffn1_norm_2': 4.05,
     'ssm_conv_b_2': 3.076,
     'ssm_norm_2': 19.801,
     'dn_norm_2': 30.022,
     'ffn2_norm_2': 5.681,
     'final_norm_2': 8.712,
     'g_norm2': 3.449}
    for name, (base, spread) in spreads.items():
        noise = np.random.default_rng([zlib.crc32(name.encode()), seed]).standard_normal(out[name].shape)
        drawn = base * np.exp(spread * noise) if base else spread * noise
        out[name] = __import__('jax').numpy.asarray(drawn.astype(out[name].dtype))
    for name, factor in factors.items():
        out[name] = (out[name] * factor).astype(out[name].dtype)
    return out
```

```python
import concourse.bass as bass
from concourse import mybir
from contextlib import ExitStack
import numpy as np

F32 = mybir.dt.float32
ACT = mybir.ActivationFunctionType
ALU = mybir.AluOpType
AX = mybir.AxisListType

P = 128
S = 256
D = 1024
KT = D // P
HD = 64
FF = 2816
HID_PAIRS = FF // (2 * P)
LAYERS = 2
EPS = 1e-6
NEG = -1e30

QA, KA, QB, KB, GATE = 0, 4, 8, 14, 20
V_COLS = 512 + 768
GRID_W, NA_KH, NA_KW = 64, 8, 16
NA_HEADS, DIL_SLOTS, DIL_GROUPS = 8, 4, 3
NA_UNITS, DIL_UNITS = 2 * NA_HEADS, 2 * DIL_SLOTS
UNITS = NA_UNITS + DIL_UNITS

XBC_TILES, QKV_TILES, ZS_TILES, ZD_TILES = 24, 24, 16, 8
CONV_TILES = XBC_TILES + QKV_TILES
B_TILE, C_TILE = 16, 20
GROUPS = 4
SSM_HEADS = 32
DN_HEADS = 8
SMALL = 48
SP_COLS = 40

PANEL = 2048
RING = 6
B1_ADA, B1_WIDE, B1_V, B1_PROJ, B1_WO = 24, 18, 5, 3, 4
FFN_PANELS = 3 * HID_PAIRS
Q_WIDE1 = B1_ADA
Q_V = Q_WIDE1 + B1_WIDE
Q_PROJ1 = Q_V + B1_V
Q_WO = Q_PROJ1 + B1_PROJ
Q_FFN0 = Q_WO + B1_WO
Q_LAYERS = Q_FFN0 + FFN_PANELS
L_CONV = CONV_TILES // 2
L_ZS, L_ZD, L_GATES = ZS_TILES // 2, ZD_TILES // 2, KT
L_WIDE = L_CONV + L_ZS + L_ZD + L_GATES
L_PROJ, L_WOUT = 12, 4
LQ_FFN1 = 0
LQ_WIDE = LQ_FFN1 + FFN_PANELS
LQ_PROJ = LQ_WIDE + L_WIDE
LQ_WOUT = LQ_PROJ + L_PROJ
LQ_FFN2 = LQ_WOUT + L_WOUT
L_PANELS = LQ_FFN2 + FFN_PANELS
N_PANELS = Q_LAYERS + LAYERS * L_PANELS
assert L_PANELS % RING == 0 and Q_FFN0 % RING == 0 and B1_ADA % RING == 0 and B1_WIDE % RING == 0
WIDE0 = B1_WIDE + B1_V

def columns(sizes):
    at, out = 0, {}
    for name, n in sizes:
        out[name] = (at, at + n)
        at += n
    return out, at


PACK1, PACK1_N = columns([("c", 8), ("b_ada", 48), ("g1", 8), ("g2", 8), ("b_gate", 16), ("final", 8),
                          ("g_qa", 1), ("g_ka", 1), ("g_qb", 1), ("g_kb", 1)])
PACK2, PACK2_N = columns([("ffn1", 8), ("mix", 8), ("ffn2", 8), ("conv_w", 4 * CONV_TILES), ("conv_b", CONV_TILES),
                          ("ssm_norm", 16), ("ssm_d", 16), ("dn_norm", 1), ("small_b", SMALL), ("a_log", SP_COLS),
                          ("small_w", KT * SMALL)])
LEVELS = 6
CONSTS, CONSTS_N = columns([("ident", P), ("cum128", P), ("cum64", P), ("strict64", P), ("same64", P),
                            ("half0", P), ("half1", P), ("levels", LEVELS * P)])
ROPES, ROPES_N = columns([("head64", P), ("swap", P), ("cos", S), ("sin", S), ("dil", DIL_GROUPS * 2 * S)])

DVE_B1, DVE_LAYER = 256, 512


def build_program(nc, w_stream, x_t, pack1, pack2, consts, ropes, na_bias, out_t):
    with ExitStack() as ctx:
        def sb(name, shape):
            return ctx.enter_context(nc.sbuf_tensor(name, shape, F32))

        def sem(name):
            return ctx.enter_context(nc.semaphore(name))

        ring = sb("ring", [P, RING, PANEL])
        H = sb("H", [P, KT, S])
        U = sb("U", [P, KT, S])
        SQ = sb("SQ", [P, KT * S])
        RMS = sb("RMS", [P, 512])
        RSTD = sb("RSTD", [P, 512])
        PK1 = sb("PK1", [P, PACK1_N])
        PK2 = sb("PK2", [P, PACK2_N])
        CON = sb("CON", [P, CONSTS_N])
        MEAN_D = sb("MEAN_D", [P, P])
        MEAN_G = sb("MEAN_G", [P, P])
        MEAN_V = sb("MEAN_V", [P, P])
        ONES = sb("ONES", [P, P])
        EPST = sb("EPST", [P, 1])
        XPAD = sb("XPAD", [P, 2, 2, S + 3])
        ARENA_N = (CONV_TILES + ZS_TILES) * S + 10752
        ARENA = sb("ARENA", [P, ARENA_N])

        taken = [0]

        def region(n):
            taken[0] += n
            assert taken[0] <= ARENA_N, taken
            return ARENA[:, taken[0] - n:taken[0]]

        FFN_AT = ARENA_N - 2048
        SG = ARENA[:, FFN_AT:FFN_AT + 1024].rearrange("p (b n) -> p b n", b=2)
        HID = ARENA[:, FFN_AT + 1024:FFN_AT + 2048].rearrange("p (b n) -> p b n", b=2)

        PROJ = region(36 * S).rearrange("p (t n) -> p t n", t=36)
        VT = region(2 * V_COLS).rearrange("p (t n) -> p t n", t=2)
        BIAS = region(NA_UNITS * S).rearrange("p (u n) -> p u n", u=NA_UNITS)
        ROP = region(ROPES_N)
        SC = region(2 * 768).rearrange("p (b n) -> p b n", b=2)
        PR = region(2 * 768).rearrange("p (b n) -> p b n", b=2)
        PT = region(2 * 768).rearrange("p (b n) -> p b n", b=2)
        NMAX = region(2 * UNITS)
        DEN = region(UNITS)
        RDEN = region(UNITS)
        OTOK = region(2 * 768).rearrange("p (t n) -> p t n", t=2)
        RSH_AT = taken[0] - 2 * 768 - 4 * UNITS - 3 * 2 * 768
        RSH = ARENA[:, RSH_AT:RSH_AT + 10 * 512].rearrange("p (t n) -> p t n", t=10)
        OT = region(6 * S).rearrange("p (t n) -> p t n", t=6)
        MOD = sb("MOD", [P, 48])
        CACT = sb("CACT", [P, 8])
        GS = sb("GS", [P, 24])

        taken[0] = 0
        CONV = region(CONV_TILES * S).rearrange("p (t n) -> p t n", t=CONV_TILES)
        ZS = region(ZS_TILES * S).rearrange("p (t n) -> p t n", t=ZS_TILES)
        TMP_AT = taken[0]
        QKV = CONV[:, XBC_TILES:, :]
        ZD = CONV[:, B_TILE:B_TILE + ZD_TILES, :]
        GT = QKV[:, DN_HEADS:DN_HEADS + 2 * KT, :]
        CACC = ARENA[:, TMP_AT:TMP_AT + 1024].rearrange("p (b t n) -> p b t n", b=2, t=2)
        SMX = sb("SMX", [P, 8, 2 * SMALL])
        SPL = sb("SPL", [P, 2, SP_COLS])
        LOGA = sb("LOGA", [P, 2, SP_COLS])
        BETA = sb("BETA", [P, 2, DN_HEADS])
        CUM = sb("CUM", [P, 160])
        CUM_A = CUM[:, 0:64].rearrange("p (t h) -> p t h", t=2)
        CUM_G = CUM[:, 64:80].rearrange("p (t h) -> p t h", t=2)
        LAST_G = CUM[:, 80:96].rearrange("p (t h) -> p t h", t=2)
        LAST_A = CUM[:, 96:128]
        LAST_C = CUM[:, 128:160].rearrange("p (c h) -> p c h", c=4)
        ECUM = sb("ECUM", [P, 128])
        END_A = ECUM[:, 0:32]
        END_G = ECUM[:, 32:48].rearrange("p (t h) -> p t h", t=2)
        BEG = ECUM[:, 48:64].rearrange("p (t h) -> p t h", t=2)
        EXP_C = ECUM[:, 64:96].rearrange("p (c h) -> p c h", c=4)
        XDT = region(2 * 2048).rearrange("p (t n) -> p t n", t=2)
        STATE = region(2048)
        CBM = region(2 * 512).rearrange("p (t n) -> p t n", t=2)
        BTOK = region(512)
        SEG = region(2 * 512).rearrange("p (b n) -> p b n", b=2)
        MIX = region(2 * 512).rearrange("p (b n) -> p b n", b=2)
        CDEC = region(2 * 512).rearrange("p (b n) -> p b n", b=2)
        XEND = SQ
        taken[0] = TMP_AT
        KBG = region(1024)
        KDEC = region(1024)
        VB = region(1024)
        MT = region(1024)
        AQK = region(1024)
        TI = region(1024)
        TT = region(1024)
        UB = region(1024)
        DEC = region(1024)
        DCY = region(1024)
        ST = SQ[:, 0:1024]
        CS = SQ[:, 1024:2048]
        WT = UB

        def ROOT(pr):
            return (DEC, DCY)[pr % 4 // 2][:, pr % 2 * 512:pr % 2 * 512 + 512]

        VN = MT

        bank = [ctx.enter_context(nc.psum_tensor(f"bank{i}", [P, 512], F32)) for i in range(8)]

        panel_loaded = [sem(f"panel_loaded{i}") for i in range(RING)]
        panel_used = sem("panel_used")
        x_loaded, pack1_loaded, consts_loaded = sem("x_loaded"), sem("pack1_loaded"), sem("consts_loaded")
        bias_loaded, ropes_loaded, pack2_loaded = sem("bias_loaded"), sem("ropes_loaded"), sem("pack2_loaded")
        fills_done = sem("fills_done")
        out_stored = sem("out_stored")
        dve_done = sem("dve_done")
        residual_ready, squares_ready, sumsq_ready = sem("residual_ready"), sem("squares_ready"), sem("sumsq_ready")
        rms_ready, u_ready = sem("rms_ready"), sem("u_ready")
        wide_free = sem("wide_free")
        conv_step, conv_ready = sem("conv_step"), sem("conv_ready")
        gate_act_ready, hidden_ready = sem("gate_act_ready"), sem("hidden_ready")
        c_ready, ada_copied = sem("c_ready"), sem("ada_copied")
        hsq_ready, hss_ready, hrms_ready = sem("hsq_ready"), sem("hss_ready"), sem("hrms_ready")
        act_part = sem("act_part")
        rope_in, rope_done, heads_ready, gates_ready = (
            sem("rope_in"), sem("rope_done"), sem("heads_ready"), sem("gates_ready"))
        scores_done, scored, nmax_ready, probs_ready = (
            sem("scores_done"), sem("scored"), sem("nmax_ready"), sem("probs_ready"))
        pt_done, pt_copied, pv_done, otok_ready = sem("pt_done"), sem("pt_copied"), sem("pv_done"), sem("otok_ready")
        ot_done, ot_copied = sem("ot_done"), sem("ot_copied")
        proj_done, merged_ready = sem("proj_done"), sem("merged_ready")
        small_done, small_x, small_abs, small_exp, small_w, small_ln = (
            sem("small_done"), sem("small_x"), sem("small_abs"), sem("small_exp"), sem("small_w"), sem("small_ln"))
        beta_ready, aneg_ready, loga_ready, cum_done, cum_copied, ecum_ready, beg_ready = (
            sem("beta_ready"), sem("aneg_ready"), sem("loga_ready"), sem("cum_done"), sem("cum_copied"),
            sem("ecum_ready"), sem("beg_ready"))
        xtok_done, xdt_ready, btok_done, btok_copied, xend_ready = (
            sem("xtok_done"), sem("xdt_ready"), sem("btok_done"), sem("btok_copied"), sem("xend_ready"))
        state_done, state_copied, cb_done, cbm_ready = (
            sem("state_done"), sem("state_copied"), sem("cb_done"), sem("cbm_ready"))
        seg_done, seg_taken, seg_ready, row_exp_ready, decay_ready, mix_ready, cdec_ready = (
            sem("seg_done"), sem("seg_taken"), sem("seg_ready"), sem("row_exp_ready"), sem("decay_ready"),
            sem("mix_ready"), sem("cdec_ready"))
        y_done, y_taken, yg_ready, ysq_ready, yss_done, yrms_ready, ys_ready = (
            sem("y_done"), sem("y_taken"), sem("yg_ready"), sem("ysq_ready"), sem("yss_done"), sem("yrms_ready"),
            sem("ys_ready"))
        qksq_ready, qkss_done, qkrms_ready, qk_ready = (
            sem("qksq_ready"), sem("qkss_done"), sem("qkrms_ready"), sem("qk_ready"))
        kv_done, kv_taken, kk_done, gseg_taken, gseg_ready, grow_ready, gdec_ready = (
            sem("kv_done"), sem("kv_taken"), sem("kk_done"), sem("gseg_taken"), sem("gseg_ready"),
            sem("grow_ready"), sem("gdec_ready"))
        strict_ready, incl_ready, mt_ready, aqk_ready, qd_ready = (
            sem("strict_ready"), sem("incl_ready"), sem("mt_ready"), sem("aqk_ready"), sem("qd_ready"))
        cs_ready, inv_u_done, inv_u_copied, inv_v_done, inv_ready = (
            sem("cs_ready"), sem("inv_u_done"), sem("inv_u_copied"), sem("inv_v_done"), sem("inv_ready"))
        wt_done, wt_copied, vn_done, vn_copied, o_done, o_copied, st_done, st_ready = (
            sem("wt_done"), sem("wt_copied"), sem("vn_done"), sem("vn_copied"), sem("o_done"), sem("o_copied"),
            sem("st_done"), sem("st_ready"))
        osq_ready, oss_done, orms_ready, yd_ready = (
            sem("osq_ready"), sem("oss_done"), sem("orms_ready"), sem("yd_ready"))

        def con(name):
            return CON[:, CONSTS[name][0]:CONSTS[name][1]]

        def rop(name):
            return ROP[:, ROPES[name][0]:ROPES[name][1]]

        def pk1(name, i=0, n=1):
            return PK1[:, PACK1[name][0] + i:PACK1[name][0] + i + n]

        def pk2(name, i=0, n=1):
            return PK2[:, PACK2[name][0] + i:PACK2[name][0] + i + n]

        def tiles(x, t):
            return x.rearrange("p (t n) -> p t n", t=t)

        def spread(x, n):
            return x.unsqueeze(2).to_broadcast([P, x.shape[1], n])

        def each(x, h):
            return x.unsqueeze(1).to_broadcast([P, h, x.shape[1]])

        def norm_no(l, i):
            return 2 + 3 * l + i

        def layer_q(l, q):
            return Q_LAYERS + q, (L_PANELS // RING) * l

        block = ctx.enter_context(nc.Block())

        @block.sync
        def _(sp):
            def load(q, slot):
                sp.dma_start(ring[:, slot, :], w_stream[q]).then_inc(panel_loaded[slot], 16)

            for q in range(RING):
                load(q, q)
            with sp.Fori(1, N_PANELS // RING) as r:
                for s in range(RING):
                    sp.wait_ge(panel_used, (r - 1) * RING + s + 1)
                    load(r * RING + s, s)
            for s in range(N_PANELS % RING):
                q = N_PANELS // RING * RING + s
                sp.wait_ge(panel_used, q - RING + 1)
                load(q, s)
            sp.wait_ge(u_ready, KT * (norm_no(LAYERS, 0) + 1))
            sp.dma_start(out_t, U[:, :, :]).then_inc(out_stored, 16)
            sp.wait_ge(out_stored, 16)

        @block.gpsimd
        def _(pool):
            pool.dma_start(CON[:, :], consts).then_inc(consts_loaded, 16)
            pool.dma_start(ROP, ropes).then_inc(ropes_loaded, 16)
            pool.dma_start(BIAS, na_bias).then_inc(bias_loaded, 16)
            pool.wait_ge(consts_loaded, 16)
            with pool.Fori(0, LAYERS) as l:
                pool.wait_ge(u_ready, KT * (2 + 3 * l))
                pool.dma_start(PK2[:, :], pack2[l]).then_inc(pack2_loaded, 16)
                for t in range(2):
                    for b in range(2):
                        n = 4 * l + 2 * t + b
                        d = tiles(DEC[:, 512 * b:512 * b + 512], 4)
                        pool.wait_ge(gdec_ready, n + 1)
                        nc.gpsimd.tensor_tensor(tiles(DCY[:, 512 * b:512 * b + 512], 4), d, each(con("cum64"), 4),
                                                ALU.mult).then_inc(incl_ready, 1)
                        nc.gpsimd.tensor_tensor(d, d, each(con("strict64"), 4), ALU.mult).then_inc(strict_ready, 1)
                    for v in range(LEVELS):
                        for b in range(2):
                            k = (2 * l + t) * LEVELS + v
                            if v == 0:
                                pool.wait_ge(mt_ready, 4 * l + 2 * t + b + 1)
                            elif v == 1:
                                pool.wait_ge(inv_ready, 2 * (k - 1) + b + 1)
                            else:
                                pool.wait_ge(inv_u_done, 2 * (k - 1) + b + 1)
                            lev = con("levels")[:, v * P:(v + 1) * P]
                            nc.gpsimd.tensor_tensor(tiles(CS[:, 512 * b:512 * b + 512], 4),
                                                    tiles(MT[:, 512 * b:512 * b + 512], 4), each(lev, 4),
                                                    ALU.mult).then_inc(cs_ready, 1)

        @block.tensor
        def _(pe):
            def panel(q, rounds=0):
                pe.wait_ge(panel_loaded[q % RING], 16 * (q // RING + 1) + rounds * 16)
                return ring[:, q % RING, :]

            def norm(n):
                for k in range(KT // 2):
                    pe.wait_ge(squares_ready, KT // 2 * n + k + 1)
                    for e in range(2):
                        mm = nc.tensor.matmul(bank[4][:, 0:S], MEAN_D[:, :], SQ[:, (2 * k + e) * S:(2 * k + e + 1) * S],
                                              start=(k + e == 0), stop=(k == KT // 2 - 1 and e == 1))
                mm.then_inc(sumsq_ready, 1)
                pe.wait_ge(u_ready, KT * n + KT)

            def wide(w, q, rounds, par):
                src = tiles(panel(q, rounds), KT)
                pe.wait_ge(wide_free, w + 1)
                for e in range(2):
                    for k in range(KT):
                        mm = nc.tensor.matmul(bank[4 + par][:, e * S:(e + 1) * S], src[:, k, e * P:(e + 1) * P],
                                              U[:, k, :], start=(k == 0), stop=(k == KT - 1))
                mm.then_inc(panel_used, 1)

            def ffn(f, q0, rounds):
                def gate_up(q, rr, par):
                    for e in range(2):
                        src = tiles(panel(q + e, rr), KT)
                        for half in range(2):
                            for k in range(KT):
                                mm = nc.tensor.matmul(bank[4 + 2 * par + half][:, e * S:(e + 1) * S],
                                                      src[:, k, half * P:(half + 1) * P], U[:, k, :],
                                                      start=(k == 0), stop=(k == KT - 1))
                        mm.then_inc(panel_used, 1)

                def down(i, q, rr, par, first=False, last=False):
                    src = panel(q, rr)
                    pe.wait_ge(hidden_ready, f * HID_PAIRS + i + 1)
                    for e in range(2):
                        for j in range(KT):
                            mm = nc.tensor.matmul(bank[j // 2][:, (j % 2) * S:(j % 2 + 1) * S],
                                                  src[:, e * D + j * P:e * D + (j + 1) * P],
                                                  HID[:, par, e * S:(e + 1) * S],
                                                  start=(first and e == 0 and j % 2 == 0),
                                                  stop=(last and e == 1), skip_group_check=True)
                    mm.then_inc(panel_used, 1)

                gate_up(q0, rounds, 0)
                gate_up(q0 + 2, rounds, 1)
                down(0, q0 + 4, rounds, 0, first=True)
                with pe.Fori(0, 4) as r:
                    for b in range(2):
                        gate_up(q0 + 5 + 3 * b, rounds + r, b)
                        down(r * 2 + 1 + b, q0 + 7 + 3 * b, rounds + r, 1 - b)
                gate_up(q0 + 29, rounds, 0)
                down(9, q0 + 31, rounds, 1)
                down(10, q0 + 32, rounds, 0, last=True)

            pe.wait_ge(c_ready, 1)
            with pe.Fori(0, B1_ADA // RING) as r:
                pe.wait_ge(ada_copied, r + 1)
                for s in range(RING):
                    src = tiles(panel(s, r), KT)
                    for e in range(2):
                        for k in range(KT):
                            mm = nc.tensor.matmul(bank[6][:, 2 * s + e:2 * s + e + 1], src[:, k, e * P:(e + 1) * P],
                                                  CACT[:, k:k + 1], start=(k == 0), stop=(k == KT - 1))
                    mm.then_inc(panel_used, 1)
            pe.wait_ge(fills_done, 1)
            norm(0)
            with pe.Fori(0, B1_WIDE // RING) as r:
                for s in range(RING):
                    wide(r * RING + s, Q_WIDE1 + s, r, s % 2)
            for c in range(B1_V):
                src = tiles(panel(Q_V + c), KT)
                pe.wait_ge(wide_free, B1_WIDE + c + 1)
                for t in range(2):
                    for k in range(KT):
                        mm = nc.tensor.matmul(bank[4 + c % 2][:, t * S:(t + 1) * S], U[:, k, t * P:(t + 1) * P],
                                              src[:, k, :], start=(k == 0), stop=(k == KT - 1))
                mm.then_inc(panel_used, 1)

            pe.wait_ge(ropes_loaded, 16)

            def rope(pr):
                pe.wait_ge(rope_in, pr - 3)
                pe.wait_ge(heads_ready, pr - 1)
                nc.tensor.matmul(bank[6 + pr % 2][:, :], rop("swap"), PROJ[:, 2 * pr:2 * pr + 2, :],
                                 start=True, stop=True).then_inc(rope_done, 1)

            for pr in range(10):
                pe.wait_ge(hsq_ready, pr + 1)
                if pr >= 4:
                    pe.wait_ge(hrms_ready, pr - 3)
                nc.tensor.matmul(bank[pr % 4][:, :], rop("head64"), SQ[:, pr % 4 * 512:pr % 4 * 512 + 512],
                                 start=True, stop=True).then_inc(hss_ready, 1)
                if pr >= 6:
                    rope(pr - 2)
            rope(8)
            rope(9)

            def heads(u):
                if u < NA_UNITS:
                    return u % 2, [(QA, KA, u // 2, (u // 2) * HD)]
                j, t = (u - NA_UNITS) // 2, u % 2
                return t, [(QB, KB, g * DIL_SLOTS + j, 512 + (g * DIL_SLOTS + j) * HD) for g in range(DIL_GROUPS)]

            def scores(u):
                t, hs = heads(u)
                if u >= 2:
                    pe.wait_ge(scored, u - 1)
                for g, (q0, k0, h, _) in enumerate(hs):
                    at = h % 2 * HD
                    mm = nc.tensor.matmul(bank[u % 2 * 2 + g // 2][:, g % 2 * S:(g % 2 + 1) * S],
                                          PROJ[at:at + HD, q0 + h // 2, t * P:(t + 1) * P],
                                          PROJ[at:at + HD, k0 + h // 2, :], start=True, stop=True)
                mm.then_inc(scores_done, 1)

            def turn(u):
                pe.wait_ge(probs_ready, u + 1)
                if u >= 1:
                    pe.wait_ge(pt_copied, u)
                for k in range(2 * len(heads(u)[1])):
                    mm = nc.tensor.transpose(bank[4 + k // 4][:, k % 4 * P:(k % 4 + 1) * P],
                                             PR[:, u % 2, k * P:(k + 1) * P], con("ident"))
                mm.then_inc(pt_done, 1)

            def values(u):
                t, hs = heads(u)
                pe.wait_ge(pt_copied, u + 1)
                if u == NA_UNITS:
                    pe.wait_ge(otok_ready, 2)
                at = (u // 2 if u < NA_UNITS else (u - NA_UNITS) // 2) * HD
                for g, (_, _, _, v0) in enumerate(hs):
                    for k in range(2):
                        mm = nc.tensor.matmul(bank[6 + t][:, at:at + HD],
                                              PT[:, u % 2, (2 * g + k) * P:(2 * g + k + 1) * P],
                                              VT[:, k, v0:v0 + HD], start=(g + k == 0),
                                              stop=(g == len(hs) - 1 and k == 1))
                mm.then_inc(pv_done, 1)

            pe.wait_ge(heads_ready, 10)
            scores(0)
            for u in range(UNITS):
                if u + 1 < UNITS:
                    scores(u + 1)
                turn(u)
                if u >= 1:
                    values(u - 1)
            values(UNITS - 1)
            pe.wait_ge(otok_ready, 4)
            for k in range(6):
                for t in range(2):
                    mm = nc.tensor.transpose(bank[k // 2][:, k % 2 * S + t * P:k % 2 * S + (t + 1) * P],
                                             OTOK[:, t, k * P:(k + 1) * P], con("ident"))
            mm.then_inc(ot_done, 1)
            pe.wait_ge(ot_copied, 3)
            src_a = [tiles(panel(Q_PROJ1 + i), 4) for i in range(2)]
            src_b = tiles(panel(Q_PROJ1 + 2), 2)
            for c in range(4):
                if c >= 2:
                    pe.wait_ge(merged_ready, c - 1)
                for e in range(2):
                    for k in range(4):
                        mm = nc.tensor.matmul(bank[4 + c % 2 * 2][:, e * S:(e + 1) * S],
                                              src_a[c // 2][:, k, c % 2 * S + e * P:c % 2 * S + (e + 1) * P],
                                              OT[:, k, :], start=(k == 0), stop=(k == 3))
                if c % 2:
                    mm.then_inc(panel_used, 1)
                for e in range(2):
                    for k in range(2):
                        mm = nc.tensor.matmul(bank[5 + c % 2 * 2][:, e * S:(e + 1) * S],
                                              src_b[:, k, c * S + e * P:c * S + (e + 1) * P],
                                              OT[:, 4 + k, :], start=(k == 0), stop=(k == 1))
                mm.then_inc(proj_done if c < 3 else panel_used, 1)

            def to_residual(q, rounds, merged, v, first):
                pe.wait_ge(merged_ready, merged)
                for j in range(4):
                    src = tiles(panel(q + j, rounds), KT)
                    if j >= 2:
                        pe.wait_ge(residual_ready, 4 * (v - 1) + j - 1)
                    for e in range(2):
                        for k in range(KT):
                            mm = nc.tensor.matmul(bank[first + j % 2][:, e * S:(e + 1) * S],
                                                  src[:, k, e * P:(e + 1) * P], U[:, k, :],
                                                  start=(k == 0), stop=(k == KT - 1))
                    mm.then_inc(panel_used, 1)

            to_residual(Q_WO, 0, 4, 1, 0)
            norm(1)
            ffn(0, Q_FFN0, 0)

            with pe.Fori(0, LAYERS) as l:
                rounds = l * (L_PANELS // RING)
                w0 = WIDE0 + L_WIDE * l
                norm(2 + 3 * l)
                ffn(1 + 2 * l, Q_LAYERS + LQ_FFN1, rounds)
                norm(3 + 3 * l)
                pe.wait_ge(pack2_loaded, 16 * l + 16)
                for t in range(2):
                    for k in range(KT):
                        mm = nc.tensor.matmul(bank[6][:, t * SMALL:(t + 1) * SMALL], U[:, k, t * P:(t + 1) * P],
                                              pk2("small_w", k * SMALL, SMALL), start=(k == 0), stop=(k == KT - 1))
                mm.then_inc(small_done, 1)
                with pe.Fori(0, L_CONV // RING) as r:
                    for s in range(RING):
                        wide(w0 + r * RING + s, Q_LAYERS + LQ_WIDE + s, rounds + r, s % 2)
                pe.wait_ge(loga_ready, l + 1)
                for t in range(2):
                    a, g = LOGA[:, t, 0:SSM_HEADS], LOGA[:, t, SSM_HEADS:SP_COLS]
                    nc.tensor.matmul(bank[6][:, 32 * t:32 * t + 32], con("cum128"), a, start=True, stop=True)
                    nc.tensor.matmul(bank[6][:, 64 + 8 * t:72 + 8 * t], con("cum64"), g, start=True, stop=True)
                    nc.tensor.matmul(bank[6][:, 80 + 8 * t:88 + 8 * t], con("same64"), g, start=True, stop=True)
                    for c in range(2):
                        at = 128 + 8 * (2 * t + c)
                        nc.tensor.matmul(bank[6][:, at:at + 8], con(f"half{c}"), g, start=True, stop=True)
                nc.tensor.matmul(bank[6][:, 96:128], ONES[:, :], LOGA[:, 0, 0:SSM_HEADS], start=True,
                                 stop=True).then_inc(cum_done, 1)
                for j in range(L_ZS):
                    wide(w0 + L_CONV + j, Q_LAYERS + LQ_WIDE + L_CONV + j, rounds, j % 2)

                pe.wait_ge(conv_ready, 2 + 24 * l + 24)
                for t in range(2):
                    for q in range(4):
                        i = 4 * t + q
                        if i >= 4:
                            pe.wait_ge(xdt_ready, 8 * l + i - 3)
                        for e in range(4):
                            mm = nc.tensor.transpose(bank[q][:, e * P:(e + 1) * P],
                                                     CONV[:, 4 * q + e, t * P:(t + 1) * P], con("ident"))
                        mm.then_inc(xtok_done, 1)
                for g in range(GROUPS):
                    mm = nc.tensor.transpose(bank[7][:, g * P:(g + 1) * P], CONV[:, B_TILE + g, 0:P], con("ident"))
                mm.then_inc(btok_done, 1)
                pe.wait_ge(btok_copied, l + 1)
                for g in range(GROUPS):
                    pe.wait_ge(xend_ready, 4 * l + g + 1)
                    nc.tensor.matmul(bank[g][:, :], BTOK[:, g * P:(g + 1) * P], XEND[:, g * 512:(g + 1) * 512],
                                     start=True, stop=True).then_inc(state_done, 1)
                pe.wait_ge(cum_copied, l + 1)
                for t in range(2):
                    for g in range(GROUPS):
                        mm = nc.tensor.matmul(bank[6 + t][:, g * P:(g + 1) * P], CONV[:, B_TILE + g, t * P:(t + 1) * P],
                                              CONV[:, C_TILE + g, t * P:(t + 1) * P], start=True, stop=True)
                    mm.then_inc(cb_done, 1)
                pe.wait_ge(state_copied, 4 * l + 4)

                def decay_rows(i):
                    t, h0 = i // 8, i % 8 * 4
                    if i >= 2:
                        pe.wait_ge(seg_taken, 16 * l + i - 1)
                    if i >= 10:
                        pe.wait_ge(row_exp_ready, 8 * l + i - 9)
                    for e in range(4):
                        mm = nc.tensor.matmul(bank[i % 2][:, e * P:(e + 1) * P],
                                              LOGA[:, t, h0 + e:h0 + e + 1].to_broadcast([P, P]), con("cum128"),
                                              start=True, stop=True)
                    mm.then_inc(seg_done, 1)

                def scan_out(i):
                    t, h0, m = i // 8, i % 8 * 4, i // 2
                    pe.wait_ge(mix_ready, 16 * l + i + 1)
                    if t == 1:
                        pe.wait_ge(cdec_ready, 8 * l + i - 7)
                    if i % 2 == 0 and m >= 2:
                        pe.wait_ge(y_taken, 8 * l + m - 1)
                    for e in range(4):
                        h = h0 + e
                        dst = bank[2 + m % 2][h % 2 * HD:h % 2 * HD + HD, h % 8 // 2 * P:(h % 8 // 2 + 1) * P]
                        mm = nc.tensor.matmul(dst, XDT[:, t, h * HD:(h + 1) * HD], MIX[:, i % 2, e * P:(e + 1) * P],
                                              start=True, stop=(t == 0))
                        if t == 1:
                            mm = nc.tensor.matmul(dst, STATE[:, h * HD:(h + 1) * HD], CDEC[:, i % 2, e * P:(e + 1) * P],
                                                  start=False, stop=True)
                    mm.then_inc(y_done, 1)

                decay_rows(0)
                for i in range(16):
                    if i + 1 < 16:
                        decay_rows(i + 1)
                    scan_out(i)
                pe.wait_ge(y_taken, 8 * l + 8)
                for g in range(GROUPS):
                    pe.wait_ge(ysq_ready, 4 * l + g + 1)
                    for e in range(4):
                        at = g % 2 * 1024 + e * S
                        mm = nc.tensor.matmul(bank[g][:, 0:S], MEAN_G[:, :], SQ[:, at:at + S], start=(e == 0),
                                              stop=(e == 3))
                    mm.then_inc(yss_done, 1)
                for j in range(L_ZD):
                    wide(w0 + L_CONV + L_ZS + j, Q_LAYERS + LQ_WIDE + L_CONV + L_ZS + j, rounds, j % 2)

                pe.wait_ge(yrms_ready, 4 * l + 4)
                for pr in range(8):
                    pe.wait_ge(qksq_ready, 8 * l + pr + 1)
                    if pr >= 4:
                        pe.wait_ge(qkrms_ready, 8 * l + pr - 3)
                    nc.tensor.matmul(bank[pr % 4][:, :], ONES[:, :], SQ[:, pr % 4 * 512:pr % 4 * 512 + 512],
                                     start=True, stop=True).then_inc(qkss_done, 1)
                pe.wait_ge(qk_ready, 8 * l + 8)
                for t in range(2):
                    tok = slice(t * P, (t + 1) * P)
                    if t == 1:
                        pe.wait_ge(st_ready, 6 * l + 4)
                        pe.wait_ge(o_copied, 4 * l + 2)
                    for m in range(4):
                        for e in range(4):
                            mm = nc.tensor.transpose(bank[m][:, e * P:(e + 1) * P], QKV[:, 8 + 4 * m + e, tok],
                                                     con("ident"))
                        mm.then_inc(kv_done, 1)
                    for b in range(2):
                        n = 4 * l + 2 * t + b
                        if 2 * t + b >= 1:
                            pe.wait_ge(mt_ready, n)
                            pe.wait_ge(aqk_ready, n)
                            pe.wait_ge(grow_ready, n)
                        for e in range(4):
                            h, at = 4 * b + e, slice(e * P, (e + 1) * P)
                            q, k = QKV[:, h, tok], QKV[:, DN_HEADS + h, tok]
                            nc.tensor.matmul(bank[6][:, at], LOGA[:, t, 32 + h:33 + h].to_broadcast([P, P]),
                                             con("cum64"), start=True, stop=True)
                            nc.tensor.matmul(bank[7][:, at], BETA[:, t, h:h + 1].to_broadcast([P, P]), con("ident"),
                                             start=True, stop=True)
                            nc.tensor.matmul(bank[4][:, at], k, k, start=True, stop=True)
                            mm = nc.tensor.matmul(bank[5][:, at], k, q, start=True, stop=True)
                        mm.then_inc(kk_done, 1)
                    for v in range(LEVELS):
                        k = (2 * l + t) * LEVELS + v
                        kc = (2 * l + t) * (LEVELS - 1) + v - 1
                        for b in range(2):
                            pe.wait_ge(cs_ready, 2 * k + b + 1)
                            if v >= 1:
                                pe.wait_ge(inv_ready, 2 * k + b - 1)
                            for e in range(4):
                                at = slice(512 * b + e * P, 512 * b + (e + 1) * P)
                                mm = nc.tensor.matmul(bank[b][:, e * P:(e + 1) * P], CS[:, at],
                                                      TI[:, at] if v else con("ident"), start=True, stop=True)
                            mm.then_inc(inv_u_done, 1)
                        for b in range(2 if v else 0):
                            pe.wait_ge(inv_u_copied, 2 * kc + b + 1)
                            for e in range(4):
                                at, to = slice(512 * b + e * P, 512 * b + (e + 1) * P), slice(e * P, (e + 1) * P)
                                if v < LEVELS - 1:
                                    nc.tensor.matmul(bank[2 + b][:, to], TT[:, at], UB[:, at], start=True, stop=True)
                                mm = nc.tensor.matmul(bank[6 + b][:, to], UB[:, at], TT[:, at], start=True, stop=True)
                            mm.then_inc(inv_v_done, 1)
                    for b in range(2):
                        pe.wait_ge(inv_ready, 2 * ((2 * l + t) * LEVELS + LEVELS - 1) + b + 1)
                        for e in range(4):
                            at = slice(512 * b + e * P, 512 * b + (e + 1) * P)
                            mm = nc.tensor.matmul(bank[b][:, e * P:(e + 1) * P], KBG[:, at], TT[:, at],
                                                  start=True, stop=True)
                        mm.then_inc(wt_done, 1)
                    pe.wait_ge(wt_copied, 4 * l + 2 * t + 2)
                    for c in range(2):
                        cg, r = 2 * t + c, c * 64
                        rows = slice(r, r + 64)
                        if cg >= 1:
                            pe.wait_ge(st_ready, 6 * l + 2 * cg)
                        for b in range(2):
                            for e in range(4):
                                h = 4 * b + e
                                to = bank[2 + b][rows, e * P:(e + 1) * P]
                                at = slice(h * P, (h + 1) * P)
                                mm = nc.tensor.matmul(to, TT[:, h * P + r:h * P + r + 64], VB[:, at], start=True,
                                                      stop=(cg == 0))
                                if cg >= 1:
                                    mm = nc.tensor.matmul(to, WT[:, h * P + r:h * P + r + 64], ST[:, at], start=False,
                                                          stop=True)
                            mm.then_inc(vn_done, 1)
                        pe.wait_ge(vn_copied, 8 * l + 2 * cg + 2)
                        if cg >= 1:
                            pe.wait_ge(o_copied, 4 * l + cg)
                        for h in range(DN_HEADS):
                            to = bank[6][:, h * 64:(h + 1) * 64]
                            if cg >= 1:
                                nc.tensor.matmul(to, ST[:, h * P:(h + 1) * P], QKV[:, h, t * P + r:t * P + r + 64],
                                                 start=True, stop=False)
                            mm = nc.tensor.matmul(to, VN[rows, h * P:(h + 1) * P],
                                                  AQK[rows, h * P + r:h * P + r + 64], start=(cg == 0), stop=True)
                        mm.then_inc(o_done, 1)
                        for b in range(2 if cg < 3 else 0):
                            for e in range(4):
                                at = slice(512 * b + e * P, 512 * b + (e + 1) * P)
                                mm = nc.tensor.matmul(bank[b][:, e * P:(e + 1) * P], KDEC[rows, at], VN[rows, at],
                                                      start=True, stop=True)
                            mm.then_inc(st_done, 1)
                for pr in range(4):
                    pe.wait_ge(osq_ready, 4 * l + pr + 1)
                    nc.tensor.matmul(bank[pr][:, :], MEAN_V[:, :], SQ[:, pr * 512:pr * 512 + 512], start=True,
                                     stop=True).then_inc(oss_done, 1)
                for j in range(L_GATES):
                    jj = L_CONV + L_ZS + L_ZD + j
                    wide(w0 + jj, Q_LAYERS + LQ_WIDE + jj, rounds, j % 2)
                pe.wait_ge(ys_ready, 4 * l + 4)
                pe.wait_ge(yd_ready, 4 * l + 4)
                for c in range(4):
                    if c >= 2:
                        pe.wait_ge(merged_ready, 4 + 4 * l + c - 1)
                    for half in range(2):
                        src = tiles(panel(Q_LAYERS + LQ_PROJ + 3 * c + half, rounds), KT)
                        for e in range(2):
                            for k in range(KT):
                                mm = nc.tensor.matmul(bank[c % 2 * 2][:, e * S:(e + 1) * S],
                                                      src[:, k, e * P:(e + 1) * P], CONV[:, half * KT + k, :],
                                                      start=(half + e + k == 0), stop=(half == 1 and k == KT - 1),
                                                      skip_group_check=True)
                        mm.then_inc(panel_used, 1)
                    src = tiles(panel(Q_LAYERS + LQ_PROJ + 3 * c + 2, rounds), KT)
                    for e in range(2):
                        for k in range(KT):
                            mm = nc.tensor.matmul(bank[c % 2 * 2 + 1][:, e * S:(e + 1) * S],
                                                  src[:, k, e * P:(e + 1) * P], QKV[:, k, :],
                                                  start=(k == 0), stop=(k == KT - 1))
                    mm.then_inc(panel_used, 1)
                to_residual(Q_LAYERS + LQ_WOUT, rounds, 4 + 4 * l + 4, 4 + 3 * l, 6)
                norm(4 + 3 * l)
                ffn(2 + 2 * l, Q_LAYERS + LQ_FFN2, rounds)
            norm(2 + 3 * LAYERS)

        @block.scalar
        def _(act):
            act.dma_start(PK1[:, :], pack1).then_inc(pack1_loaded, 16)
            act.dma_start(H[:, :, :], x_t).then_inc(x_loaded, 16)
            act.sem_inc(wide_free, 2)
            act.sem_inc(conv_ready, 2)
            act.wait_ge(pack1_loaded, 16)
            nc.scalar.activation(CACT[:, :], pk1("c", 0, 8), ACT.Silu).then_inc(c_ready, 1)

            def norm(n, loaded=False):
                for k in range(KT // 2):
                    if loaded:
                        act.wait_ge(x_loaded, 16)
                    else:
                        act.wait_ge(residual_ready, KT // 2 * (n - 1) + k + 1)
                    nc.scalar.activation(tiles(SQ[:, k * 512:(k + 1) * 512], 2), H[:, 2 * k:2 * k + 2, :],
                                         ACT.Square).then_inc(squares_ready, 1)
                act.wait_ge(sumsq_ready, n + 1)
                nc.scalar.activation(RMS[:, 0:S], bank[4][:, 0:S], ACT.Sqrt, bias=EPST[:, :]).then_inc(rms_ready, 1)

            def ffn(f, q0, layer):
                def silu(i, count, par):
                    act.wait_ge(panel_used, q0 + count)
                    nc.scalar.activation(SG[:, par, :], bank[4 + 2 * par][:, :], ACT.Silu).then_inc(gate_act_ready, 1)

                silu(0, 2, 0)
                with act.Fori(0, 5) as r:
                    for b in range(2):
                        silu(None, 6 * r + 3 * b + 4, 1 - b)

            act.wait_ge(fills_done, 1)
            norm(0, loaded=True)
            proj2 = ARENA[:, 0:36 * S].rearrange("p (w n) -> p w n", w=B1_WIDE)
            with act.Fori(0, B1_WIDE // 2) as r:
                for b in range(2):
                    act.wait_ge(panel_used, Q_WIDE1 + 2 * r + b + 1)
                    nc.scalar.activation(proj2[:, 2 * r + b, :], bank[4 + b][:, :], ACT.Copy).then_inc(wide_free, 1)
            for c in range(B1_V):
                act.wait_ge(panel_used, Q_V + c + 1)
                nc.scalar.activation(VT[:, :, c * S:(c + 1) * S], tiles(bank[4 + c % 2][:, :], 2),
                                     ACT.Copy).then_inc(wide_free, 1)
            act.wait_ge(wide_free, 2 + WIDE0)
            for i in range(16):
                nc.scalar.activation(PROJ[:, GATE + i, :], PROJ[:, GATE + i, :], ACT.Sigmoid,
                                     bias=pk1("b_gate", i)).then_inc(gates_ready, 1)

            def head_rms(pr):
                act.wait_ge(hss_ready, pr + 1)
                nc.scalar.activation(RSH[:, pr, :], bank[pr % 4][:, :], ACT.Sqrt, bias=EPST[:, :]).then_inc(hrms_ready, 1)

            for pr in range(10):
                nc.scalar.activation(tiles(SQ[:, pr % 4 * 512:pr % 4 * 512 + 512], 2), PROJ[:, 2 * pr:2 * pr + 2, :],
                                     ACT.Square).then_inc(hsq_ready, 1)
                if pr >= 1:
                    head_rms(pr - 1)
            head_rms(9)

            def keys(u):
                return S if u < NA_UNITS else DIL_GROUPS * S

            def softmax_exp(u):
                act.wait_ge(nmax_ready, u + 1)
                if u >= 2:
                    act.wait_ge(pt_done, u - 1)
                nc.scalar.activation(PR[:, u % 2, 0:keys(u)], SC[:, u % 2, 0:keys(u)], ACT.Exp,
                                     bias=NMAX[:, UNITS + u:UNITS + u + 1],
                                     accum_out=DEN[:, u:u + 1]).then_inc(probs_ready, 1)

            def turned(u):
                act.wait_ge(pt_done, u + 1)
                if u >= 2:
                    act.wait_ge(pv_done, u - 1)
                nc.scalar.activation(PT[:, u % 2, 0:min(512, keys(u))], bank[4][:, 0:min(512, keys(u))], ACT.Copy)\
                    .then_inc(pt_copied if keys(u) <= 512 else act_part, 1)
                if keys(u) > 512:
                    nc.scalar.activation(PT[:, u % 2, 512:keys(u)], bank[5][:, 0:keys(u) - 512],
                                         ACT.Copy).then_inc(pt_copied, 1)

            softmax_exp(0)
            for u in range(UNITS):
                if u + 1 < UNITS:
                    softmax_exp(u + 1)
                turned(u)
            act.wait_ge(ot_done, 1)
            for i in range(3):
                nc.scalar.activation(OT[:, 2 * i:2 * i + 2, :], tiles(bank[i][:, :], 2), ACT.Copy).then_inc(ot_copied, 1)
            norm(1)
            ffn(0, Q_FFN0, 0)

            conv2 = ARENA[:, 0:CONV_TILES * S].rearrange("p (w n) -> p w n", w=L_CONV)
            with act.Fori(0, LAYERS) as l:
                used0 = Q_LAYERS + L_PANELS * l
                norm(2 + 3 * l)
                ffn(1 + 2 * l, used0 + LQ_FFN1, l)
                norm(3 + 3 * l)
                act.wait_ge(small_abs, l + 1)
                nc.scalar.activation(SMX[:, 2, :], SMX[:, 1, :], ACT.Exp).then_inc(small_exp, 1)
                nc.scalar.activation(SMX[:, 7, 0:SP_COLS], pk2("a_log", 0, SP_COLS), ACT.Exp).then_inc(aneg_ready, 1)
                act.wait_ge(small_w, l + 1)
                nc.scalar.activation(SMX[:, 4, :], SMX[:, 3, :], ACT.Ln).then_inc(small_ln, 1)
                nc.scalar.activation(BETA[:, :, :], tiles(SMX[:, 0, :], 2)[:, :, SP_COLS:SMALL],
                                     ACT.Sigmoid).then_inc(beta_ready, 1)
                with act.Fori(0, L_CONV // 2) as r:
                    for b in range(2):
                        j = 2 * r + b
                        act.wait_ge(panel_used, used0 + LQ_WIDE + j + 1)
                        act.wait_ge(conv_step, 192 * l + 8 * j + 8)
                        nc.scalar.activation(XPAD[:, b, :, 3:S + 3], tiles(bank[4 + b][:, :], 2),
                                             ACT.Copy).then_inc(wide_free, 1)
                        act.wait_ge(conv_step, 192 * l + 8 * j + 24)
                        nc.scalar.activation(tiles(conv2[:, j, :], 2), CACC[:, b, :, :],
                                             ACT.Silu).then_inc(conv_ready, 1)
                for j in range(L_ZS):
                    act.wait_ge(panel_used, used0 + LQ_WIDE + L_CONV + j + 1)
                    nc.scalar.activation(ZS[:, 2 * j:2 * j + 2, :], tiles(bank[4 + j % 2][:, :], 2),
                                         ACT.Silu).then_inc(wide_free, 1)
                act.wait_ge(cum_copied, l + 1)
                nc.scalar.activation(ECUM[:, 0:96], ECUM[:, 0:96], ACT.Exp).then_inc(ecum_ready, 1)
                act.wait_ge(btok_done, l + 1)
                nc.scalar.activation(BTOK[:, :], bank[7][:, :], ACT.Copy).then_inc(btok_copied, 1)
                for g in range(GROUPS):
                    act.wait_ge(state_done, 4 * l + g + 1)
                    nc.scalar.activation(STATE[:, g * 512:(g + 1) * 512], bank[g][:, :], ACT.Copy).then_inc(state_copied, 1)
                for i in range(16):
                    if i >= 8:
                        act.wait_ge(seg_taken, 16 * l + i + 1)
                        if i >= 10:
                            act.wait_ge(y_done, 16 * l + i - 1)
                        nc.scalar.activation(CDEC[:, i % 2, :], bank[i % 2][:, :], ACT.Exp).then_inc(row_exp_ready, 1)
                    act.wait_ge(seg_ready, 16 * l + i + 1)
                    nc.scalar.activation(SEG[:, i % 2, :], SEG[:, i % 2, :], ACT.Exp).then_inc(decay_ready, 1)

                def group_rms(g):
                    act.wait_ge(yss_done, 4 * l + g + 1)
                    if g >= 2:
                        act.wait_ge(ys_ready, 4 * l + g - 1)
                    nc.scalar.activation(RMS[:, g % 2 * S:g % 2 * S + S], bank[g][:, 0:S], ACT.Sqrt,
                                         bias=EPST[:, :]).then_inc(yrms_ready, 1)

                for g in range(GROUPS):
                    act.wait_ge(yg_ready, 8 * l + 4 + g + 1)
                    if g >= 2:
                        act.wait_ge(yss_done, 4 * l + g - 1)
                    nc.scalar.activation(tiles(SQ[:, g % 2 * 1024:g % 2 * 1024 + 1024], 4),
                                         CONV[:, 4 * g:4 * g + 4, :], ACT.Square).then_inc(ysq_ready, 1)
                    if g >= 1:
                        group_rms(g - 1)
                group_rms(GROUPS - 1)
                for j in range(L_ZD):
                    act.wait_ge(panel_used, used0 + LQ_WIDE + L_CONV + L_ZS + j + 1)
                    nc.scalar.activation(ZD[:, 2 * j:2 * j + 2, :], tiles(bank[4 + j % 2][:, :], 2),
                                         ACT.Silu).then_inc(wide_free, 1)
                def qk_rms(pr):
                    act.wait_ge(qkss_done, 8 * l + pr + 1)
                    if pr >= 4:
                        act.wait_ge(qk_ready, 8 * l + pr - 3)
                    nc.scalar.activation(ROOT(pr), bank[pr % 4][:, :], ACT.Sqrt, bias=EPST[:, :]).then_inc(qkrms_ready, 1)

                for pr in range(8):
                    if pr >= 4:
                        act.wait_ge(qkss_done, 8 * l + pr - 3)
                    nc.scalar.activation(tiles(SQ[:, pr % 4 * 512:pr % 4 * 512 + 512], 2),
                                         QKV[:, 2 * pr:2 * pr + 2, :], ACT.Square).then_inc(qksq_ready, 1)
                    if pr >= 1:
                        qk_rms(pr - 1)
                qk_rms(7)
                for t in range(2):
                    for b in range(2):
                        n = 4 * l + 2 * t + b
                        act.wait_ge(gseg_taken, n + 1)
                        if 2 * t + b >= 1:
                            act.wait_ge(qd_ready, n)
                        nc.scalar.activation(RSTD[:, :], bank[6][:, :], ACT.Exp).then_inc(grow_ready, 1)
                        act.wait_ge(gseg_ready, n + 1)
                        nc.scalar.activation(DEC[:, 512 * b:512 * b + 512], DCY[:, 512 * b:512 * b + 512],
                                             ACT.Exp).then_inc(gdec_ready, 1)
                    for v in range(1, LEVELS):
                        k = (2 * l + t) * LEVELS + v
                        for b in range(2):
                            act.wait_ge(inv_u_done, 2 * k + b + 1)
                            nc.scalar.activation(UB[:, 512 * b:512 * b + 512], bank[b][:, :],
                                                 ACT.Copy).then_inc(inv_u_copied, 1)
                    for b in range(2):
                        act.wait_ge(wt_done, 4 * l + 2 * t + b + 1)
                        nc.scalar.activation(WT[:, 512 * b:512 * b + 512], bank[b][:, :], ACT.Copy,
                                             scale=-1.0).then_inc(wt_copied, 1)
                    for c in range(2):
                        cg, rows = 2 * t + c, slice(64 * c, 64 * c + 64)
                        for b in range(2):
                            act.wait_ge(vn_done, 8 * l + 2 * cg + b + 1)
                            nc.scalar.activation(VN[rows, 512 * b:512 * b + 512], bank[2 + b][rows, :],
                                                 ACT.Copy).then_inc(vn_copied, 1)
                act.wait_ge(o_copied, 4 * l + 4)
                for pr in range(4):
                    nc.scalar.activation(tiles(SQ[:, pr * 512:pr * 512 + 512], 2), QKV[:, 2 * pr:2 * pr + 2, :],
                                         ACT.Square).then_inc(osq_ready, 1)
                for pr in range(4):
                    act.wait_ge(oss_done, 4 * l + pr + 1)
                    nc.scalar.activation(ROOT(pr), bank[pr][:, :], ACT.Sqrt, bias=EPST[:, :]).then_inc(orms_ready, 1)
                for j in range(L_GATES):
                    act.wait_ge(panel_used, used0 + LQ_WIDE + L_CONV + L_ZS + L_ZD + j + 1)
                    nc.scalar.activation(GT[:, 2 * j:2 * j + 2, :], tiles(bank[4 + j % 2][:, :], 2),
                                         ACT.Sigmoid).then_inc(wide_free, 1)
                norm(4 + 3 * l)
                ffn(2 + 2 * l, used0 + LQ_FFN2, l)
            norm(2 + 3 * LAYERS)

        @block.vector
        def _(dve):
            base, count = [0], [0]

            def step(ins):
                ins.then_inc(dve_done, 1)
                count[0] += 1
                return count[0]

            def need(number):
                dve.wait_ge(dve_done, base[0] + number)

            def pad(total):
                assert count[0] <= total, count
                need(count[0])
                dve.sem_inc(dve_done, total - count[0])
                count[0] = 0

            nc.vector.memset(MEAN_D[:, :], 1.0 / D)
            nc.vector.memset(MEAN_G[:, :], 1.0 / 512)
            nc.vector.memset(MEAN_V[:, :], 1.0 / P)
            nc.vector.memset(ONES[:, :], 1.0)
            nc.vector.memset(XPAD[:, :, :, :], 0.0)
            nc.vector.memset(EPST[:, :], EPS).then_inc(fills_done, 1)
            dve.sem_inc(ada_copied, 1)
            dve.sem_inc(conv_step, 16)

            def norm(n, gain, shift=None):
                dve.wait_ge(rms_ready, n + 1)
                need(step(nc.vector.reciprocal(RSTD[:, 0:S], RMS[:, 0:S])))
                for k in range(KT):
                    ins = nc.vector.scalar_tensor_tensor(U[:, k, :], H[:, k, :], gain[:, k:k + 1], RSTD[:, 0:S],
                                                         ALU.mult, ALU.mult)
                    if shift is None:
                        ins.then_inc(u_ready, 1)
                    else:
                        need(step(ins))
                        nc.vector.tensor_scalar(U[:, k, :], U[:, k, :], shift[:, k:k + 1], None,
                                                ALU.add).then_inc(u_ready, 1)

            def ffn_hidden(f):
                def hidden(i, par):
                    dve.wait_ge(gate_act_ready, f * HID_PAIRS + i + 1)
                    nc.vector.tensor_tensor(HID[:, par, :], SG[:, par, :], bank[5 + 2 * par][:, :],
                                            ALU.mult).then_inc(hidden_ready, 1)

                with dve.Fori(0, 5) as r:
                    for b in range(2):
                        hidden(r * 2 + b, b)
                hidden(10, 0)

            def residual(j, src, scale):
                if isinstance(scale, float):
                    nc.vector.scalar_tensor_tensor(H[:, 2 * j:2 * j + 2, :], tiles(src, 2), scale, H[:, 2 * j:2 * j + 2, :],
                                                   ALU.mult, ALU.add).then_inc(residual_ready, 1)
                    return
                for e in range(2):
                    ins = nc.vector.scalar_tensor_tensor(H[:, 2 * j + e, :], src[:, e * S:(e + 1) * S],
                                                         scale[:, 2 * j + e:2 * j + e + 1], H[:, 2 * j + e, :],
                                                         ALU.mult, ALU.add)
                ins.then_inc(residual_ready, 1)

            dve.wait_ge(pack1_loaded, 16)
            mod3 = MOD[:, :].rearrange("p (r n) -> p r n", n=2 * RING)
            bada3 = pk1("b_ada", 0, 48).rearrange("p (r n) -> p r n", n=2 * RING)
            with dve.Fori(0, B1_ADA // RING) as r:
                dve.wait_ge(panel_used, RING * r + RING)
                nc.vector.tensor_tensor(mod3[:, r, :], bank[6][:, 0:2 * RING], bada3[:, r, :],
                                        ALU.add).then_inc(ada_copied, 1)
            shift1, scale1, gate1, shift2, scale2, gate2 = [MOD[:, 8 * i:8 * i + 8] for i in range(6)]
            dve.wait_ge(ada_copied, 1 + B1_ADA // RING)
            step(nc.vector.scalar_tensor_tensor(GS[:, 0:8], scale1, 1.0, pk1("g1", 0, 8), ALU.add, ALU.mult))
            step(nc.vector.scalar_tensor_tensor(GS[:, 8:16], scale2, 1.0, pk1("g2", 0, 8), ALU.add, ALU.mult))
            step(nc.vector.tensor_scalar(GS[:, 16:17], pk1("g_qa"), HD ** -0.5, None, ALU.mult))
            need(step(nc.vector.tensor_scalar(GS[:, 17:18], pk1("g_qb"), HD ** -0.5, None, ALU.mult)))
            norm(0, GS[:, 0:8], shift1)

            dve.wait_ge(ropes_loaded, 16)

            def rotate(pr):
                x = PROJ[:, 2 * pr:2 * pr + 2, :]
                dve.wait_ge(rope_done, pr - 3)
                need(step(nc.vector.tensor_tensor(tiles(RSH[:, pr, :], 2), tiles(bank[6 + pr % 2][:, :], 2),
                                                  each(rop("sin"), 2), ALU.mult)))
                need(step(nc.vector.tensor_tensor(x, x, each(rop("cos"), 2), ALU.mult)))
                nc.vector.tensor_tensor(x, x, tiles(RSH[:, pr, :], 2), ALU.add).then_inc(heads_ready, 1)

            gains = [GS[:, 16:17]] * 2 + [pk1("g_ka")] * 2 + [GS[:, 17:18]] * 3 + [pk1("g_kb")] * 3
            for pr in range(10):
                dve.wait_ge(hrms_ready, pr + 1)
                need(step(nc.vector.reciprocal(RSH[:, pr, :], RSH[:, pr, :])))
                x = PROJ[:, 2 * pr:2 * pr + 2, :]
                nc.vector.scalar_tensor_tensor(x, x, gains[pr], tiles(RSH[:, pr, :], 2), ALU.mult, ALU.mult)\
                    .then_inc(heads_ready if pr < 4 else rope_in, 1)
                if pr >= 6:
                    rotate(pr - 2)
            rotate(8)
            rotate(9)

            dve.wait_ge(bias_loaded, 16)

            def score(u):
                t = u % 2
                dve.wait_ge(scores_done, u + 1)
                if u >= 2:
                    dve.wait_ge(probs_ready, u - 1)
                if u < NA_UNITS:
                    nc.vector.tensor_tensor(SC[:, u % 2, 0:S], bank[u % 2 * 2][:, 0:S], BIAS[:, u, :],
                                            ALU.add).then_inc(scored, 1)
                    n = S
                else:
                    masks = tiles(rop("dil"), 2 * DIL_GROUPS)
                    nc.vector.tensor_tensor(tiles(SC[:, u % 2, 0:512], 2), tiles(bank[u % 2 * 2][:, :], 2),
                                            masks[:, 3 * t:3 * t + 2, :], ALU.add)
                    nc.vector.tensor_tensor(SC[:, u % 2, 512:768], bank[u % 2 * 2 + 1][:, 0:S], masks[:, 3 * t + 2, :],
                                            ALU.add).then_inc(scored, 1)
                    n = 768
                dve.wait_ge(scored, u + 1)
                need(step(nc.vector.tensor_reduce(NMAX[:, u:u + 1], SC[:, u % 2, 0:n], AX.X, ALU.max)))
                nc.vector.tensor_scalar(NMAX[:, UNITS + u:UNITS + u + 1], NMAX[:, u:u + 1], -1.0, None,
                                        ALU.mult).then_inc(nmax_ready, 1)

            def outputs(u0, units, at):
                dve.wait_ge(pv_done, u0 + units)
                need(step(nc.vector.reciprocal(RDEN[:, u0:u0 + units], DEN[:, u0:u0 + units])))
                heads = units // 2
                for t in range(2):
                    nc.vector.tensor_tensor(OTOK[:, t, at:at + heads * HD].rearrange("p (h n) -> p h n", h=heads),
                                            bank[6 + t][:, 0:heads * HD].rearrange("p (h n) -> p h n", h=heads),
                                            spread(RDEN[:, u0 + t:u0 + units:2], HD), ALU.mult).then_inc(otok_ready, 1)

            for u in range(UNITS):
                score(u)
                if u == NA_UNITS + 1:
                    outputs(0, NA_UNITS, 0)
            outputs(NA_UNITS, DIL_UNITS, 512)

            def merge(c, m0, bank_a, bank_b, gate_a, gate_b, ta, tb):
                if c >= 2:
                    dve.wait_ge(merged_ready, m0 + c - 1)
                step(nc.vector.tensor_tensor(tiles(ta, 2), tiles(bank_a[:, :], 2), gate_a[:, 2 * c:2 * c + 2, :],
                                             ALU.mult))
                need(step(nc.vector.tensor_tensor(tiles(tb, 2), tiles(bank_b[:, :], 2), gate_b[:, 2 * c:2 * c + 2, :],
                                                  ALU.mult)))
                nc.vector.tensor_tensor(U[:, 2 * c:2 * c + 2, :], tiles(ta, 2), tiles(tb, 2),
                                        ALU.add).then_inc(merged_ready, 1)

            dve.wait_ge(gates_ready, 16)
            for c in range(4):
                if c < 3:
                    dve.wait_ge(proj_done, c + 1)
                else:
                    dve.wait_ge(panel_used, Q_PROJ1 + B1_PROJ)
                ta, tb = [(x[:, 0, 0:512], x[:, 1, 0:512]) for x in (SC, PR)][c % 2]
                merge(c, 0, bank[4 + c % 2 * 2], bank[5 + c % 2 * 2], PROJ[:, GATE:GATE + 8, :],
                      PROJ[:, GATE + 8:GATE + 16, :], ta, tb)
            for j in range(4):
                dve.wait_ge(panel_used, Q_WO + j + 1)
                residual(j, bank[j % 2][:, :], gate1)
            dve.wait_ge(residual_ready, 4)
            norm(1, GS[:, 8:16], shift2)
            ffn_hidden(0)
            dve.wait_ge(panel_used, Q_LAYERS)
            for j in range(4):
                residual(j, bank[j][:, :], gate2)
            dve.wait_ge(residual_ready, 8)
            pad(DVE_B1)

            with dve.Fori(0, LAYERS) as l:
                base[0] = DVE_B1 + DVE_LAYER * l
                used0 = Q_LAYERS + L_PANELS * l
                dve.wait_ge(pack2_loaded, 16 * l + 16)
                norm(2 + 3 * l, pk2("ffn1", 0, 8))
                ffn_hidden(1 + 2 * l)
                dve.wait_ge(panel_used, used0 + LQ_WIDE)
                for j in range(4):
                    residual(j, bank[j][:, :], 0.5)
                dve.wait_ge(residual_ready, 4 * (3 + 3 * l))
                norm(3 + 3 * l, pk2("mix", 0, 8))

                x, e, w, ln, d, m, r_ = [SMX[:, i, :] for i in (0, 2, 3, 4, 5, 6, 1)]
                dve.wait_ge(small_done, l + 1)
                nc.vector.tensor_tensor(tiles(x, 2), tiles(bank[6][:, 0:2 * SMALL], 2), each(pk2("small_b", 0, SMALL), 2),
                                        ALU.add).then_inc(small_x, 1)
                dve.wait_ge(small_x, l + 1)
                nc.vector.scalar_tensor_tensor(SMX[:, 1, :], x, -1.0, x, ALU.mult, ALU.min).then_inc(small_abs, 1)
                dve.wait_ge(small_exp, l + 1)
                nc.vector.tensor_scalar(w, e, 1.0, None, ALU.add).then_inc(small_w, 1)
                dve.wait_ge(small_w, l + 1)
                need(step(nc.vector.tensor_scalar(d, w, -1.0, None, ALU.add)))
                need(step(nc.vector.tensor_scalar(m, d, 0.0, None, ALU.is_equal)))
                need(step(nc.vector.tensor_tensor(d, d, m, ALU.add)))
                need(step(nc.vector.reciprocal(r_, d)))
                need(step(nc.vector.tensor_tensor(r_, r_, e, ALU.mult)))
                dve.wait_ge(small_ln, l + 1)
                need(step(nc.vector.tensor_tensor(ln, ln, m, ALU.add)))
                need(step(nc.vector.tensor_tensor(ln, ln, r_, ALU.mult)))
                need(step(nc.vector.scalar_tensor_tensor(SPL[:, :, :], tiles(x, 2)[:, :, 0:SP_COLS], 0.0,
                                                         tiles(ln, 2)[:, :, 0:SP_COLS], ALU.max, ALU.add)))
                dve.wait_ge(aneg_ready, l + 1)
                nc.vector.scalar_tensor_tensor(LOGA[:, :, :], SPL[:, :, :], -1.0, each(SMX[:, 7, 0:SP_COLS], 2),
                                               ALU.mult, ALU.mult).then_inc(loga_ready, 1)

                w3 = pk2("conv_w", 0, 4 * CONV_TILES).rearrange("p (j n) -> p j n", n=8)
                b3 = pk2("conv_b", 0, CONV_TILES).rearrange("p (j n) -> p j n", n=2)
                with dve.Fori(0, L_CONV // 2) as r:
                    for b in range(2):
                        j = 2 * r + b
                        steps = 16 + 192 * l + 8 * j
                        dve.wait_ge(wide_free, WIDE0 + L_WIDE * l + j + 3)
                        dve.wait_ge(conv_ready, 24 * l + j + 1)
                        for tap in (3, 2, 1, 0):
                            for e2 in range(2):
                                acc, src = CACC[:, b, e2, :], XPAD[:, b, e2, tap:tap + S]
                                wt = w3[:, j, 4 * e2 + tap:4 * e2 + tap + 1]
                                if tap == 3:
                                    ins = nc.vector.tensor_scalar(acc, src, wt, b3[:, j, e2:e2 + 1], ALU.mult, ALU.add)
                                else:
                                    dve.wait_ge(conv_step, steps + 2 * (3 - tap) + e2 - 1)
                                    ins = nc.vector.scalar_tensor_tensor(acc, src, wt, acc, ALU.mult, ALU.add)
                                ins.then_inc(conv_step, 1)

                dve.wait_ge(cum_done, l + 1)
                need(step(nc.vector.tensor_copy(CUM[:, :], bank[6][:, 0:160])))
                nc.vector.tensor_tensor(END_A, LAST_A, CUM_A[:, 0, :], ALU.subtract)
                nc.vector.tensor_tensor(END_G, LAST_G, CUM_G, ALU.subtract)
                nc.vector.tensor_copy(BEG, CUM_G)
                nc.vector.tensor_copy(EXP_C, LAST_C).then_inc(cum_copied, 1)
                dve.wait_ge(ecum_ready, l + 1)
                dve.wait_ge(beta_ready, l + 1)
                step(nc.vector.tensor_tensor(BEG, BEG, BETA[:, :, :], ALU.mult))

                for t in range(2):
                    for q in range(4):
                        dve.wait_ge(xtok_done, 8 * l + 4 * t + q + 1)
                        nc.vector.tensor_tensor(tiles(XDT[:, t, q * 512:(q + 1) * 512], 8), tiles(bank[q][:, :], 8),
                                                spread(SPL[:, t, 8 * q:8 * q + 8], HD), ALU.mult).then_inc(xdt_ready, 1)
                dve.wait_ge(xdt_ready, 8 * l + 8)
                for g in range(GROUPS):
                    nc.vector.tensor_tensor(tiles(XEND[:, g * 512:(g + 1) * 512], 8),
                                            tiles(XDT[:, 0, g * 512:(g + 1) * 512], 8),
                                            spread(END_A[:, 8 * g:8 * g + 8], HD), ALU.mult).then_inc(xend_ready, 1)
                for t in range(2):
                    dve.wait_ge(cb_done, 2 * l + t + 1)
                    nc.vector.tensor_tensor(tiles(CBM[:, t, :], 4), tiles(bank[6 + t][:, :], 4), each(con("cum128"), 4),
                                            ALU.mult).then_inc(cbm_ready, 1)
                dve.wait_ge(cbm_ready, 2 * l + 2)
                dve.wait_ge(wide_free, 2 + WIDE0 + L_WIDE * l + L_CONV + L_ZS)

                def segment(i):
                    t, h0 = i // 8, i % 8 * 4
                    dve.wait_ge(seg_done, 16 * l + i + 1)
                    seg = tiles(SEG[:, i % 2, :], 4)
                    nc.vector.tensor_tensor(seg, tiles(bank[i % 2][:, :], 4), spread(CUM_A[:, t, h0:h0 + 4], P),
                                            ALU.subtract).then_inc(seg_taken, 1)
                    dve.wait_ge(seg_taken, 16 * l + i + 1)
                    nc.vector.tensor_scalar(SEG[:, i % 2, :], SEG[:, i % 2, :], 0.0, None, ALU.min).then_inc(seg_ready, 1)

                def mix(i):
                    t, g = i // 8, i % 8 // 2
                    dve.wait_ge(decay_ready, 16 * l + i + 1)
                    if i >= 2:
                        dve.wait_ge(y_done, 16 * l + i - 1)
                    nc.vector.tensor_tensor(tiles(MIX[:, i % 2, :], 4), tiles(SEG[:, i % 2, :], 4),
                                            each(CBM[:, t, g * P:(g + 1) * P], 4), ALU.mult).then_inc(mix_ready, 1)
                    if t == 1:
                        dve.wait_ge(row_exp_ready, 8 * l + i - 7)
                        nc.vector.tensor_tensor(tiles(CDEC[:, i % 2, :], 4), tiles(CDEC[:, i % 2, :], 4),
                                                each(CONV[:, C_TILE + g, P:2 * P], 4), ALU.mult).then_inc(cdec_ready, 1)

                def scan_out(m):
                    t, g = m // 4, m % 4
                    tok = slice(t * P, (t + 1) * P)
                    dve.wait_ge(y_done, 16 * l + 2 * m + 2)
                    for e2 in range(4):
                        x_ = CONV[:, 4 * g + e2, tok]
                        ins = nc.vector.scalar_tensor_tensor(x_, x_, pk2("ssm_d", 4 * g + e2),
                                                             bank[2 + m % 2][:, e2 * P:(e2 + 1) * P], ALU.mult, ALU.add)
                    ins.then_inc(y_taken, 1)
                    dve.wait_ge(y_taken, 8 * l + m + 1)
                    x_ = CONV[:, 4 * g:4 * g + 4, tok]
                    nc.vector.tensor_tensor(x_, x_, ZS[:, 4 * g:4 * g + 4, tok], ALU.mult).then_inc(yg_ready, 1)

                segment(0)
                for i in range(16):
                    if i + 1 < 16:
                        segment(i + 1)
                    mix(i)
                    if i % 2 == 0 and i >= 2:
                        scan_out(i // 2 - 1)
                scan_out(7)
                for g in range(GROUPS):
                    dve.wait_ge(yrms_ready, 4 * l + g + 1)
                    rs = slice(g % 2 * S, g % 2 * S + S)
                    need(step(nc.vector.reciprocal(RSTD[:, rs], RMS[:, rs])))
                    for e2 in range(4):
                        x_ = CONV[:, 4 * g + e2, :]
                        ins = nc.vector.scalar_tensor_tensor(x_, x_, pk2("ssm_norm", 4 * g + e2), RSTD[:, rs],
                                                             ALU.mult, ALU.mult)
                    ins.then_inc(ys_ready, 1)

                for pr in range(8):
                    dve.wait_ge(qkrms_ready, 8 * l + pr + 1)
                    need(step(nc.vector.reciprocal(ROOT(pr), ROOT(pr))))
                    x_ = QKV[:, 2 * pr:2 * pr + 2, :]
                    nc.vector.scalar_tensor_tensor(x_, x_, P ** -0.5 if pr < 4 else 1.0, tiles(ROOT(pr), 2), ALU.mult,
                                                   ALU.mult).then_inc(qk_ready, 1)
                for t in range(2):
                    tok = slice(t * P, (t + 1) * P)
                    for m_ in range(4):
                        b = m_ % 2
                        at, hs = slice(512 * b, 512 * b + 512), slice(4 * b, 4 * b + 4)
                        dve.wait_ge(kv_done, 8 * l + 4 * t + m_ + 1)
                        src = tiles(bank[m_][:, :], 4)
                        if m_ < 2:
                            nc.vector.tensor_tensor(tiles(KBG[:, at], 4), src, spread(BEG[:, t, hs], P), ALU.mult)
                            nc.vector.tensor_tensor(tiles(KDEC[:, at], 4), src, spread(END_G[:, t, hs], P),
                                                    ALU.mult).then_inc(kv_taken, 1)
                        else:
                            nc.vector.tensor_tensor(tiles(VB[:, at], 4), src, spread(BETA[:, t, hs], P),
                                                    ALU.mult).then_inc(kv_taken, 1)

                    def gseg(b):
                        n, at, hs = 4 * l + 2 * t + b, slice(512 * b, 512 * b + 512), slice(4 * b, 4 * b + 4)
                        dve.wait_ge(kk_done, n + 1)
                        nc.vector.tensor_tensor(tiles(DCY[:, at], 4), tiles(bank[6][:, :], 4),
                                                spread(CUM_G[:, t, hs], P), ALU.subtract).then_inc(gseg_taken, 1)
                        dve.wait_ge(gseg_taken, n + 1)
                        nc.vector.tensor_scalar(DCY[:, at], DCY[:, at], 0.0, None, ALU.min).then_inc(gseg_ready, 1)
                        dve.wait_ge(grow_ready, n + 1)
                        nc.vector.tensor_tensor(QKV[:, hs, tok], QKV[:, hs, tok], tiles(RSTD[:, :], 4),
                                                ALU.mult).then_inc(qd_ready, 1)

                    def weights(b):
                        n, at = 4 * l + 2 * t + b, slice(512 * b, 512 * b + 512)
                        dve.wait_ge(incl_ready, n + 1)
                        nc.vector.tensor_tensor(AQK[:, at], bank[5][:, :], DCY[:, at], ALU.mult).then_inc(aqk_ready, 1)
                        dve.wait_ge(strict_ready, n + 1)
                        need(step(nc.vector.tensor_tensor(MT[:, at], bank[4][:, :], DEC[:, at], ALU.mult)))
                        nc.vector.tensor_tensor(MT[:, at], MT[:, at], bank[7][:, :], ALU.mult).then_inc(mt_ready, 1)

                    for b in range(2):
                        gseg(b)
                        weights(b)
                    for v in range(LEVELS):
                        k = (2 * l + t) * LEVELS + v
                        kc = (2 * l + t) * (LEVELS - 1) + v - 1
                        for b in range(2):
                            at = slice(512 * b, 512 * b + 512)
                            if v == 0:
                                dve.wait_ge(inv_u_done, 2 * k + b + 1)
                                nc.vector.tensor_tensor(tiles(TI[:, at], 4), each(con("ident"), 4),
                                                        tiles(bank[b][:, :], 4), ALU.subtract)
                                nc.vector.tensor_tensor(tiles(TT[:, at], 4), each(con("ident"), 4),
                                                        tiles(CS[:, at], 4), ALU.subtract).then_inc(inv_ready, 1)
                                continue
                            dve.wait_ge(inv_ready, 2 * k + b - 1)
                            dve.wait_ge(inv_v_done, 2 * kc + b + 1)
                            if v < LEVELS - 1:
                                nc.vector.tensor_tensor(TI[:, at], TI[:, at], bank[2 + b][:, :], ALU.subtract)
                            nc.vector.tensor_tensor(TT[:, at], TT[:, at], bank[6 + b][:, :],
                                                    ALU.subtract).then_inc(inv_ready, 1)
                    for c in range(2):
                        cg, r0 = 2 * t + c, t * P + 64 * c
                        dve.wait_ge(o_done, 4 * l + cg + 1)
                        nc.vector.tensor_copy(QKV[:, 0:DN_HEADS, r0:r0 + 64],
                                              tiles(bank[6][:, :], 8)).then_inc(o_copied, 1)
                        for b in range(2 if cg < 3 else 0):
                            at = slice(512 * b, 512 * b + 512)
                            if cg >= 1:
                                need(step(nc.vector.tensor_tensor(tiles(ST[:, at], 4), tiles(ST[:, at], 4),
                                                                  spread(EXP_C[:, cg, 4 * b:4 * b + 4], P), ALU.mult)))
                            dve.wait_ge(st_done, 6 * l + 2 * cg + b + 1)
                            if cg >= 1:
                                nc.vector.tensor_tensor(ST[:, at], ST[:, at], bank[b][:, :],
                                                        ALU.add).then_inc(st_ready, 1)
                            else:
                                nc.vector.tensor_copy(ST[:, at], bank[b][:, :]).then_inc(st_ready, 1)
                for pr in range(4):
                    dve.wait_ge(orms_ready, 4 * l + pr + 1)
                    need(step(nc.vector.reciprocal(ROOT(pr), ROOT(pr))))
                    x_ = QKV[:, 2 * pr:2 * pr + 2, :]
                    need(step(nc.vector.scalar_tensor_tensor(x_, x_, pk2("dn_norm"), tiles(ROOT(pr), 2), ALU.mult,
                                                             ALU.mult)))
                    nc.vector.tensor_tensor(x_, x_, ZD[:, 2 * pr:2 * pr + 2, :], ALU.mult).then_inc(yd_ready, 1)

                dve.wait_ge(wide_free, 2 + WIDE0 + L_WIDE * l + L_WIDE)
                for c in range(4):
                    dve.wait_ge(panel_used, used0 + LQ_PROJ + 3 * (c + 1))
                    merge(c, 4 + 4 * l, bank[c % 2 * 2], bank[c % 2 * 2 + 1], GT[:, 0:8, :], GT[:, 8:16, :],
                          SG[:, c % 2, :], HID[:, c % 2, :])
                for j in range(4):
                    dve.wait_ge(panel_used, used0 + LQ_WOUT + j + 1)
                    residual(j, bank[6 + j % 2][:, :], 1.0)
                dve.wait_ge(residual_ready, 4 * (4 + 3 * l))
                norm(4 + 3 * l, pk2("ffn2", 0, 8))
                ffn_hidden(2 + 2 * l)
                dve.wait_ge(panel_used, used0 + L_PANELS)
                for j in range(4):
                    residual(j, bank[j][:, :], 0.5)
                dve.wait_ge(residual_ready, 4 * (5 + 3 * l))
                pad(DVE_LAYER)
            base[0] = DVE_B1 + DVE_LAYER * LAYERS
            norm(2 + 3 * LAYERS, pk1("final", 0, 8))


def _wide_panels(w):
    n = w.shape[1] // 256
    return w.reshape(KT, P, n, 256).transpose(2, 1, 0, 3).reshape(n, P, PANEL)


def _ffn_panels(w_in, w_out):
    gu = w_in.reshape(KT, P, 2, 2 * HID_PAIRS, P).transpose(3, 1, 0, 2, 4).reshape(2 * HID_PAIRS, P, PANEL)
    dn = w_out.reshape(HID_PAIRS, 2, P, D).transpose(0, 2, 1, 3).reshape(HID_PAIRS, P, PANEL)
    order = [gu[0], gu[1]]
    for i in range(HID_PAIRS):
        if i + 1 < HID_PAIRS:
            order += [gu[2 * i + 2], gu[2 * i + 3]]
        order.append(dn[i])
    return np.stack(order)


def _columns_of(v):
    return v.reshape(-1, P).T


def _pack(layout, width, parts):
    out = np.zeros((P, width), np.float32)
    for name, part in parts.items():
        a, b = layout[name]
        out[:, a:b] = part
    return out


def _constants():
    i = np.arange(P)
    s, l = i[:, None], i[None, :]
    same = s // 64 == l // 64
    parts = {
        "ident": s == l, "cum128": s <= l, "cum64": same & (s <= l), "strict64": same & (s < l), "same64": same,
        "half0": (s < 64) & (l >= 0), "half1": (s >= 64) & (l >= 0),
    }
    levels = []
    for v in range(LEVELS):
        n = 1 << v
        levels.append((s // (2 * n) == l // (2 * n)) & (s // n % 2 == 0) & (l // n % 2 == 1))
    parts["levels"] = np.concatenate(levels, 1)
    return _pack(CONSTS, CONSTS_N, parts)


def _rope_constants():
    i = np.arange(P)
    half = HD // 8
    inv = np.float32(500000.0) ** (-(np.arange(half, dtype=np.float32) * np.float32(2.0)) / np.float32(2 * half))
    ang = np.arange(S, dtype=np.float32)[:, None] * inv[None, :]
    cos, sin = np.ones((P, S), np.float32), np.zeros((P, S), np.float32)
    swap = np.zeros((P, P), np.float32)
    for at in (0, HD):
        for d in range(half):
            cos[at + d] = cos[at + half + d] = np.cos(ang[:, d])
            sin[at + d] = sin[at + half + d] = np.sin(ang[:, d])
            swap[at + half + d, at + d] = -1.0
            swap[at + d, at + half + d] = 1.0
    q, k = np.arange(S)[:, None], np.arange(S)[None, :]
    masks = []
    for window, dil in ((128, 1), (512, 4), (2048, 16)):
        seen = (np.abs(q - k) % dil == 0) & (np.abs(q - k) // dil <= window // 2 // dil)
        masks.append(np.where(seen, 0.0, NEG))
    dil_masks = np.stack(masks).reshape(DIL_GROUPS, 2, P, S).transpose(2, 1, 0, 3).reshape(P, -1)
    return _pack(ROPES, ROPES_N, {"head64": (i[:, None] // HD == i[None, :] // HD) / HD, "swap": swap, "cos": cos,
                                  "sin": sin, "dil": dil_masks})


def _na_bias(rpb):
    rows = S // GRID_W
    kh = min(NA_KH, rows)
    pos = np.arange(S)
    r, c = pos // GRID_W, pos % GRID_W
    assert kh == rows
    row_off = r[None, :] - r[:, None] + NA_KH - 1
    start = np.clip(c - NA_KW // 2, 0, GRID_W - NA_KW)
    seen = (c[None, :] >= start[:, None]) & (c[None, :] < start[:, None] + NA_KW)
    col_off = np.clip(c[None, :] - c[:, None] + NA_KW - 1, 0, 2 * NA_KW - 2)
    flat = np.concatenate([rpb.reshape(NA_HEADS, -1), np.full((NA_HEADS, 1), NEG, np.float32)], 1)
    at = np.where(seen, row_off * (2 * NA_KW - 1) + col_off, flat.shape[1] - 1)
    return flat[:, at].reshape(NA_HEADS, 2, P, S).transpose(2, 0, 1, 3).reshape(P, NA_UNITS * S)


def _layout(a):
    w_in = a["w_in"][0]
    wa, wb = 512, 768
    qa, ka, va, qb, kb, vb, gates = np.split(w_in, np.cumsum([wa, wa, wa, wb, wb, wb]), axis=1)
    wpa = a["w_proj_a"][0].reshape(4, P, 2, 512).transpose(2, 1, 0, 3).reshape(2, P, PANEL)
    wpb = a["w_proj_b"][0].reshape(2, P, D).transpose(1, 0, 2).reshape(1, P, PANEL)
    stream = [_wide_panels(a["w_ada"][0]), _wide_panels(np.concatenate([qa, ka, qb, kb, gates], 1)),
              _wide_panels(np.concatenate([va, vb], 1)), wpa, wpb, _wide_panels(a["w_o"][0]),
              _ffn_panels(a["w_ffn_in"][0], a["w_ffn_out"][0])]
    packs = []
    for l in range(LAYERS):
        stream.append(_ffn_panels(a["ffn1_w_in_2"][l], a["ffn1_w_out_2"][l]))
        z, xbc, dt, qkv, zd, b_, a_, gs, gd = np.split(
            a["w_in_2"][l], np.cumsum([2048, 3072, 32, 3072, 1024, 8, 8, 1024]), axis=1)
        stream.append(_wide_panels(np.concatenate([xbc, qkv, z, zd, gs, gd], 1)))
        ssm = _wide_panels(a["ssm_w_branch_2"][l][:D]), _wide_panels(a["ssm_w_branch_2"][l][D:])
        dn = _wide_panels(a["dn_w_branch_2"][l])
        stream.append(np.stack([x for c in range(4) for x in (ssm[0][c], ssm[1][c], dn[c])]))
        stream.append(_wide_panels(a["w_out_2"][l]))
        stream.append(_ffn_panels(a["ffn2_w_in_2"][l], a["ffn2_w_out_2"][l]))
        conv_w = np.concatenate([a["ssm_conv_w_2"][l], a["dn_conv_w_2"][l]], 1)
        small_w = np.concatenate([dt, a_, b_], 1).reshape(KT, P, SMALL).transpose(1, 0, 2).reshape(P, KT * SMALL)
        packs.append(_pack(PACK2, PACK2_N, {
            "ffn1": _columns_of(a["ffn1_norm_2"][l]), "mix": _columns_of(a["mix_norm_2"][l]),
            "ffn2": _columns_of(a["ffn2_norm_2"][l]),
            "conv_w": conv_w.reshape(4, CONV_TILES, P).transpose(2, 1, 0).reshape(P, 4 * CONV_TILES),
            "conv_b": np.concatenate([_columns_of(a["ssm_conv_b_2"][l]), np.zeros((P, QKV_TILES), np.float32)], 1),
            "ssm_norm": _columns_of(a["ssm_norm_2"][l]), "ssm_d": _columns_of(np.repeat(a["ssm_d_2"][l], HD)),
            "dn_norm": _columns_of(a["dn_norm_2"][l]),
            "small_b": np.concatenate([a["ssm_dt_bias_2"][l], a["dn_dt_bias_2"][l], np.zeros(8, np.float32)]),
            "a_log": np.concatenate([a["ssm_a_log_2"][l], a["dn_a_log_2"][l]]), "small_w": small_w}))
    two = lambda g: np.concatenate([g, g])[:, None]
    pack1 = _pack(PACK1, PACK1_N, {
        "c": _columns_of(a["c"][0]), "b_ada": _columns_of(a["b_ada"][0]), "g1": _columns_of(a["g_norm1"][0]),
        "g2": _columns_of(a["g_norm2"][0]), "b_gate": _columns_of(a["b_gate"][0]),
        "final": _columns_of(a["final_norm_2"]), "g_qa": two(a["g_qa"][0]), "g_ka": two(a["g_ka"][0]),
        "g_qb": two(a["g_qb"][0]), "g_kb": two(a["g_kb"][0])})
    return {
        "w_stream": np.concatenate(stream), "x_t": a["x"][0].T.reshape(KT, P, S).transpose(1, 0, 2),
        "pack1": pack1, "pack2": np.stack(packs), "consts": _constants(), "ropes": _rope_constants(),
        "na_bias": _na_bias(a["rpb"][0])}


def kernel(**inputs):
    import concourse.bacc as bacc
    from concourse.bass_utils import run_bass_kernel_spmd

    laid = {k: np.ascontiguousarray(v, np.float32) for k, v in _layout({k: np.asarray(v) for k, v in inputs.items()}).items()}
    nc = bacc.Bacc("TRN2", target_bir_lowering=False, num_devices=1)
    args = {k: nc.dram_tensor(f"in_{k}", v.shape, F32, kind="ExternalInput").ap() for k, v in laid.items()}
    args["out_t"] = nc.dram_tensor("out_t", (P, KT, S), F32, kind="ExternalOutput").ap()
    build_program(nc, **args)
    r = run_bass_kernel_spmd(nc, [{f"in_{k}": v for k, v in laid.items()}], core_ids=[0])
    out = r.results[0]["out_t"]
    return out.transpose(1, 0, 2).reshape(D, S).T[None]
```

```python
import concourse.bass as bass
from concourse import mybir
from contextlib import ExitStack
import numpy as np

F32 = mybir.dt.float32
F32R = mybir.dt.float32r
ACT = mybir.ActivationFunctionType
ALU = mybir.AluOpType
AX = mybir.AxisListType

P = 128
S = 256
D = 1024
KT = D // P
HD = 64
FF = 2816
HID_PAIRS = FF // (2 * P)
LAYERS = 2
EPS = 1e-6
NEG = -1e30

QA, KA, QB, KB, GATE = 0, 4, 8, 14, 20
V_COLS = 512 + 768
GRID_W, NA_KH, NA_KW = 64, 8, 16
NA_HEADS, DIL_SLOTS, DIL_GROUPS = 8, 4, 3
NA_UNITS, DIL_UNITS = 2 * NA_HEADS, 2 * DIL_SLOTS
UNITS = NA_UNITS + DIL_UNITS

XBC_TILES, QKV_TILES, ZS_TILES, ZD_TILES = 24, 24, 16, 8
CONV_TILES = XBC_TILES + QKV_TILES
B_TILE, C_TILE = 16, 20
GROUPS = 4
SSM_HEADS = 32
DN_HEADS = 8
SMALL = 48
SP_COLS = 40

PANEL = 2048
RING = 3
PARTS = 2
ROUND = 6
ADA_FIRST, ADA_PANELS = 8, 24
B1_WIDE, B1_V, B1_PROJ, B1_WO = 18, 5, 3, 4
FFN_PANELS = 3 * HID_PAIRS
Q_WIDE1 = 0
Q_V = Q_WIDE1 + B1_WIDE
Q_PROJ1 = Q_V + B1_V
Q_WO = Q_PROJ1 + B1_PROJ
Q_FFN0 = Q_WO + B1_WO
Q_LAYERS = Q_FFN0 + FFN_PANELS
L_CONV = CONV_TILES // 2
L_ZS, L_ZD, L_GATES = ZS_TILES // 2, ZD_TILES // 2, KT
L_WIDE = L_CONV + L_ZS + L_ZD + L_GATES
L_PROJ, L_WOUT = 12, 4
LQ_FFN1 = 0
LQ_WIDE = LQ_FFN1 + FFN_PANELS
LQ_PROJ = LQ_WIDE + L_WIDE
LQ_WOUT = LQ_PROJ + L_PROJ
LQ_FFN2 = LQ_WOUT + L_WOUT
L_PANELS = LQ_FFN2 + FFN_PANELS
N_PANELS = Q_LAYERS + LAYERS * L_PANELS
assert L_PANELS % ROUND == 0 and Q_FFN0 % ROUND == 0 and B1_WIDE % ROUND == 0 and L_CONV % ROUND == 0
L_ROUNDS = L_PANELS // ROUND
assert N_PANELS % RING == 0
WIDE0 = B1_WIDE + B1_V

def columns(sizes):
    at, out = 0, {}
    for name, n in sizes:
        out[name] = (at, at + n)
        at += n
    return out, at


PACK1, PACK1_N = columns([("c", 8), ("b_ada", 48), ("g1", 8), ("g2", 8), ("b_gate", 16), ("final", 8),
                          ("g_qa", 1), ("g_ka", 1), ("g_qb", 1), ("g_kb", 1)])
PACK2, PACK2_N = columns([("ffn1", 8), ("mix", 8), ("ffn2", 8), ("conv_w", 4 * CONV_TILES), ("conv_b", CONV_TILES),
                          ("ssm_norm", 16), ("ssm_d", 16), ("dn_norm", 1), ("small_b", SMALL), ("a_log", SP_COLS),
                          ("small_w", KT * SMALL)])
LEVELS = 6
CONSTS, CONSTS_N = columns([("ident", P), ("cum128", P), ("cum64", P), ("strict64", P), ("same64", P),
                            ("half0", P), ("half1", P), ("levels", LEVELS * P)])
ROPES, ROPES_N = columns([("head64", P), ("swap", P), ("cos", S), ("sin", S), ("dil", DIL_GROUPS * 2 * S)])

DVE_B1, DVE_LAYER = 256, 512


def build_program(nc, w_stream, ada_stream, x_t, pack1, pack2, consts, ropes, na_bias, out_t):
    with ExitStack() as ctx:
        def sb(name, shape):
            return ctx.enter_context(nc.sbuf_tensor(name, shape, F32))

        def sem(name):
            return ctx.enter_context(nc.semaphore(name))

        ARENA_N = CONV_TILES * S + 10752
        ARENA = sb("ARENA", [P, ARENA_N])
        arena_at = nc.sbuf_base - 4 * ARENA_N

        def part_over(name, at, shape):
            return nc.alloc_sbuf_tensor_at(name, shape, F32R, offset=arena_at + 4 * at)

        ring = sb("ring", [P, RING, PANEL])
        H = sb("H", [P, KT, S])
        SQ = sb("SQ", [P, KT * S])
        U = SQ[:, :].rearrange("p (t n) -> p t n", t=KT)

        def sb_part(name, shape):
            return ctx.enter_context(nc.sbuf_tensor(name, shape, F32R))

        HI, LO = sb_part("HI", [P, PARTS, PANEL]), sb_part("LO", [P, PARTS, PANEL])
        UH, UL = sb_part("UH", [P, KT, S]), sb_part("UL", [P, KT, S])
        RMS = sb("RMS", [P, 512])
        RSTD = sb("RSTD", [P, 512])
        PK1 = sb("PK1", [P, PACK1_N])
        PK2 = sb("PK2", [P, PACK2_N])
        CON = sb("CON", [P, CONSTS_N])
        MEAN_D = sb("MEAN_D", [P, P])
        MEAN_G = sb("MEAN_G", [P, P])
        MEAN_V = sb("MEAN_V", [P, P])
        ONES = sb("ONES", [P, P])
        EPST = sb("EPST", [P, 1])
        XPAD = sb("XPAD", [P, 2, 2, S + 3])
        taken = [0]

        def region(n):
            taken[0] += n
            assert taken[0] <= ARENA_N, taken
            return ARENA[:, taken[0] - n:taken[0]]

        FFN_AT = ARENA_N - 4096
        SG = ARENA[:, FFN_AT:FFN_AT + 1024].rearrange("p (b n) -> p b n", b=2)
        HID = ARENA[:, FFN_AT + 1024:FFN_AT + 2048].rearrange("p (b n) -> p b n", b=2)
        HIDH = part_over("HIDH", FFN_AT + 2048, [P, 2, 512])
        HIDL = part_over("HIDL", FFN_AT + 3072, [P, 2, 512])

        PROJ = region(36 * S).rearrange("p (t n) -> p t n", t=36)
        VT = region(2 * V_COLS).rearrange("p (t n) -> p t n", t=2)
        BIAS_AT = taken[0]
        BIAS = region(NA_UNITS * S).rearrange("p (u n) -> p u n", u=NA_UNITS)
        ROP = region(ROPES_N)
        SC_AT = taken[0]
        SC = region(2 * 768).rearrange("p (b n) -> p b n", b=2)
        PT = region(2 * 768).rearrange("p (b n) -> p b n", b=2)
        NMAX = region(2 * UNITS)
        DEN = region(UNITS)
        RDEN = region(UNITS)
        OTOK = region(2 * 768).rearrange("p (t n) -> p t n", t=2)
        RSH = ARENA[:, SC_AT:SC_AT + 8 * 512].rearrange("p (t n) -> p t n", t=8)
        MTMP = ARENA[:, SC_AT:SC_AT + 2048].rearrange("p (t n) -> p t n", t=4)
        OTH, OTL = part_over("OTH", BIAS_AT, [P, 6, S]), part_over("OTL", BIAS_AT + 6 * S, [P, 6, S])
        ADA1 = ARENA[:, 0:ADA_FIRST * PANEL].rearrange("p (b n) -> p b n", b=ADA_FIRST)
        ADA2 = ARENA[:, BIAS_AT:BIAS_AT + 2 * PANEL].rearrange("p (b n) -> p b n", b=2)
        ADA_SUM = ARENA[:, SC_AT:SC_AT + 4096].rearrange("p (b n) -> p b n", b=16)
        assert ADA_FIRST * PANEL <= SC_AT
        MOD = sb("MOD", [P, 48])
        CACT = sb("CACT", [P, 8])
        GS = sb("GS", [P, 24])

        taken[0] = 0
        CONV = region(CONV_TILES * S).rearrange("p (t n) -> p t n", t=CONV_TILES)
        TMP_AT = taken[0]
        QKV = CONV[:, XBC_TILES:, :]
        ZD = CONV[:, B_TILE:B_TILE + ZD_TILES, :]
        GT = QKV[:, DN_HEADS:DN_HEADS + 2 * KT, :]
        CACC = ARENA[:, TMP_AT:TMP_AT + 1024].rearrange("p (b t n) -> p b t n", b=2, t=2)
        SMX = sb("SMX", [P, 8, 2 * SMALL])
        SPL = sb("SPL", [P, 2, SP_COLS])
        LOGA = sb("LOGA", [P, 2, SP_COLS])
        BETA = sb("BETA", [P, 2, DN_HEADS])
        CUM = sb("CUM", [P, 160])
        CUM_A = CUM[:, 0:64].rearrange("p (t h) -> p t h", t=2)
        CUM_G = CUM[:, 64:80].rearrange("p (t h) -> p t h", t=2)
        LAST_G = CUM[:, 80:96].rearrange("p (t h) -> p t h", t=2)
        LAST_A = CUM[:, 96:128]
        LAST_C = CUM[:, 128:160].rearrange("p (c h) -> p c h", c=4)
        ECUM = sb("ECUM", [P, 128])
        END_A = ECUM[:, 0:32]
        END_G = ECUM[:, 32:48].rearrange("p (t h) -> p t h", t=2)
        BEG = ECUM[:, 48:64].rearrange("p (t h) -> p t h", t=2)
        EXP_C = ECUM[:, 64:96].rearrange("p (c h) -> p c h", c=4)
        XDT = region(2 * 2048).rearrange("p (t n) -> p t n", t=2)
        STATE = region(2048)
        CBM = region(2 * 512).rearrange("p (t n) -> p t n", t=2)
        BTOK = region(512)
        SEG = region(2 * 512).rearrange("p (b n) -> p b n", b=2)
        MIX = region(2 * 512).rearrange("p (b n) -> p b n", b=2)
        CDEC = region(2 * 512).rearrange("p (b n) -> p b n", b=2)
        XEND = SQ
        ZT = SEG
        YSL, YDL = part_over("YSL", 0, [P, 16, S]), part_over("YDL", XBC_TILES * S, [P, 8, S])
        YSH, YDH = part_over("YSH", TMP_AT, [P, 16, S]), part_over("YDH", TMP_AT + 16 * S, [P, 8, S])
        taken[0] = TMP_AT
        KBG = region(1024)
        KDEC = region(1024)
        VB = region(1024)
        MT = region(1024)
        AQK = region(1024)
        TI = region(1024)
        TT = region(1024)
        UB = region(1024)
        DEC = region(1024)
        DCY = region(1024)
        ST = SQ[:, 0:1024]
        CS = SQ[:, 1024:2048]
        WT = UB

        def ROOT(pr):
            return (DEC, DCY)[pr % 4 // 2][:, pr % 2 * 512:pr % 2 * 512 + 512]

        VN = MT

        bank = [ctx.enter_context(nc.psum_tensor(f"bank{i}", [P, 512], F32)) for i in range(8)]

        panel_loaded = [sem(f"panel_loaded{i}") for i in range(RING)]
        hi_ready, lo_ready = sem("hi_ready"), sem("lo_ready")
        panel_used = sem("panel_used")
        uh_ready, ul_ready = sem("uh_ready"), sem("ul_ready")
        ada1_loaded = [sem(f"ada1_loaded{i}") for i in range(ADA_FIRST)]
        ada2_loaded = [sem(f"ada2_loaded{i}") for i in range(2)]
        ada1_step, ada2_step, ada_done, ada_copied = sem("ada1_step"), sem("ada2_step"), sem("ada_done"), sem("ada_copied")
        hid_product, hidh_ready = sem("hid_product"), sem("hidh_ready")
        oth_ready, otl_ready = sem("oth_ready"), sem("otl_ready")
        branch_hi, branch_lo = sem("branch_hi"), sem("branch_lo")
        x_loaded, pack1_loaded, consts_loaded = sem("x_loaded"), sem("pack1_loaded"), sem("consts_loaded")
        bias_loaded, ropes_loaded, pack2_loaded = sem("bias_loaded"), sem("ropes_loaded"), sem("pack2_loaded")
        fills_done = sem("fills_done")
        out_stored = sem("out_stored")
        dve_done = sem("dve_done")
        residual_ready, squares_ready, sumsq_ready = sem("residual_ready"), sem("squares_ready"), sem("sumsq_ready")
        rms_ready, u_ready = sem("rms_ready"), sem("u_ready")
        wide_free = sem("wide_free")
        conv_step, conv_ready = sem("conv_step"), sem("conv_ready")
        gate_act_ready, hidden_ready = sem("gate_act_ready"), sem("hidden_ready")
        c_ready = sem("c_ready")
        hsq_ready, hss_ready, hrms_ready = sem("hsq_ready"), sem("hss_ready"), sem("hrms_ready")
        pt_half = sem("pt_half")
        rope_in, rope_done, heads_ready, gates_ready = (
            sem("rope_in"), sem("rope_done"), sem("heads_ready"), sem("gates_ready"))
        scores_done, scored, nmax_ready, probs_ready = (
            sem("scores_done"), sem("scored"), sem("nmax_ready"), sem("probs_ready"))
        pt_done, pt_copied, pv_done, otok_ready = sem("pt_done"), sem("pt_copied"), sem("pv_done"), sem("otok_ready")
        ot_done = sem("ot_done")
        proj_done, merged_ready = sem("proj_done"), sem("merged_ready")
        small_done, small_x, small_abs, small_exp, small_w, small_ln = (
            sem("small_done"), sem("small_x"), sem("small_abs"), sem("small_exp"), sem("small_w"), sem("small_ln"))
        beta_ready, aneg_ready, loga_ready, cum_done, cum_copied, ecum_ready, beg_ready = (
            sem("beta_ready"), sem("aneg_ready"), sem("loga_ready"), sem("cum_done"), sem("cum_copied"),
            sem("ecum_ready"), sem("beg_ready"))
        xtok_done, xdt_ready, btok_done, btok_copied, xend_ready = (
            sem("xtok_done"), sem("xdt_ready"), sem("btok_done"), sem("btok_copied"), sem("xend_ready"))
        state_done, state_copied, cb_done, cbm_ready = (
            sem("state_done"), sem("state_copied"), sem("cb_done"), sem("cbm_ready"))
        seg_done, seg_taken, seg_ready, row_exp_ready, decay_ready, mix_ready, cdec_ready = (
            sem("seg_done"), sem("seg_taken"), sem("seg_ready"), sem("row_exp_ready"), sem("decay_ready"),
            sem("mix_ready"), sem("cdec_ready"))
        y_done, y_taken, yg_ready, ysq_ready, yss_done, yrms_ready, ys_ready = (
            sem("y_done"), sem("y_taken"), sem("yg_ready"), sem("ysq_ready"), sem("yss_done"), sem("yrms_ready"),
            sem("ys_ready"))
        qksq_ready, qkss_done, qkrms_ready, qk_ready = (
            sem("qksq_ready"), sem("qkss_done"), sem("qkrms_ready"), sem("qk_ready"))
        kv_done, kv_taken, kk_done, gseg_taken, gseg_ready, grow_ready, gdec_ready = (
            sem("kv_done"), sem("kv_taken"), sem("kk_done"), sem("gseg_taken"), sem("gseg_ready"),
            sem("grow_ready"), sem("gdec_ready"))
        strict_ready, incl_ready, mt_ready, aqk_ready, qd_ready = (
            sem("strict_ready"), sem("incl_ready"), sem("mt_ready"), sem("aqk_ready"), sem("qd_ready"))
        cs_ready, inv_u_done, inv_u_copied, inv_v_done, inv_ready = (
            sem("cs_ready"), sem("inv_u_done"), sem("inv_u_copied"), sem("inv_v_done"), sem("inv_ready"))
        wt_done, wt_copied, vn_done, vn_copied, o_done, o_copied, st_done, st_ready = (
            sem("wt_done"), sem("wt_copied"), sem("vn_done"), sem("vn_copied"), sem("o_done"), sem("o_copied"),
            sem("st_done"), sem("st_ready"))
        osq_ready, oss_done, orms_ready, yd_ready = (
            sem("osq_ready"), sem("oss_done"), sem("orms_ready"), sem("yd_ready"))

        def con(name):
            return CON[:, CONSTS[name][0]:CONSTS[name][1]]

        def rop(name):
            return ROP[:, ROPES[name][0]:ROPES[name][1]]

        def pk1(name, i=0, n=1):
            return PK1[:, PACK1[name][0] + i:PACK1[name][0] + i + n]

        def pk2(name, i=0, n=1):
            return PK2[:, PACK2[name][0] + i:PACK2[name][0] + i + n]

        def tiles(x, t):
            return x.rearrange("p (t n) -> p t n", t=t)

        def spread(x, n):
            return x.unsqueeze(2).to_broadcast([P, x.shape[1], n])

        def each(x, h):
            return x.unsqueeze(1).to_broadcast([P, h, x.shape[1]])

        def norm_no(l, i):
            return 2 + 3 * l + i

        FILL_B1_NORM1, FILL_B1_MERGE, FILL_B1_NORM2, FILL_LAYER = 0, 1, 2, 3

        block = ctx.enter_context(nc.Block())

        @block.sync
        def _(sp):
            for i in range(ADA_FIRST):
                sp.dma_start(ADA1[:, i, :], ada_stream[i]).then_inc(ada1_loaded[i], 16)

            def load(q, slot):
                sp.dma_start(ring[:, slot, :], w_stream[q]).then_inc(panel_loaded[slot], 16)

            for q in range(RING):
                load(q, q)
            with sp.Fori(1, N_PANELS // RING) as r:
                for s in range(RING):
                    sp.wait_ge(lo_ready, (r - 1) * RING + s + 1)
                    load(r * RING + s, s)
            sp.wait_ge(u_ready, KT * (norm_no(LAYERS, 0) + 1))
            sp.dma_start(out_t, U[:, :, :]).then_inc(out_stored, 16)
            sp.wait_ge(out_stored, 16)

        @block.gpsimd
        def _(pool):
            pool.dma_start(CON[:, :], consts).then_inc(consts_loaded, 16)
            pool.wait_ge(ada1_step, KT * ADA_FIRST)
            for b in range(2):
                pool.dma_start(ADA2[:, b, :], ada_stream[ADA_FIRST + b]).then_inc(ada2_loaded[b], 16)
            pool.dma_start(ROP, ropes).then_inc(ropes_loaded, 16)
            pool.wait_ge(ada_copied, 1)
            sums4 = ADA_SUM.rearrange("p (r b) n -> p r b n", b=2)

            def ada_sum(r, b):
                pool.wait_ge(ada2_loaded[b], 16 * r + 16)
                src, done = tiles(ADA2[:, b, :], KT), 8 * r + 4 * b
                nc.gpsimd.tensor_tensor(src, src, spread(CACT[:, :], S), ALU.mult).then_inc(ada2_step, 1)
                for i, n in enumerate((4, 2)):
                    pool.wait_ge(ada2_step, done + i + 1)
                    nc.gpsimd.tensor_tensor(src[:, 0:n, :], src[:, 0:n, :], src[:, n:2 * n, :],
                                            ALU.add).then_inc(ada2_step, 1)
                pool.wait_ge(ada2_step, done + 3)
                nc.gpsimd.tensor_tensor(sums4[:, r, b, :], src[:, 0, :], src[:, 1, :], ALU.add).then_inc(ada2_step, 1)

            last = (ADA_PANELS - ADA_FIRST) // 2 - 1
            with pool.Fori(0, last) as r:
                for b in range(2):
                    ada_sum(r, b)
                    pool.wait_ge(ada2_step, 8 * r + 4 * b + 4)
                    pool.dma_start(ADA2[:, b, :], ada_stream[ADA_FIRST + 2 + 2 * r + b]).then_inc(ada2_loaded[b], 16)
            for b in range(2):
                ada_sum(last, b)
            pool.wait_ge(ada2_step, 8 * last + 8)
            pool.dma_start(BIAS, na_bias).then_inc(bias_loaded, 16)
            pool.wait_ge(consts_loaded, 16)
            with pool.Fori(0, LAYERS) as l:
                pool.wait_ge(u_ready, KT * (2 + 3 * l))
                pool.dma_start(PK2[:, :], pack2[l]).then_inc(pack2_loaded, 16)
                for t in range(2):
                    for b in range(2):
                        n = 4 * l + 2 * t + b
                        d = tiles(DEC[:, 512 * b:512 * b + 512], 4)
                        pool.wait_ge(gdec_ready, n + 1)
                        nc.gpsimd.tensor_tensor(tiles(DCY[:, 512 * b:512 * b + 512], 4), d, each(con("cum64"), 4),
                                                ALU.mult).then_inc(incl_ready, 1)
                        nc.gpsimd.tensor_tensor(d, d, each(con("strict64"), 4), ALU.mult).then_inc(strict_ready, 1)
                    for v in range(LEVELS):
                        for b in range(2):
                            k = (2 * l + t) * LEVELS + v
                            if v == 0:
                                pool.wait_ge(mt_ready, 4 * l + 2 * t + b + 1)
                            elif v == 1:
                                pool.wait_ge(inv_ready, 2 * (k - 1) + b + 1)
                            else:
                                pool.wait_ge(inv_u_done, 2 * (k - 1) + b + 1)
                            lev = con("levels")[:, v * P:(v + 1) * P]
                            nc.gpsimd.tensor_tensor(tiles(CS[:, 512 * b:512 * b + 512], 4),
                                                    tiles(MT[:, 512 * b:512 * b + 512], 4), each(lev, 4),
                                                    ALU.mult).then_inc(cs_ready, 1)

        @block.tensor
        def _(pe):
            def panel(q, rounds=0):
                pe.wait_ge(lo_ready, q + 1 + ROUND * rounds)
                return HI[:, q % PARTS, :], LO[:, q % PARTS, :]

            def product(out, left, right, start, stop, **kw):
                (lh, ll), (rh, rl) = left, right
                nc.tensor.matmul(out, lh, rh, start=start, stop=False, **kw)
                nc.tensor.matmul(out, lh, rl, start=False, stop=False, **kw)
                return nc.tensor.matmul(out, ll, rh, start=False, stop=stop, **kw)

            def both(parts, f):
                return f(parts[0]), f(parts[1])

            def u_parts(k):
                return UH[:, k, :], UL[:, k, :]

            def norm(n, fill):
                for k in range(KT // 2):
                    pe.wait_ge(squares_ready, KT // 2 * n + k + 1)
                    for e in range(2):
                        mm = nc.tensor.matmul(bank[4][:, 0:S], MEAN_D[:, :], SQ[:, (2 * k + e) * S:(2 * k + e + 1) * S],
                                              start=(k + e == 0), stop=(k == KT // 2 - 1 and e == 1))
                mm.then_inc(sumsq_ready, 1)
                if fill is not None:
                    pe.wait_ge(ul_ready, 4 * fill + 4)

            def wide(w, q, rounds, par):
                src = both(panel(q, rounds), lambda x: tiles(x, KT))
                pe.wait_ge(wide_free, w + 1)
                for e in range(2):
                    for k in range(KT):
                        mm = product(bank[4 + par][:, e * S:(e + 1) * S], both(src, lambda x: x[:, k, e * P:(e + 1) * P]),
                                     u_parts(k), start=(k == 0), stop=(k == KT - 1))
                mm.then_inc(panel_used, 1)

            def ffn(f, q0, rounds):
                def gate_up(q, rr, par):
                    for e in range(2):
                        src = both(panel(q + e, rr), lambda x: tiles(x, KT))
                        for half in range(2):
                            for k in range(KT):
                                mm = product(bank[4 + 2 * par + half][:, e * S:(e + 1) * S],
                                             both(src, lambda x: x[:, k, half * P:(half + 1) * P]), u_parts(k),
                                             start=(k == 0), stop=(k == KT - 1))
                        mm.then_inc(panel_used, 1)

                def down(i, q, rr, par, first=False, last=False):
                    src = panel(q, rr)
                    pe.wait_ge(hidden_ready, f * HID_PAIRS + i + 1)
                    for e in range(2):
                        for j in range(KT):
                            mm = product(bank[j // 2][:, (j % 2) * S:(j % 2 + 1) * S],
                                         both(src, lambda x: x[:, e * D + j * P:e * D + (j + 1) * P]),
                                         both((HIDH, HIDL), lambda x: x[:, par, e * S:(e + 1) * S]),
                                         start=(first and e == 0 and j % 2 == 0),
                                         stop=(last and e == 1), skip_group_check=True)
                    mm.then_inc(panel_used, 1)

                gate_up(q0, rounds, 0)
                gate_up(q0 + 2, rounds, 1)
                down(0, q0 + 4, rounds, 0, first=True)
                with pe.Fori(0, 4) as r:
                    for b in range(2):
                        gate_up(q0 + 5 + 3 * b, rounds + r, b)
                        down(r * 2 + 1 + b, q0 + 7 + 3 * b, rounds + r, 1 - b)
                gate_up(q0 + 29, rounds, 0)
                down(9, q0 + 31, rounds, 1)
                down(10, q0 + 32, rounds, 0, last=True)

            def ada_columns(n, done):
                for i in range(n):
                    pe.wait_ge(*done(i))
                    for e in range(2):
                        mm = nc.tensor.matmul(bank[6][:, 2 * i + e:2 * i + e + 1], ADA_SUM[:, i, e * P:(e + 1) * P],
                                              ONES[:, 0:1], start=True, stop=True)
                mm.then_inc(ada_done, 1)

            pe.wait_ge(fills_done, 1)
            ada_columns(ADA_FIRST, lambda i: (ada1_step, KT * (i + 1)))
            norm(0, FILL_B1_NORM1)
            with pe.Fori(0, B1_WIDE // ROUND) as r:
                for s in range(ROUND):
                    wide(r * ROUND + s, Q_WIDE1 + s, r, s % 2)
            for c in range(B1_V):
                src = both(panel(Q_V + c), lambda x: tiles(x, KT))
                pe.wait_ge(wide_free, B1_WIDE + c + 1)
                for t in range(2):
                    for k in range(KT):
                        mm = product(bank[4 + c % 2][:, t * S:(t + 1) * S], both(u_parts(k), lambda x: x[:, t * P:(t + 1) * P]),
                                     both(src, lambda x: x[:, k, :]), start=(k == 0), stop=(k == KT - 1))
                mm.then_inc(panel_used, 1)
            ada_columns(ADA_PANELS - ADA_FIRST, lambda i: (ada2_step, 4 * (i + 1)))

            pe.wait_ge(ropes_loaded, 16)

            def rope(pr):
                pe.wait_ge(rope_in, pr - 3)
                pe.wait_ge(heads_ready, pr - 1)
                nc.tensor.matmul(bank[6 + pr % 2][:, :], rop("swap"), PROJ[:, 2 * pr:2 * pr + 2, :],
                                 start=True, stop=True).then_inc(rope_done, 1)

            for pr in range(10):
                pe.wait_ge(hsq_ready, pr + 1)
                if pr >= 4:
                    pe.wait_ge(hrms_ready, pr - 3)
                nc.tensor.matmul(bank[pr % 4][:, :], rop("head64"), SQ[:, pr % 4 * 512:pr % 4 * 512 + 512],
                                 start=True, stop=True).then_inc(hss_ready, 1)
                if pr >= 6:
                    rope(pr - 2)
            rope(8)
            rope(9)

            def heads(u):
                if u < NA_UNITS:
                    return u % 2, [(QA, KA, u // 2, (u // 2) * HD)]
                j, t = (u - NA_UNITS) // 2, u % 2
                return t, [(QB, KB, g * DIL_SLOTS + j, 512 + (g * DIL_SLOTS + j) * HD) for g in range(DIL_GROUPS)]

            def scores(u):
                t, hs = heads(u)
                if u >= 2:
                    pe.wait_ge(scored, u - 1)
                for g, (q0, k0, h, _) in enumerate(hs):
                    at = h % 2 * HD
                    mm = nc.tensor.matmul(bank[u % 2 * 2 + g // 2][:, g % 2 * S:(g % 2 + 1) * S],
                                          PROJ[at:at + HD, q0 + h // 2, t * P:(t + 1) * P],
                                          PROJ[at:at + HD, k0 + h // 2, :], start=True, stop=True)
                mm.then_inc(scores_done, 1)

            def turn(u):
                pe.wait_ge(probs_ready, u + 1)
                if u >= 1:
                    pe.wait_ge(pt_copied, u)
                for k in range(2 * len(heads(u)[1])):
                    mm = nc.tensor.transpose(bank[4 + k // 4][:, k % 4 * P:(k % 4 + 1) * P],
                                             SC[:, u % 2, k * P:(k + 1) * P], con("ident"))
                mm.then_inc(pt_done, 1)

            def values(u):
                t, hs = heads(u)
                pe.wait_ge(pt_copied, u + 1)
                if u == NA_UNITS:
                    pe.wait_ge(otok_ready, 2)
                at = (u // 2 if u < NA_UNITS else (u - NA_UNITS) // 2) * HD
                for g, (_, _, _, v0) in enumerate(hs):
                    for k in range(2):
                        mm = nc.tensor.matmul(bank[6 + t][:, at:at + HD],
                                              PT[:, u % 2, (2 * g + k) * P:(2 * g + k + 1) * P],
                                              VT[:, k, v0:v0 + HD], start=(g + k == 0),
                                              stop=(g == len(hs) - 1 and k == 1))
                mm.then_inc(pv_done, 1)

            pe.wait_ge(heads_ready, 10)
            scores(0)
            for u in range(UNITS):
                if u + 1 < UNITS:
                    scores(u + 1)
                turn(u)
                if u >= 1:
                    values(u - 1)
            values(UNITS - 1)
            pe.wait_ge(otok_ready, 4)
            for k in range(6):
                for t in range(2):
                    mm = nc.tensor.transpose(bank[k // 2][:, k % 2 * S + t * P:k % 2 * S + (t + 1) * P],
                                             OTOK[:, t, k * P:(k + 1) * P], con("ident"))
            mm.then_inc(ot_done, 1)
            pe.wait_ge(otl_ready, 3)
            for i in range(2):
                src = both(panel(Q_PROJ1 + i), lambda x: tiles(x, 4))
                for c in (2 * i, 2 * i + 1):
                    for e in range(2):
                        for k in range(4):
                            at = c % 2 * S + e * P
                            mm = product(bank[c][:, e * S:(e + 1) * S], both(src, lambda x: x[:, k, at:at + P]),
                                         (OTH[:, k, :], OTL[:, k, :]), start=(k == 0), stop=(k == 3))
                mm.then_inc(panel_used, 1)
            src = both(panel(Q_PROJ1 + 2), lambda x: tiles(x, 2))
            for c in range(4):
                for e in range(2):
                    for k in range(2):
                        at = c * S + e * P
                        mm = product(bank[4 + c][:, e * S:(e + 1) * S], both(src, lambda x: x[:, k, at:at + P]),
                                     (OTH[:, 4 + k, :], OTL[:, 4 + k, :]), start=(k == 0), stop=(k == 1))
                mm.then_inc(proj_done if c < 3 else panel_used, 1)

            def to_residual(q, rounds, fill, v, first):
                pe.wait_ge(ul_ready, 4 * fill + 4)
                for j in range(4):
                    src = both(panel(q + j, rounds), lambda x: tiles(x, KT))
                    if j >= 2:
                        pe.wait_ge(residual_ready, 4 * (v - 1) + j - 1)
                    for e in range(2):
                        for k in range(KT):
                            mm = product(bank[first + j % 2][:, e * S:(e + 1) * S],
                                         both(src, lambda x: x[:, k, e * P:(e + 1) * P]), u_parts(k),
                                         start=(k == 0), stop=(k == KT - 1))
                    mm.then_inc(panel_used, 1)

            to_residual(Q_WO, 0, FILL_B1_MERGE, 1, 0)
            norm(1, FILL_B1_NORM2)
            ffn(0, Q_FFN0, 0)

            with pe.Fori(0, LAYERS) as l:
                rounds = l * L_ROUNDS
                fill = FILL_LAYER + 4 * l
                w0 = WIDE0 + L_WIDE * l
                norm(2 + 3 * l, fill)
                ffn(1 + 2 * l, Q_LAYERS + LQ_FFN1, rounds)
                norm(3 + 3 * l, fill + 1)
                pe.wait_ge(pack2_loaded, 16 * l + 16)
                for t in range(2):
                    for k in range(KT):
                        mm = nc.tensor.matmul(bank[6][:, t * SMALL:(t + 1) * SMALL], U[:, k, t * P:(t + 1) * P],
                                              pk2("small_w", k * SMALL, SMALL), start=(k == 0), stop=(k == KT - 1))
                mm.then_inc(small_done, 1)
                with pe.Fori(0, L_CONV // ROUND) as r:
                    for s in range(ROUND):
                        wide(w0 + r * ROUND + s, Q_LAYERS + LQ_WIDE + s, rounds + r, s % 2)
                pe.wait_ge(loga_ready, l + 1)
                for t in range(2):
                    a, g = LOGA[:, t, 0:SSM_HEADS], LOGA[:, t, SSM_HEADS:SP_COLS]
                    nc.tensor.matmul(bank[6][:, 32 * t:32 * t + 32], con("cum128"), a, start=True, stop=True)
                    nc.tensor.matmul(bank[6][:, 64 + 8 * t:72 + 8 * t], con("cum64"), g, start=True, stop=True)
                    nc.tensor.matmul(bank[6][:, 80 + 8 * t:88 + 8 * t], con("same64"), g, start=True, stop=True)
                    for c in range(2):
                        at = 128 + 8 * (2 * t + c)
                        nc.tensor.matmul(bank[6][:, at:at + 8], con(f"half{c}"), g, start=True, stop=True)
                nc.tensor.matmul(bank[6][:, 96:128], ONES[:, :], LOGA[:, 0, 0:SSM_HEADS], start=True,
                                 stop=True).then_inc(cum_done, 1)
                pe.wait_ge(conv_ready, 2 + 24 * l + 24)
                for t in range(2):
                    for q in range(4):
                        i = 4 * t + q
                        if i >= 4:
                            pe.wait_ge(xdt_ready, 8 * l + i - 3)
                        for e in range(4):
                            mm = nc.tensor.transpose(bank[q][:, e * P:(e + 1) * P],
                                                     CONV[:, 4 * q + e, t * P:(t + 1) * P], con("ident"))
                        mm.then_inc(xtok_done, 1)
                for g in range(GROUPS):
                    mm = nc.tensor.transpose(bank[7][:, g * P:(g + 1) * P], CONV[:, B_TILE + g, 0:P], con("ident"))
                mm.then_inc(btok_done, 1)
                pe.wait_ge(btok_copied, l + 1)
                for g in range(GROUPS):
                    pe.wait_ge(xend_ready, 4 * l + g + 1)
                    nc.tensor.matmul(bank[g][:, :], BTOK[:, g * P:(g + 1) * P], XEND[:, g * 512:(g + 1) * 512],
                                     start=True, stop=True).then_inc(state_done, 1)
                pe.wait_ge(cum_copied, l + 1)
                for t in range(2):
                    for g in range(GROUPS):
                        mm = nc.tensor.matmul(bank[6 + t][:, g * P:(g + 1) * P], CONV[:, B_TILE + g, t * P:(t + 1) * P],
                                              CONV[:, C_TILE + g, t * P:(t + 1) * P], start=True, stop=True)
                    mm.then_inc(cb_done, 1)
                pe.wait_ge(state_copied, 4 * l + 4)

                def decay_rows(i):
                    t, h0 = i // 8, i % 8 * 4
                    if i >= 2:
                        pe.wait_ge(seg_taken, 16 * l + i - 1)
                    if i >= 10:
                        pe.wait_ge(row_exp_ready, 8 * l + i - 9)
                    for e in range(4):
                        mm = nc.tensor.matmul(bank[i % 2][:, e * P:(e + 1) * P],
                                              LOGA[:, t, h0 + e:h0 + e + 1].to_broadcast([P, P]), con("cum128"),
                                              start=True, stop=True)
                    mm.then_inc(seg_done, 1)

                def scan_out(i):
                    t, h0, m = i // 8, i % 8 * 4, i // 2
                    pe.wait_ge(mix_ready, 16 * l + i + 1)
                    if t == 1:
                        pe.wait_ge(cdec_ready, 8 * l + i - 7)
                    if i % 2 == 0 and m >= 2:
                        pe.wait_ge(y_taken, 8 * l + m - 1)
                    for e in range(4):
                        h = h0 + e
                        dst = bank[2 + m % 2][h % 2 * HD:h % 2 * HD + HD, h % 8 // 2 * P:(h % 8 // 2 + 1) * P]
                        mm = nc.tensor.matmul(dst, XDT[:, t, h * HD:(h + 1) * HD], MIX[:, i % 2, e * P:(e + 1) * P],
                                              start=True, stop=(t == 0))
                        if t == 1:
                            mm = nc.tensor.matmul(dst, STATE[:, h * HD:(h + 1) * HD], CDEC[:, i % 2, e * P:(e + 1) * P],
                                                  start=False, stop=True)
                    mm.then_inc(y_done, 1)

                decay_rows(0)
                for i in range(16):
                    if i + 1 < 16:
                        decay_rows(i + 1)
                    scan_out(i)
                pe.wait_ge(y_taken, 8 * l + 8)
                for j in range(L_ZS + L_ZD):
                    wide(w0 + L_CONV + j, Q_LAYERS + LQ_WIDE + L_CONV + j, rounds, j % 2)
                    if j % 2 == 0 or j < 3 or (j - 3) // 2 >= GROUPS:
                        continue
                    g = (j - 3) // 2
                    pe.wait_ge(ysq_ready, 4 * l + g + 1)
                    for e in range(4):
                        at = g % 2 * 1024 + e * S
                        mm = nc.tensor.matmul(bank[g][:, 0:S], MEAN_G[:, :], SQ[:, at:at + S], start=(e == 0),
                                              stop=(e == 3))
                    mm.then_inc(yss_done, 1)

                pe.wait_ge(yrms_ready, 4 * l + 4)
                for pr in range(8):
                    pe.wait_ge(qksq_ready, 8 * l + pr + 1)
                    if pr >= 4:
                        pe.wait_ge(qkrms_ready, 8 * l + pr - 3)
                    nc.tensor.matmul(bank[pr % 4][:, :], ONES[:, :], SQ[:, pr % 4 * 512:pr % 4 * 512 + 512],
                                     start=True, stop=True).then_inc(qkss_done, 1)
                pe.wait_ge(qk_ready, 8 * l + 8)
                for t in range(2):
                    tok = slice(t * P, (t + 1) * P)
                    if t == 1:
                        pe.wait_ge(st_ready, 6 * l + 4)
                        pe.wait_ge(o_copied, 4 * l + 2)
                    for m in range(4):
                        for e in range(4):
                            mm = nc.tensor.transpose(bank[m][:, e * P:(e + 1) * P], QKV[:, 8 + 4 * m + e, tok],
                                                     con("ident"))
                        mm.then_inc(kv_done, 1)
                    for b in range(2):
                        n = 4 * l + 2 * t + b
                        if 2 * t + b >= 1:
                            pe.wait_ge(mt_ready, n)
                            pe.wait_ge(aqk_ready, n)
                            pe.wait_ge(grow_ready, n)
                        for e in range(4):
                            h, at = 4 * b + e, slice(e * P, (e + 1) * P)
                            q, k = QKV[:, h, tok], QKV[:, DN_HEADS + h, tok]
                            nc.tensor.matmul(bank[6][:, at], LOGA[:, t, 32 + h:33 + h].to_broadcast([P, P]),
                                             con("cum64"), start=True, stop=True)
                            nc.tensor.matmul(bank[7][:, at], BETA[:, t, h:h + 1].to_broadcast([P, P]), con("ident"),
                                             start=True, stop=True)
                            nc.tensor.matmul(bank[4][:, at], k, k, start=True, stop=True)
                            mm = nc.tensor.matmul(bank[5][:, at], k, q, start=True, stop=True)
                        mm.then_inc(kk_done, 1)
                    for v in range(LEVELS):
                        k = (2 * l + t) * LEVELS + v
                        kc = (2 * l + t) * (LEVELS - 1) + v - 1
                        for b in range(2):
                            pe.wait_ge(cs_ready, 2 * k + b + 1)
                            if v >= 1:
                                pe.wait_ge(inv_ready, 2 * k + b - 1)
                            for e in range(4):
                                at = slice(512 * b + e * P, 512 * b + (e + 1) * P)
                                mm = nc.tensor.matmul(bank[b][:, e * P:(e + 1) * P], CS[:, at],
                                                      TI[:, at] if v else con("ident"), start=True, stop=True)
                            mm.then_inc(inv_u_done, 1)
                        for b in range(2 if v else 0):
                            pe.wait_ge(inv_u_copied, 2 * kc + b + 1)
                            for e in range(4):
                                at, to = slice(512 * b + e * P, 512 * b + (e + 1) * P), slice(e * P, (e + 1) * P)
                                if v < LEVELS - 1:
                                    nc.tensor.matmul(bank[2 + b][:, to], TT[:, at], UB[:, at], start=True, stop=True)
                                mm = nc.tensor.matmul(bank[6 + b][:, to], UB[:, at], TT[:, at], start=True, stop=True)
                            mm.then_inc(inv_v_done, 1)
                    for b in range(2):
                        pe.wait_ge(inv_ready, 2 * ((2 * l + t) * LEVELS + LEVELS - 1) + b + 1)
                        for e in range(4):
                            at = slice(512 * b + e * P, 512 * b + (e + 1) * P)
                            mm = nc.tensor.matmul(bank[b][:, e * P:(e + 1) * P], KBG[:, at], TT[:, at],
                                                  start=True, stop=True)
                        mm.then_inc(wt_done, 1)
                    pe.wait_ge(wt_copied, 4 * l + 2 * t + 2)
                    for c in range(2):
                        cg, r = 2 * t + c, c * 64
                        rows = slice(r, r + 64)
                        if cg >= 1:
                            pe.wait_ge(st_ready, 6 * l + 2 * cg)
                        for b in range(2):
                            for e in range(4):
                                h = 4 * b + e
                                to = bank[2 + b][rows, e * P:(e + 1) * P]
                                at = slice(h * P, (h + 1) * P)
                                mm = nc.tensor.matmul(to, TT[:, h * P + r:h * P + r + 64], VB[:, at], start=True,
                                                      stop=(cg == 0))
                                if cg >= 1:
                                    mm = nc.tensor.matmul(to, WT[:, h * P + r:h * P + r + 64], ST[:, at], start=False,
                                                          stop=True)
                            mm.then_inc(vn_done, 1)
                        pe.wait_ge(vn_copied, 8 * l + 2 * cg + 2)
                        if cg >= 1:
                            pe.wait_ge(o_copied, 4 * l + cg)
                        for h in range(DN_HEADS):
                            to = bank[6][:, h * 64:(h + 1) * 64]
                            if cg >= 1:
                                nc.tensor.matmul(to, ST[:, h * P:(h + 1) * P], QKV[:, h, t * P + r:t * P + r + 64],
                                                 start=True, stop=False)
                            mm = nc.tensor.matmul(to, VN[rows, h * P:(h + 1) * P],
                                                  AQK[rows, h * P + r:h * P + r + 64], start=(cg == 0), stop=True)
                        mm.then_inc(o_done, 1)
                        for b in range(2 if cg < 3 else 0):
                            for e in range(4):
                                at = slice(512 * b + e * P, 512 * b + (e + 1) * P)
                                mm = nc.tensor.matmul(bank[b][:, e * P:(e + 1) * P], KDEC[rows, at], VN[rows, at],
                                                      start=True, stop=True)
                            mm.then_inc(st_done, 1)
                for pr in range(4):
                    pe.wait_ge(osq_ready, 4 * l + pr + 1)
                    nc.tensor.matmul(bank[pr][:, :], MEAN_V[:, :], SQ[:, pr * 512:pr * 512 + 512], start=True,
                                     stop=True).then_inc(oss_done, 1)
                for j in range(L_GATES):
                    jj = L_CONV + L_ZS + L_ZD + j
                    wide(w0 + jj, Q_LAYERS + LQ_WIDE + jj, rounds, j % 2)
                pe.wait_ge(branch_lo, 12 * l + 12)
                for c in range(4):
                    if c >= 2:
                        pe.wait_ge(merged_ready, 4 + 4 * l + c - 1)
                    for half in range(2):
                        src = both(panel(Q_LAYERS + LQ_PROJ + 3 * c + half, rounds), lambda x: tiles(x, KT))
                        for e in range(2):
                            for k in range(KT):
                                mm = product(bank[c % 2 * 2][:, e * S:(e + 1) * S],
                                             both(src, lambda x: x[:, k, e * P:(e + 1) * P]),
                                             both((YSH, YSL), lambda x: x[:, half * KT + k, :]),
                                             start=(half + e + k == 0), stop=(half == 1 and k == KT - 1),
                                             skip_group_check=True)
                        mm.then_inc(panel_used, 1)
                    src = both(panel(Q_LAYERS + LQ_PROJ + 3 * c + 2, rounds), lambda x: tiles(x, KT))
                    for e in range(2):
                        for k in range(KT):
                            mm = product(bank[c % 2 * 2 + 1][:, e * S:(e + 1) * S],
                                         both(src, lambda x: x[:, k, e * P:(e + 1) * P]),
                                         (YDH[:, k, :], YDL[:, k, :]), start=(k == 0), stop=(k == KT - 1))
                    mm.then_inc(panel_used, 1)
                to_residual(Q_LAYERS + LQ_WOUT, rounds, fill + 2, 4 + 3 * l, 6)
                norm(4 + 3 * l, fill + 3)
                ffn(2 + 2 * l, Q_LAYERS + LQ_FFN2, rounds)
            norm(2 + 3 * LAYERS, None)

        @block.scalar
        def _(act):
            act.dma_start(PK1[:, :], pack1).then_inc(pack1_loaded, 16)
            act.dma_start(H[:, :, :], x_t).then_inc(x_loaded, 16)
            act.sem_inc(wide_free, 2)
            act.sem_inc(conv_ready, 2)
            act.wait_ge(pack1_loaded, 16)
            nc.scalar.activation(CACT[:, :], pk1("c", 0, 8), ACT.Silu).then_inc(c_ready, 1)

            def split(q, rounds=0):
                act.wait_ge(panel_loaded[q % RING], 16 * (q // RING + 1) + 16 * (ROUND // RING) * rounds)
                if q >= PARTS:
                    act.wait_ge(panel_used, q - PARTS + 1 + ROUND * rounds)
                nc.scalar.activation(HI[:, q % PARTS, :], ring[:, q % RING, :], ACT.Copy).then_inc(hi_ready, 1)

            def fill_high(f, counter, before):
                for k in range(KT // 2):
                    act.wait_ge(counter, before(k))
                    nc.scalar.activation(UH[:, 2 * k:2 * k + 2, :], U[:, 2 * k:2 * k + 2, :],
                                         ACT.Copy).then_inc(uh_ready, 1)

            def norm(n, fill, loaded=False):
                for k in range(KT // 2):
                    if loaded:
                        act.wait_ge(x_loaded, 16)
                    else:
                        act.wait_ge(residual_ready, KT // 2 * (n - 1) + k + 1)
                    nc.scalar.activation(tiles(SQ[:, k * 512:(k + 1) * 512], 2), H[:, 2 * k:2 * k + 2, :],
                                         ACT.Square).then_inc(squares_ready, 1)
                act.wait_ge(sumsq_ready, n + 1)
                nc.scalar.activation(RMS[:, 0:S], bank[4][:, 0:S], ACT.Sqrt, bias=EPST[:, :]).then_inc(rms_ready, 1)
                if fill is not None:
                    fill_high(fill, u_ready, lambda k: KT * n + 2 * k + 2)

            def ffn(q0, rounds):
                def silu(q, rr, par):
                    act.wait_ge(panel_used, q + 1 + ROUND * rr)
                    nc.scalar.activation(SG[:, par, :], bank[4 + 2 * par][:, :], ACT.Silu).then_inc(gate_act_ready, 1)

                split(q0 + 2, rounds)
                split(q0 + 3, rounds)
                silu(q0 + 1, rounds, 0)
                split(q0 + 4, rounds)
                split(q0 + 5, rounds)
                silu(q0 + 3, rounds, 1)
                split(q0 + 6, rounds)
                with act.Fori(0, 4) as r:
                    for b in range(2):
                        split(q0 + 7 + 3 * b, rounds + r)
                        split(q0 + 8 + 3 * b, rounds + r)
                        silu(q0 + 6 + 3 * b, rounds + r, b)
                        split(q0 + 9 + 3 * b, rounds + r)
                split(q0 + 31, rounds)
                split(q0 + 32, rounds)
                silu(q0 + 30, rounds, 0)

            split(0)
            split(1)
            act.wait_ge(fills_done, 1)
            norm(0, FILL_B1_NORM1, loaded=True)
            proj2 = ARENA[:, 0:36 * S].rearrange("p (w n) -> p w n", w=B1_WIDE)
            with act.Fori(0, B1_WIDE // ROUND) as r:
                for i in range(ROUND):
                    split(Q_WIDE1 + i + PARTS, r)
                    act.wait_ge(panel_used, Q_WIDE1 + ROUND * r + i + 1)
                    nc.scalar.activation(proj2[:, ROUND * r + i, :], bank[4 + i % 2][:, :], ACT.Copy).then_inc(wide_free, 1)
            for c in range(B1_V):
                split(Q_V + c + PARTS)
                act.wait_ge(panel_used, Q_V + c + 1)
                nc.scalar.activation(VT[:, :, c * S:(c + 1) * S], tiles(bank[4 + c % 2][:, :], 2),
                                     ACT.Copy).then_inc(wide_free, 1)
            act.wait_ge(wide_free, 2 + WIDE0)
            for i in range(16):
                nc.scalar.activation(PROJ[:, GATE + i, :], PROJ[:, GATE + i, :], ACT.Sigmoid,
                                     bias=pk1("b_gate", i)).then_inc(gates_ready, 1)

            def head_rms(pr):
                act.wait_ge(hss_ready, pr + 1)
                if pr == 0:
                    act.wait_ge(ada_done, 2)
                if pr >= 8:
                    act.wait_ge(heads_ready, pr - 7)
                nc.scalar.activation(RSH[:, pr % 8, :], bank[pr % 4][:, :], ACT.Sqrt, bias=EPST[:, :]).then_inc(hrms_ready, 1)

            for pr in range(10):
                nc.scalar.activation(tiles(SQ[:, pr % 4 * 512:pr % 4 * 512 + 512], 2), PROJ[:, 2 * pr:2 * pr + 2, :],
                                     ACT.Square).then_inc(hsq_ready, 1)
                if pr >= 1:
                    head_rms(pr - 1)
            head_rms(9)

            def keys(u):
                return S if u < NA_UNITS else DIL_GROUPS * S

            def softmax_exp(u):
                act.wait_ge(nmax_ready, u + 1)
                nc.scalar.activation(SC[:, u % 2, 0:keys(u)], SC[:, u % 2, 0:keys(u)], ACT.Exp,
                                     bias=NMAX[:, UNITS + u:UNITS + u + 1],
                                     accum_out=DEN[:, u:u + 1]).then_inc(probs_ready, 1)

            def turned(u):
                act.wait_ge(pt_done, u + 1)
                if u >= 2:
                    act.wait_ge(pv_done, u - 1)
                nc.scalar.activation(PT[:, u % 2, 0:min(512, keys(u))], bank[4][:, 0:min(512, keys(u))], ACT.Copy)\
                    .then_inc(pt_copied if keys(u) <= 512 else pt_half, 1)
                if keys(u) > 512:
                    nc.scalar.activation(PT[:, u % 2, 512:keys(u)], bank[5][:, 0:keys(u) - 512],
                                         ACT.Copy).then_inc(pt_copied, 1)

            softmax_exp(0)
            for u in range(UNITS):
                if u + 1 < UNITS:
                    softmax_exp(u + 1)
                turned(u)
            act.wait_ge(ot_done, 1)
            for i in range(3):
                nc.scalar.activation(OTH[:, 2 * i:2 * i + 2, :], tiles(bank[i][:, :], 2), ACT.Copy).then_inc(oth_ready, 1)
            for i in range(B1_PROJ):
                split(Q_PROJ1 + i + PARTS)
            fill_high(FILL_B1_MERGE, merged_ready, lambda k: k + 1)
            for i in range(B1_WO):
                split(Q_WO + i + PARTS)
            norm(1, FILL_B1_NORM2)
            ffn(Q_FFN0, 0)

            conv2 = ARENA[:, 0:CONV_TILES * S].rearrange("p (w n) -> p w n", w=L_CONV)
            with act.Fori(0, LAYERS) as l:
                used0 = Q_LAYERS + L_PANELS * l
                rounds = L_ROUNDS * l
                fill = FILL_LAYER + 4 * l

                def ahead(q):
                    split(Q_LAYERS + q + PARTS, rounds)

                split(Q_LAYERS, rounds)
                split(Q_LAYERS + 1, rounds)
                norm(2 + 3 * l, fill)
                ffn(Q_LAYERS + LQ_FFN1, rounds)
                ahead(LQ_WIDE - 2)
                ahead(LQ_WIDE - 1)
                norm(3 + 3 * l, fill + 1)
                act.wait_ge(small_abs, l + 1)
                nc.scalar.activation(SMX[:, 2, :], SMX[:, 1, :], ACT.Exp).then_inc(small_exp, 1)
                nc.scalar.activation(SMX[:, 7, 0:SP_COLS], pk2("a_log", 0, SP_COLS), ACT.Exp).then_inc(aneg_ready, 1)
                act.wait_ge(small_w, l + 1)
                nc.scalar.activation(SMX[:, 4, :], SMX[:, 3, :], ACT.Ln).then_inc(small_ln, 1)
                nc.scalar.activation(BETA[:, :, :], tiles(SMX[:, 0, :], 2)[:, :, SP_COLS:SMALL],
                                     ACT.Sigmoid).then_inc(beta_ready, 1)
                def conv_silu(j, b):
                    act.wait_ge(conv_step, 192 * l + 8 * j + 24)
                    nc.scalar.activation(tiles(conv2[:, j, :], 2), CACC[:, b, :, :], ACT.Silu).then_inc(conv_ready, 1)

                def conv_in(j, b):
                    act.wait_ge(panel_used, used0 + LQ_WIDE + j + 1)
                    act.wait_ge(conv_step, 192 * l + 8 * j + 8)
                    nc.scalar.activation(XPAD[:, b, :, 3:S + 3], tiles(bank[4 + b][:, :], 2),
                                         ACT.Copy).then_inc(wide_free, 1)

                for i in range(ROUND):
                    ahead(LQ_WIDE + i)
                    conv_in(i, i % 2)
                    if i >= 1:
                        conv_silu(i - 1, (i - 1) % 2)
                with act.Fori(1, L_CONV // ROUND) as r:
                    for i in range(ROUND):
                        split(Q_LAYERS + LQ_WIDE + i + PARTS, rounds + r)
                        conv_in(ROUND * r + i, i % 2)
                        conv_silu(ROUND * r + i - 1, (i - 1) % 2)
                conv_silu(L_CONV - 1, 1)
                act.wait_ge(cum_copied, l + 1)
                nc.scalar.activation(ECUM[:, 0:96], ECUM[:, 0:96], ACT.Exp).then_inc(ecum_ready, 1)
                act.wait_ge(btok_done, l + 1)
                nc.scalar.activation(BTOK[:, :], bank[7][:, :], ACT.Copy).then_inc(btok_copied, 1)
                for g in range(GROUPS):
                    act.wait_ge(state_done, 4 * l + g + 1)
                    nc.scalar.activation(STATE[:, g * 512:(g + 1) * 512], bank[g][:, :], ACT.Copy).then_inc(state_copied, 1)
                for i in range(16):
                    if i >= 8:
                        act.wait_ge(seg_taken, 16 * l + i + 1)
                        if i >= 10:
                            act.wait_ge(y_done, 16 * l + i - 1)
                        nc.scalar.activation(CDEC[:, i % 2, :], bank[i % 2][:, :], ACT.Exp).then_inc(row_exp_ready, 1)
                    act.wait_ge(seg_ready, 16 * l + i + 1)
                    nc.scalar.activation(SEG[:, i % 2, :], SEG[:, i % 2, :], ACT.Exp).then_inc(decay_ready, 1)

                def group_rms(g):
                    act.wait_ge(yss_done, 4 * l + g + 1)
                    if g >= 2:
                        act.wait_ge(ys_ready, 4 * l + g - 1)
                    nc.scalar.activation(RMS[:, g % 2 * S:g % 2 * S + S], bank[g][:, 0:S], ACT.Sqrt,
                                         bias=EPST[:, :]).then_inc(yrms_ready, 1)

                def group_squares(g):
                    act.wait_ge(yg_ready, 8 * l + 2 * g + 2)
                    if g >= 2:
                        act.wait_ge(yss_done, 4 * l + g - 1)
                    nc.scalar.activation(tiles(SQ[:, g % 2 * 1024:g % 2 * 1024 + 1024], 4),
                                         CONV[:, 4 * g:4 * g + 4, :], ACT.Square).then_inc(ysq_ready, 1)

                for j in range(L_ZS + L_ZD):
                    ahead(LQ_WIDE + L_CONV + j)
                    act.wait_ge(panel_used, used0 + LQ_WIDE + L_CONV + j + 1)
                    src = tiles(bank[4 + j % 2][:, :], 2)
                    if j < L_ZS:
                        if j == 0:
                            act.wait_ge(y_taken, 8 * l + 8)
                        if j >= 2:
                            act.wait_ge(yg_ready, 8 * l + j - 1)
                        nc.scalar.activation(tiles(ZT[:, j % 2, :], 2), src, ACT.Silu).then_inc(wide_free, 1)
                    else:
                        z0 = 2 * (j - L_ZS)
                        nc.scalar.activation(ZD[:, z0:z0 + 2, :], src, ACT.Silu).then_inc(wide_free, 1)
                    if j % 2 == 0 and 2 <= j <= 2 * GROUPS:
                        group_squares(j // 2 - 1)
                    if j % 2 == 0 and 4 <= j < 4 + 2 * GROUPS:
                        group_rms(j // 2 - 2)
                def qk_rms(pr):
                    act.wait_ge(qkss_done, 8 * l + pr + 1)
                    if pr >= 4:
                        act.wait_ge(qk_ready, 8 * l + pr - 3)
                    nc.scalar.activation(ROOT(pr), bank[pr % 4][:, :], ACT.Sqrt, bias=EPST[:, :]).then_inc(qkrms_ready, 1)

                for pr in range(8):
                    if pr >= 4:
                        act.wait_ge(qkss_done, 8 * l + pr - 3)
                    nc.scalar.activation(tiles(SQ[:, pr % 4 * 512:pr % 4 * 512 + 512], 2),
                                         QKV[:, 2 * pr:2 * pr + 2, :], ACT.Square).then_inc(qksq_ready, 1)
                    if pr >= 1:
                        qk_rms(pr - 1)
                qk_rms(7)
                for t in range(2):
                    for b in range(2):
                        n = 4 * l + 2 * t + b
                        act.wait_ge(gseg_taken, n + 1)
                        if 2 * t + b >= 1:
                            act.wait_ge(qd_ready, n)
                        nc.scalar.activation(RSTD[:, :], bank[6][:, :], ACT.Exp).then_inc(grow_ready, 1)
                        act.wait_ge(gseg_ready, n + 1)
                        nc.scalar.activation(DEC[:, 512 * b:512 * b + 512], DCY[:, 512 * b:512 * b + 512],
                                             ACT.Exp).then_inc(gdec_ready, 1)
                    for v in range(1, LEVELS):
                        k = (2 * l + t) * LEVELS + v
                        for b in range(2):
                            act.wait_ge(inv_u_done, 2 * k + b + 1)
                            nc.scalar.activation(UB[:, 512 * b:512 * b + 512], bank[b][:, :],
                                                 ACT.Copy).then_inc(inv_u_copied, 1)
                    for b in range(2):
                        act.wait_ge(wt_done, 4 * l + 2 * t + b + 1)
                        nc.scalar.activation(WT[:, 512 * b:512 * b + 512], bank[b][:, :], ACT.Copy,
                                             scale=-1.0).then_inc(wt_copied, 1)
                    for c in range(2):
                        cg, rows = 2 * t + c, slice(64 * c, 64 * c + 64)
                        for b in range(2):
                            act.wait_ge(vn_done, 8 * l + 2 * cg + b + 1)
                            nc.scalar.activation(VN[rows, 512 * b:512 * b + 512], bank[2 + b][rows, :],
                                                 ACT.Copy).then_inc(vn_copied, 1)
                act.wait_ge(o_copied, 4 * l + 4)
                for pr in range(4):
                    nc.scalar.activation(tiles(SQ[:, pr * 512:pr * 512 + 512], 2), QKV[:, 2 * pr:2 * pr + 2, :],
                                         ACT.Square).then_inc(osq_ready, 1)
                for pr in range(4):
                    act.wait_ge(oss_done, 4 * l + pr + 1)
                    nc.scalar.activation(ROOT(pr), bank[pr][:, :], ACT.Sqrt, bias=EPST[:, :]).then_inc(orms_ready, 1)
                for j in range(L_GATES):
                    q = LQ_WIDE + L_CONV + L_ZS + L_ZD + j
                    ahead(q)
                    act.wait_ge(panel_used, used0 + q + 1)
                    nc.scalar.activation(GT[:, 2 * j:2 * j + 2, :], tiles(bank[4 + j % 2][:, :], 2),
                                         ACT.Sigmoid).then_inc(wide_free, 1)
                    nc.scalar.activation(YSH[:, 2 * j:2 * j + 2, :], CONV[:, 2 * j:2 * j + 2, :],
                                         ACT.Copy).then_inc(branch_hi, 1)
                    if j >= 4:
                        act.wait_ge(yd_ready, 4 * l + j - 3)
                        nc.scalar.activation(YDH[:, 2 * j - 8:2 * j - 6, :], QKV[:, 2 * j - 8:2 * j - 6, :],
                                             ACT.Copy).then_inc(branch_hi, 1)
                def merged_high(c):
                    act.wait_ge(merged_ready, 4 + 4 * l + c + 1)
                    nc.scalar.activation(UH[:, 2 * c:2 * c + 2, :], U[:, 2 * c:2 * c + 2, :],
                                         ACT.Copy).then_inc(uh_ready, 1)

                for j in range(L_PROJ):
                    ahead(LQ_PROJ + j)
                    if j % 3 == 2 and j >= 5:
                        merged_high((j - 5) // 3)
                merged_high(3)
                for j in range(L_WOUT):
                    ahead(LQ_WOUT + j)
                norm(4 + 3 * l, fill + 3)
                ffn(Q_LAYERS + LQ_FFN2, rounds)
            norm(2 + 3 * LAYERS, None)

        @block.vector
        def _(dve):
            base, count = [0], [0]

            def step(ins):
                ins.then_inc(dve_done, 1)
                count[0] += 1
                return count[0]

            def need(number):
                dve.wait_ge(dve_done, base[0] + number)

            def pad(total):
                assert count[0] <= total, count
                need(count[0])
                dve.sem_inc(dve_done, total - count[0])
                count[0] = 0

            nc.vector.memset(MEAN_D[:, :], 1.0 / D)
            nc.vector.memset(MEAN_G[:, :], 1.0 / 512)
            nc.vector.memset(MEAN_V[:, :], 1.0 / P)
            nc.vector.memset(ONES[:, :], 1.0)
            nc.vector.memset(XPAD[:, :, :, :], 0.0)
            nc.vector.memset(EPST[:, :], EPS).then_inc(fills_done, 1)
            dve.sem_inc(conv_step, 16)

            def split(q, rounds=0):
                dve.wait_ge(hi_ready, q + 1 + ROUND * rounds)
                nc.vector.tensor_tensor(LO[:, q % PARTS, :], ring[:, q % RING, :], HI[:, q % PARTS, :].bitcast(F32),
                                        ALU.subtract).then_inc(lo_ready, 1)

            def fill_low(f, k):
                dve.wait_ge(uh_ready, 4 * f + k + 1)
                at = slice(2 * k, 2 * k + 2)
                nc.vector.tensor_tensor(UL[:, at, :], U[:, at, :], UH[:, at, :].bitcast(F32),
                                        ALU.subtract).then_inc(ul_ready, 1)

            def norm(n, fill, gain, shift=None):
                dve.wait_ge(rms_ready, n + 1)
                need(step(nc.vector.reciprocal(RSTD[:, 0:S], RMS[:, 0:S])))
                for k in range(KT):
                    ins = nc.vector.scalar_tensor_tensor(U[:, k, :], H[:, k, :], gain[:, k:k + 1], RSTD[:, 0:S],
                                                         ALU.mult, ALU.mult)
                    if shift is None:
                        ins.then_inc(u_ready, 1)
                    else:
                        need(step(ins))
                        nc.vector.tensor_scalar(U[:, k, :], U[:, k, :], shift[:, k:k + 1], None,
                                                ALU.add).then_inc(u_ready, 1)
                for k in range(KT // 2 if fill is not None else 0):
                    fill_low(fill, k)

            def ffn_hidden(f, q0, rounds):
                def hidden(i, par):
                    dve.wait_ge(gate_act_ready, f * HID_PAIRS + i + 1)
                    n = f * HID_PAIRS + i + 1
                    nc.vector.tensor_tensor(HID[:, par, :], SG[:, par, :], bank[5 + 2 * par][:, :],
                                            ALU.mult).then_inc(hid_product, 1)
                    dve.wait_ge(hid_product, n)
                    nc.vector.tensor_copy(HIDH[:, par, :], HID[:, par, :]).then_inc(hidh_ready, 1)
                    dve.wait_ge(hidh_ready, n)
                    nc.vector.tensor_tensor(HIDL[:, par, :], HID[:, par, :], HIDH[:, par, :].bitcast(F32),
                                            ALU.subtract).then_inc(hidden_ready, 1)

                split(q0 + 2, rounds)
                split(q0 + 3, rounds)
                hidden(0, 0)
                split(q0 + 4, rounds)
                split(q0 + 5, rounds)
                hidden(1, 1)
                split(q0 + 6, rounds)
                with dve.Fori(0, 4) as r:
                    for b in range(2):
                        split(q0 + 7 + 3 * b, rounds + r)
                        split(q0 + 8 + 3 * b, rounds + r)
                        hidden(2 + 2 * r + b, b)
                        split(q0 + 9 + 3 * b, rounds + r)
                split(q0 + 31, rounds)
                split(q0 + 32, rounds)
                hidden(10, 0)

            def residual(j, src, scale):
                if isinstance(scale, float):
                    nc.vector.scalar_tensor_tensor(H[:, 2 * j:2 * j + 2, :], tiles(src, 2), scale, H[:, 2 * j:2 * j + 2, :],
                                                   ALU.mult, ALU.add).then_inc(residual_ready, 1)
                    return
                for e in range(2):
                    ins = nc.vector.scalar_tensor_tensor(H[:, 2 * j + e, :], src[:, e * S:(e + 1) * S],
                                                         scale[:, 2 * j + e:2 * j + e + 1], H[:, 2 * j + e, :],
                                                         ALU.mult, ALU.add)
                ins.then_inc(residual_ready, 1)

            dve.wait_ge(pack1_loaded, 16)
            dve.wait_ge(c_ready, 1)
            for i in range(ADA_FIRST):
                dve.wait_ge(ada1_loaded[i], 16)
                src = tiles(ADA1[:, i, :], KT)
                for k in range(KT):
                    out, c = ADA_SUM[:, i, :], CACT[:, k:k + 1]
                    if k == 0:
                        ins = nc.vector.tensor_scalar(out, src[:, k, :], c, None, ALU.mult)
                    else:
                        dve.wait_ge(ada1_step, KT * i + k)
                        ins = nc.vector.scalar_tensor_tensor(out, src[:, k, :], c, out, ALU.mult, ALU.add)
                    ins.then_inc(ada1_step, 1)
            shift1, scale1, gate1, shift2, scale2, gate2 = [MOD[:, 8 * i:8 * i + 8] for i in range(6)]
            dve.wait_ge(ada_done, 1)
            nc.vector.tensor_tensor(MOD[:, 0:2 * ADA_FIRST], bank[6][:, 0:2 * ADA_FIRST], pk1("b_ada", 0, 2 * ADA_FIRST),
                                    ALU.add).then_inc(ada_copied, 1)
            dve.wait_ge(ada_copied, 1)
            step(nc.vector.scalar_tensor_tensor(GS[:, 0:8], scale1, 1.0, pk1("g1", 0, 8), ALU.add, ALU.mult))
            step(nc.vector.tensor_scalar(GS[:, 16:17], pk1("g_qa"), HD ** -0.5, None, ALU.mult))
            need(step(nc.vector.tensor_scalar(GS[:, 17:18], pk1("g_qb"), HD ** -0.5, None, ALU.mult)))
            split(0)
            split(1)
            norm(0, FILL_B1_NORM1, GS[:, 0:8], shift1)
            with dve.Fori(0, B1_WIDE // ROUND) as r:
                for i in range(ROUND):
                    split(Q_WIDE1 + i + PARTS, r)
            for c in range(B1_V):
                split(Q_V + c + PARTS)
            rest = slice(2 * ADA_FIRST, 2 * ADA_PANELS)
            dve.wait_ge(ada_done, 2)
            nc.vector.tensor_tensor(MOD[:, rest], bank[6][:, 0:2 * (ADA_PANELS - ADA_FIRST)],
                                    pk1("b_ada", 2 * ADA_FIRST, 2 * (ADA_PANELS - ADA_FIRST)), ALU.add).then_inc(ada_copied, 1)
            dve.wait_ge(ada_copied, 2)
            step(nc.vector.scalar_tensor_tensor(GS[:, 8:16], scale2, 1.0, pk1("g2", 0, 8), ALU.add, ALU.mult))

            dve.wait_ge(ropes_loaded, 16)

            def rotate(pr):
                x = PROJ[:, 2 * pr:2 * pr + 2, :]
                dve.wait_ge(rope_done, pr - 3)
                need(step(nc.vector.tensor_tensor(tiles(RSH[:, pr % 8, :], 2), tiles(bank[6 + pr % 2][:, :], 2),
                                                  each(rop("sin"), 2), ALU.mult)))
                need(step(nc.vector.tensor_tensor(x, x, each(rop("cos"), 2), ALU.mult)))
                nc.vector.tensor_tensor(x, x, tiles(RSH[:, pr % 8, :], 2), ALU.add).then_inc(heads_ready, 1)

            gains = [GS[:, 16:17]] * 2 + [pk1("g_ka")] * 2 + [GS[:, 17:18]] * 3 + [pk1("g_kb")] * 3
            for pr in range(10):
                dve.wait_ge(hrms_ready, pr + 1)
                need(step(nc.vector.reciprocal(RSH[:, pr % 8, :], RSH[:, pr % 8, :])))
                x = PROJ[:, 2 * pr:2 * pr + 2, :]
                nc.vector.scalar_tensor_tensor(x, x, gains[pr], tiles(RSH[:, pr % 8, :], 2), ALU.mult, ALU.mult)\
                    .then_inc(heads_ready if pr < 4 else rope_in, 1)
                if pr >= 6:
                    rotate(pr - 2)
            rotate(8)
            rotate(9)

            dve.wait_ge(bias_loaded, 16)

            def score(u):
                t = u % 2
                dve.wait_ge(scores_done, u + 1)
                if u >= 2:
                    dve.wait_ge(pt_done, u - 1)
                if u < NA_UNITS:
                    nc.vector.tensor_tensor(SC[:, u % 2, 0:S], bank[u % 2 * 2][:, 0:S], BIAS[:, u, :],
                                            ALU.add).then_inc(scored, 1)
                    n = S
                else:
                    masks = tiles(rop("dil"), 2 * DIL_GROUPS)
                    nc.vector.tensor_tensor(tiles(SC[:, u % 2, 0:512], 2), tiles(bank[u % 2 * 2][:, :], 2),
                                            masks[:, 3 * t:3 * t + 2, :], ALU.add)
                    nc.vector.tensor_tensor(SC[:, u % 2, 512:768], bank[u % 2 * 2 + 1][:, 0:S], masks[:, 3 * t + 2, :],
                                            ALU.add).then_inc(scored, 1)
                    n = 768
                dve.wait_ge(scored, u + 1)
                need(step(nc.vector.tensor_reduce(NMAX[:, u:u + 1], SC[:, u % 2, 0:n], AX.X, ALU.max)))
                nc.vector.tensor_scalar(NMAX[:, UNITS + u:UNITS + u + 1], NMAX[:, u:u + 1], -1.0, None,
                                        ALU.mult).then_inc(nmax_ready, 1)

            def outputs(u0, units, at):
                dve.wait_ge(pv_done, u0 + units)
                need(step(nc.vector.reciprocal(RDEN[:, u0:u0 + units], DEN[:, u0:u0 + units])))
                heads = units // 2
                for t in range(2):
                    nc.vector.tensor_tensor(OTOK[:, t, at:at + heads * HD].rearrange("p (h n) -> p h n", h=heads),
                                            bank[6 + t][:, 0:heads * HD].rearrange("p (h n) -> p h n", h=heads),
                                            spread(RDEN[:, u0 + t:u0 + units:2], HD), ALU.mult).then_inc(otok_ready, 1)

            for u in range(UNITS):
                score(u)
                if u == NA_UNITS + 1:
                    outputs(0, NA_UNITS, 0)
            outputs(NA_UNITS, DIL_UNITS, 512)

            def merge(c, m0, bank_a, bank_b, gate_a, gate_b, ta, tb):
                if c >= 2:
                    dve.wait_ge(merged_ready, m0 + c - 1)
                step(nc.vector.tensor_tensor(tiles(ta, 2), tiles(bank_a[:, :], 2), gate_a[:, 2 * c:2 * c + 2, :],
                                             ALU.mult))
                need(step(nc.vector.tensor_tensor(tiles(tb, 2), tiles(bank_b[:, :], 2), gate_b[:, 2 * c:2 * c + 2, :],
                                                  ALU.mult)))
                nc.vector.tensor_tensor(U[:, 2 * c:2 * c + 2, :], tiles(ta, 2), tiles(tb, 2),
                                        ALU.add).then_inc(merged_ready, 1)

            for i in range(3):
                dve.wait_ge(oth_ready, i + 1)
                nc.vector.tensor_tensor(OTL[:, 2 * i:2 * i + 2, :], tiles(bank[i][:, :], 2),
                                        OTH[:, 2 * i:2 * i + 2, :].bitcast(F32), ALU.subtract).then_inc(otl_ready, 1)
            for i in range(B1_PROJ):
                split(Q_PROJ1 + i + PARTS)
            dve.wait_ge(gates_ready, 16)
            for c in range(4):
                if c < 3:
                    dve.wait_ge(proj_done, c + 1)
                else:
                    dve.wait_ge(panel_used, Q_PROJ1 + B1_PROJ)
                merge(c, 0, bank[c], bank[4 + c], PROJ[:, GATE:GATE + 8, :], PROJ[:, GATE + 8:GATE + 16, :],
                      MTMP[:, c % 2, :], MTMP[:, 2 + c % 2, :])
            for c in range(4):
                fill_low(FILL_B1_MERGE, c)
            for j in range(B1_WO):
                split(Q_WO + j + PARTS)
                dve.wait_ge(panel_used, Q_WO + j + 1)
                residual(j, bank[j % 2][:, :], gate1)
            dve.wait_ge(residual_ready, 4)
            norm(1, FILL_B1_NORM2, GS[:, 8:16], shift2)
            ffn_hidden(0, Q_FFN0, 0)
            dve.wait_ge(panel_used, Q_LAYERS)
            for j in range(4):
                residual(j, bank[j][:, :], gate2)
            dve.wait_ge(residual_ready, 8)
            pad(DVE_B1)

            with dve.Fori(0, LAYERS) as l:
                base[0] = DVE_B1 + DVE_LAYER * l
                used0 = Q_LAYERS + L_PANELS * l
                dve.wait_ge(pack2_loaded, 16 * l + 16)
                rounds = L_ROUNDS * l
                fill = FILL_LAYER + 4 * l

                def ahead(q):
                    split(Q_LAYERS + q + PARTS, rounds)

                split(Q_LAYERS, rounds)
                split(Q_LAYERS + 1, rounds)
                norm(2 + 3 * l, fill, pk2("ffn1", 0, 8))
                ffn_hidden(1 + 2 * l, Q_LAYERS + LQ_FFN1, rounds)
                ahead(LQ_WIDE - 2)
                ahead(LQ_WIDE - 1)
                dve.wait_ge(panel_used, used0 + LQ_WIDE)
                for j in range(4):
                    residual(j, bank[j][:, :], 0.5)
                dve.wait_ge(residual_ready, 4 * (3 + 3 * l))
                norm(3 + 3 * l, fill + 1, pk2("mix", 0, 8))

                x, e, w, ln, d, m, r_ = [SMX[:, i, :] for i in (0, 2, 3, 4, 5, 6, 1)]
                dve.wait_ge(small_done, l + 1)
                nc.vector.tensor_tensor(tiles(x, 2), tiles(bank[6][:, 0:2 * SMALL], 2), each(pk2("small_b", 0, SMALL), 2),
                                        ALU.add).then_inc(small_x, 1)
                dve.wait_ge(small_x, l + 1)
                nc.vector.scalar_tensor_tensor(SMX[:, 1, :], x, -1.0, x, ALU.mult, ALU.min).then_inc(small_abs, 1)
                dve.wait_ge(small_exp, l + 1)
                nc.vector.tensor_scalar(w, e, 1.0, None, ALU.add).then_inc(small_w, 1)
                dve.wait_ge(small_w, l + 1)
                need(step(nc.vector.tensor_scalar(d, w, -1.0, None, ALU.add)))
                need(step(nc.vector.tensor_scalar(m, d, 0.0, None, ALU.is_equal)))
                need(step(nc.vector.tensor_tensor(d, d, m, ALU.add)))
                need(step(nc.vector.reciprocal(r_, d)))
                need(step(nc.vector.tensor_tensor(r_, r_, e, ALU.mult)))
                dve.wait_ge(small_ln, l + 1)
                need(step(nc.vector.tensor_tensor(ln, ln, m, ALU.add)))
                need(step(nc.vector.tensor_tensor(ln, ln, r_, ALU.mult)))
                need(step(nc.vector.scalar_tensor_tensor(SPL[:, :, :], tiles(x, 2)[:, :, 0:SP_COLS], 0.0,
                                                         tiles(ln, 2)[:, :, 0:SP_COLS], ALU.max, ALU.add)))
                dve.wait_ge(aneg_ready, l + 1)
                nc.vector.scalar_tensor_tensor(LOGA[:, :, :], SPL[:, :, :], -1.0, each(SMX[:, 7, 0:SP_COLS], 2),
                                               ALU.mult, ALU.mult).then_inc(loga_ready, 1)

                w3 = pk2("conv_w", 0, 4 * CONV_TILES).rearrange("p (j n) -> p j n", n=8)
                b3 = pk2("conv_b", 0, CONV_TILES).rearrange("p (j n) -> p j n", n=2)
                with dve.Fori(0, L_CONV // ROUND) as r:
                    for i in range(ROUND):
                        j, b = ROUND * r + i, i % 2
                        split(Q_LAYERS + LQ_WIDE + i + PARTS, rounds + r)
                        steps = 16 + 192 * l + 8 * j
                        dve.wait_ge(wide_free, WIDE0 + L_WIDE * l + j + 3)
                        dve.wait_ge(conv_ready, 24 * l + j + 1)
                        for tap in (3, 2, 1, 0):
                            for e2 in range(2):
                                acc, src = CACC[:, b, e2, :], XPAD[:, b, e2, tap:tap + S]
                                wt = w3[:, j, 4 * e2 + tap:4 * e2 + tap + 1]
                                if tap == 3:
                                    ins = nc.vector.tensor_scalar(acc, src, wt, b3[:, j, e2:e2 + 1], ALU.mult, ALU.add)
                                else:
                                    dve.wait_ge(conv_step, steps + 2 * (3 - tap) + e2 - 1)
                                    ins = nc.vector.scalar_tensor_tensor(acc, src, wt, acc, ALU.mult, ALU.add)
                                ins.then_inc(conv_step, 1)

                dve.wait_ge(cum_done, l + 1)
                need(step(nc.vector.tensor_copy(CUM[:, :], bank[6][:, 0:160])))
                nc.vector.tensor_tensor(END_A, LAST_A, CUM_A[:, 0, :], ALU.subtract)
                nc.vector.tensor_tensor(END_G, LAST_G, CUM_G, ALU.subtract)
                nc.vector.tensor_copy(BEG, CUM_G)
                nc.vector.tensor_copy(EXP_C, LAST_C).then_inc(cum_copied, 1)
                dve.wait_ge(ecum_ready, l + 1)
                dve.wait_ge(beta_ready, l + 1)
                step(nc.vector.tensor_tensor(BEG, BEG, BETA[:, :, :], ALU.mult))

                for t in range(2):
                    for q in range(4):
                        dve.wait_ge(xtok_done, 8 * l + 4 * t + q + 1)
                        nc.vector.tensor_tensor(tiles(XDT[:, t, q * 512:(q + 1) * 512], 8), tiles(bank[q][:, :], 8),
                                                spread(SPL[:, t, 8 * q:8 * q + 8], HD), ALU.mult).then_inc(xdt_ready, 1)
                dve.wait_ge(xdt_ready, 8 * l + 8)
                for g in range(GROUPS):
                    nc.vector.tensor_tensor(tiles(XEND[:, g * 512:(g + 1) * 512], 8),
                                            tiles(XDT[:, 0, g * 512:(g + 1) * 512], 8),
                                            spread(END_A[:, 8 * g:8 * g + 8], HD), ALU.mult).then_inc(xend_ready, 1)
                for t in range(2):
                    dve.wait_ge(cb_done, 2 * l + t + 1)
                    nc.vector.tensor_tensor(tiles(CBM[:, t, :], 4), tiles(bank[6 + t][:, :], 4), each(con("cum128"), 4),
                                            ALU.mult).then_inc(cbm_ready, 1)
                dve.wait_ge(cbm_ready, 2 * l + 2)

                def segment(i):
                    t, h0 = i // 8, i % 8 * 4
                    dve.wait_ge(seg_done, 16 * l + i + 1)
                    seg = tiles(SEG[:, i % 2, :], 4)
                    nc.vector.tensor_tensor(seg, tiles(bank[i % 2][:, :], 4), spread(CUM_A[:, t, h0:h0 + 4], P),
                                            ALU.subtract).then_inc(seg_taken, 1)
                    dve.wait_ge(seg_taken, 16 * l + i + 1)
                    nc.vector.tensor_scalar(SEG[:, i % 2, :], SEG[:, i % 2, :], 0.0, None, ALU.min).then_inc(seg_ready, 1)

                def mix(i):
                    t, g = i // 8, i % 8 // 2
                    dve.wait_ge(decay_ready, 16 * l + i + 1)
                    if i >= 2:
                        dve.wait_ge(y_done, 16 * l + i - 1)
                    nc.vector.tensor_tensor(tiles(MIX[:, i % 2, :], 4), tiles(SEG[:, i % 2, :], 4),
                                            each(CBM[:, t, g * P:(g + 1) * P], 4), ALU.mult).then_inc(mix_ready, 1)
                    if t == 1:
                        dve.wait_ge(row_exp_ready, 8 * l + i - 7)
                        nc.vector.tensor_tensor(tiles(CDEC[:, i % 2, :], 4), tiles(CDEC[:, i % 2, :], 4),
                                                each(CONV[:, C_TILE + g, P:2 * P], 4), ALU.mult).then_inc(cdec_ready, 1)

                def scan_out(m):
                    t, g = m // 4, m % 4
                    tok = slice(t * P, (t + 1) * P)
                    dve.wait_ge(y_done, 16 * l + 2 * m + 2)
                    for e2 in range(4):
                        x_ = CONV[:, 4 * g + e2, tok]
                        ins = nc.vector.scalar_tensor_tensor(x_, x_, pk2("ssm_d", 4 * g + e2),
                                                             bank[2 + m % 2][:, e2 * P:(e2 + 1) * P], ALU.mult, ALU.add)
                    ins.then_inc(y_taken, 1)

                segment(0)
                for i in range(16):
                    if i + 1 < 16:
                        segment(i + 1)
                    mix(i)
                    if i % 2 == 0 and i >= 2:
                        scan_out(i // 2 - 1)
                scan_out(7)
                for j in range(L_ZS + L_ZD):
                    ahead(LQ_WIDE + L_CONV + j)
                    if j < L_ZS:
                        dve.wait_ge(wide_free, 2 + WIDE0 + L_WIDE * l + L_CONV + j + 1)
                        x_ = CONV[:, 2 * j:2 * j + 2, :]
                        nc.vector.tensor_tensor(x_, x_, tiles(ZT[:, j % 2, :], 2), ALU.mult).then_inc(yg_ready, 1)
                    if j % 2 == 1 or not 4 <= j < 4 + 2 * GROUPS:
                        continue
                    g = j // 2 - 2
                    dve.wait_ge(yrms_ready, 4 * l + g + 1)
                    rs = slice(g % 2 * S, g % 2 * S + S)
                    need(step(nc.vector.reciprocal(RSTD[:, rs], RMS[:, rs])))
                    for e2 in range(4):
                        x_ = CONV[:, 4 * g + e2, :]
                        ins = nc.vector.scalar_tensor_tensor(x_, x_, pk2("ssm_norm", 4 * g + e2), RSTD[:, rs],
                                                             ALU.mult, ALU.mult)
                    ins.then_inc(ys_ready, 1)

                for pr in range(8):
                    dve.wait_ge(qkrms_ready, 8 * l + pr + 1)
                    need(step(nc.vector.reciprocal(ROOT(pr), ROOT(pr))))
                    x_ = QKV[:, 2 * pr:2 * pr + 2, :]
                    nc.vector.scalar_tensor_tensor(x_, x_, P ** -0.5 if pr < 4 else 1.0, tiles(ROOT(pr), 2), ALU.mult,
                                                   ALU.mult).then_inc(qk_ready, 1)
                for t in range(2):
                    tok = slice(t * P, (t + 1) * P)
                    for m_ in range(4):
                        b = m_ % 2
                        at, hs = slice(512 * b, 512 * b + 512), slice(4 * b, 4 * b + 4)
                        dve.wait_ge(kv_done, 8 * l + 4 * t + m_ + 1)
                        src = tiles(bank[m_][:, :], 4)
                        if m_ < 2:
                            nc.vector.tensor_tensor(tiles(KBG[:, at], 4), src, spread(BEG[:, t, hs], P), ALU.mult)
                            nc.vector.tensor_tensor(tiles(KDEC[:, at], 4), src, spread(END_G[:, t, hs], P),
                                                    ALU.mult).then_inc(kv_taken, 1)
                        else:
                            nc.vector.tensor_tensor(tiles(VB[:, at], 4), src, spread(BETA[:, t, hs], P),
                                                    ALU.mult).then_inc(kv_taken, 1)

                    def gseg(b):
                        n, at, hs = 4 * l + 2 * t + b, slice(512 * b, 512 * b + 512), slice(4 * b, 4 * b + 4)
                        dve.wait_ge(kk_done, n + 1)
                        nc.vector.tensor_tensor(tiles(DCY[:, at], 4), tiles(bank[6][:, :], 4),
                                                spread(CUM_G[:, t, hs], P), ALU.subtract).then_inc(gseg_taken, 1)
                        dve.wait_ge(gseg_taken, n + 1)
                        nc.vector.tensor_scalar(DCY[:, at], DCY[:, at], 0.0, None, ALU.min).then_inc(gseg_ready, 1)
                        dve.wait_ge(grow_ready, n + 1)
                        nc.vector.tensor_tensor(QKV[:, hs, tok], QKV[:, hs, tok], tiles(RSTD[:, :], 4),
                                                ALU.mult).then_inc(qd_ready, 1)

                    def weights(b):
                        n, at = 4 * l + 2 * t + b, slice(512 * b, 512 * b + 512)
                        dve.wait_ge(incl_ready, n + 1)
                        nc.vector.tensor_tensor(AQK[:, at], bank[5][:, :], DCY[:, at], ALU.mult).then_inc(aqk_ready, 1)
                        dve.wait_ge(strict_ready, n + 1)
                        need(step(nc.vector.tensor_tensor(MT[:, at], bank[4][:, :], DEC[:, at], ALU.mult)))
                        nc.vector.tensor_tensor(MT[:, at], MT[:, at], bank[7][:, :], ALU.mult).then_inc(mt_ready, 1)

                    for b in range(2):
                        gseg(b)
                        weights(b)
                    for v in range(LEVELS):
                        k = (2 * l + t) * LEVELS + v
                        kc = (2 * l + t) * (LEVELS - 1) + v - 1
                        for b in range(2):
                            at = slice(512 * b, 512 * b + 512)
                            if v == 0:
                                dve.wait_ge(inv_u_done, 2 * k + b + 1)
                                nc.vector.tensor_tensor(tiles(TI[:, at], 4), each(con("ident"), 4),
                                                        tiles(bank[b][:, :], 4), ALU.subtract)
                                nc.vector.tensor_tensor(tiles(TT[:, at], 4), each(con("ident"), 4),
                                                        tiles(CS[:, at], 4), ALU.subtract).then_inc(inv_ready, 1)
                                continue
                            dve.wait_ge(inv_ready, 2 * k + b - 1)
                            dve.wait_ge(inv_v_done, 2 * kc + b + 1)
                            if v < LEVELS - 1:
                                nc.vector.tensor_tensor(TI[:, at], TI[:, at], bank[2 + b][:, :], ALU.subtract)
                            nc.vector.tensor_tensor(TT[:, at], TT[:, at], bank[6 + b][:, :],
                                                    ALU.subtract).then_inc(inv_ready, 1)
                    for c in range(2):
                        cg, r0 = 2 * t + c, t * P + 64 * c
                        dve.wait_ge(o_done, 4 * l + cg + 1)
                        nc.vector.tensor_copy(QKV[:, 0:DN_HEADS, r0:r0 + 64],
                                              tiles(bank[6][:, :], 8)).then_inc(o_copied, 1)
                        for b in range(2 if cg < 3 else 0):
                            at = slice(512 * b, 512 * b + 512)
                            if cg >= 1:
                                need(step(nc.vector.tensor_tensor(tiles(ST[:, at], 4), tiles(ST[:, at], 4),
                                                                  spread(EXP_C[:, cg, 4 * b:4 * b + 4], P), ALU.mult)))
                            dve.wait_ge(st_done, 6 * l + 2 * cg + b + 1)
                            if cg >= 1:
                                nc.vector.tensor_tensor(ST[:, at], ST[:, at], bank[b][:, :],
                                                        ALU.add).then_inc(st_ready, 1)
                            else:
                                nc.vector.tensor_copy(ST[:, at], bank[b][:, :]).then_inc(st_ready, 1)
                def branch_low(i, low, high, x_):
                    dve.wait_ge(branch_hi, 12 * l + i)
                    nc.vector.tensor_tensor(low, x_, high.bitcast(F32), ALU.subtract).then_inc(branch_lo, 1)

                for j in range(L_GATES):
                    ahead(LQ_WIDE + L_CONV + L_ZS + L_ZD + j)
                    if j < 4:
                        dve.wait_ge(orms_ready, 4 * l + j + 1)
                        need(step(nc.vector.reciprocal(ROOT(j), ROOT(j))))
                        x_ = QKV[:, 2 * j:2 * j + 2, :]
                        need(step(nc.vector.scalar_tensor_tensor(x_, x_, pk2("dn_norm"), tiles(ROOT(j), 2), ALU.mult,
                                                                 ALU.mult)))
                        nc.vector.tensor_tensor(x_, x_, ZD[:, 2 * j:2 * j + 2, :], ALU.mult).then_inc(yd_ready, 1)
                    at = slice(2 * j, 2 * j + 2)
                    branch_low(j + 1 + max(0, j - 4), YSL[:, at, :], YSH[:, at, :], CONV[:, at, :])
                    if j >= 4:
                        at = slice(2 * j - 8, 2 * j - 6)
                        branch_low(j + 1 + j - 3, YDL[:, at, :], YDH[:, at, :], QKV[:, at, :])

                dve.wait_ge(wide_free, 2 + WIDE0 + L_WIDE * l + L_WIDE)
                for j in range(3):
                    ahead(LQ_PROJ + j)
                for c in range(4):
                    dve.wait_ge(panel_used, used0 + LQ_PROJ + 3 * (c + 1))
                    merge(c, 4 + 4 * l, bank[c % 2 * 2], bank[c % 2 * 2 + 1], GT[:, 0:8, :], GT[:, 8:16, :],
                          SG[:, c % 2, :], HID[:, c % 2, :])
                    for j in range(3 * c + 3, min(3 * c + 6, L_PROJ)):
                        ahead(LQ_PROJ + j)
                    fill_low(fill + 2, c)
                for j in range(4):
                    ahead(LQ_WOUT + j)
                    dve.wait_ge(panel_used, used0 + LQ_WOUT + j + 1)
                    residual(j, bank[6 + j % 2][:, :], 1.0)
                dve.wait_ge(residual_ready, 4 * (4 + 3 * l))
                norm(4 + 3 * l, fill + 3, pk2("ffn2", 0, 8))
                ffn_hidden(2 + 2 * l, Q_LAYERS + LQ_FFN2, rounds)
                dve.wait_ge(panel_used, used0 + L_PANELS)
                for j in range(4):
                    residual(j, bank[j][:, :], 0.5)
                dve.wait_ge(residual_ready, 4 * (5 + 3 * l))
                pad(DVE_LAYER)
            base[0] = DVE_B1 + DVE_LAYER * LAYERS
            norm(2 + 3 * LAYERS, None, pk1("final", 0, 8))


def _wide_panels(w):
    n = w.shape[1] // 256
    return w.reshape(KT, P, n, 256).transpose(2, 1, 0, 3).reshape(n, P, PANEL)


def _ffn_panels(w_in, w_out):
    gu = w_in.reshape(KT, P, 2, 2 * HID_PAIRS, P).transpose(3, 1, 0, 2, 4).reshape(2 * HID_PAIRS, P, PANEL)
    dn = w_out.reshape(HID_PAIRS, 2, P, D).transpose(0, 2, 1, 3).reshape(HID_PAIRS, P, PANEL)
    order = [gu[0], gu[1]]
    for i in range(HID_PAIRS):
        if i + 1 < HID_PAIRS:
            order += [gu[2 * i + 2], gu[2 * i + 3]]
        order.append(dn[i])
    return np.stack(order)


def _columns_of(v):
    return v.reshape(-1, P).T


def _pack(layout, width, parts):
    out = np.zeros((P, width), np.float32)
    for name, part in parts.items():
        a, b = layout[name]
        out[:, a:b] = part
    return out


def _constants():
    i = np.arange(P)
    s, l = i[:, None], i[None, :]
    same = s // 64 == l // 64
    parts = {
        "ident": s == l, "cum128": s <= l, "cum64": same & (s <= l), "strict64": same & (s < l), "same64": same,
        "half0": (s < 64) & (l >= 0), "half1": (s >= 64) & (l >= 0),
    }
    levels = []
    for v in range(LEVELS):
        n = 1 << v
        levels.append((s // (2 * n) == l // (2 * n)) & (s // n % 2 == 0) & (l // n % 2 == 1))
    parts["levels"] = np.concatenate(levels, 1)
    return _pack(CONSTS, CONSTS_N, parts)


def _rope_constants():
    i = np.arange(P)
    half = HD // 8
    inv = np.float32(500000.0) ** (-(np.arange(half, dtype=np.float32) * np.float32(2.0)) / np.float32(2 * half))
    ang = np.arange(S, dtype=np.float32)[:, None] * inv[None, :]
    cos, sin = np.ones((P, S), np.float32), np.zeros((P, S), np.float32)
    swap = np.zeros((P, P), np.float32)
    for at in (0, HD):
        for d in range(half):
            cos[at + d] = cos[at + half + d] = np.cos(ang[:, d])
            sin[at + d] = sin[at + half + d] = np.sin(ang[:, d])
            swap[at + half + d, at + d] = -1.0
            swap[at + d, at + half + d] = 1.0
    q, k = np.arange(S)[:, None], np.arange(S)[None, :]
    masks = []
    for window, dil in ((128, 1), (512, 4), (2048, 16)):
        seen = (np.abs(q - k) % dil == 0) & (np.abs(q - k) // dil <= window // 2 // dil)
        masks.append(np.where(seen, 0.0, NEG))
    dil_masks = np.stack(masks).reshape(DIL_GROUPS, 2, P, S).transpose(2, 1, 0, 3).reshape(P, -1)
    return _pack(ROPES, ROPES_N, {"head64": (i[:, None] // HD == i[None, :] // HD) / HD, "swap": swap, "cos": cos,
                                  "sin": sin, "dil": dil_masks})


def _na_bias(rpb):
    rows = S // GRID_W
    kh = min(NA_KH, rows)
    pos = np.arange(S)
    r, c = pos // GRID_W, pos % GRID_W
    assert kh == rows
    row_off = r[None, :] - r[:, None] + NA_KH - 1
    start = np.clip(c - NA_KW // 2, 0, GRID_W - NA_KW)
    seen = (c[None, :] >= start[:, None]) & (c[None, :] < start[:, None] + NA_KW)
    col_off = np.clip(c[None, :] - c[:, None] + NA_KW - 1, 0, 2 * NA_KW - 2)
    flat = np.concatenate([rpb.reshape(NA_HEADS, -1), np.full((NA_HEADS, 1), NEG, np.float32)], 1)
    at = np.where(seen, row_off * (2 * NA_KW - 1) + col_off, flat.shape[1] - 1)
    return flat[:, at].reshape(NA_HEADS, 2, P, S).transpose(2, 0, 1, 3).reshape(P, NA_UNITS * S)


def _layout(a):
    w_in = a["w_in"][0]
    wa, wb = 512, 768
    qa, ka, va, qb, kb, vb, gates = np.split(w_in, np.cumsum([wa, wa, wa, wb, wb, wb]), axis=1)
    wpa = a["w_proj_a"][0].reshape(4, P, 2, 512).transpose(2, 1, 0, 3).reshape(2, P, PANEL)
    wpb = a["w_proj_b"][0].reshape(2, P, D).transpose(1, 0, 2).reshape(1, P, PANEL)
    stream = [_wide_panels(np.concatenate([qa, ka, qb, kb, gates], 1)),
              _wide_panels(np.concatenate([va, vb], 1)), wpa, wpb, _wide_panels(a["w_o"][0]),
              _ffn_panels(a["w_ffn_in"][0], a["w_ffn_out"][0])]
    packs = []
    for l in range(LAYERS):
        stream.append(_ffn_panels(a["ffn1_w_in_2"][l], a["ffn1_w_out_2"][l]))
        z, xbc, dt, qkv, zd, b_, a_, gs, gd = np.split(
            a["w_in_2"][l], np.cumsum([2048, 3072, 32, 3072, 1024, 8, 8, 1024]), axis=1)
        stream.append(_wide_panels(np.concatenate([xbc, qkv, z, zd, gs, gd], 1)))
        ssm = _wide_panels(a["ssm_w_branch_2"][l][:D]), _wide_panels(a["ssm_w_branch_2"][l][D:])
        dn = _wide_panels(a["dn_w_branch_2"][l])
        stream.append(np.stack([x for c in range(4) for x in (ssm[0][c], ssm[1][c], dn[c])]))
        stream.append(_wide_panels(a["w_out_2"][l]))
        stream.append(_ffn_panels(a["ffn2_w_in_2"][l], a["ffn2_w_out_2"][l]))
        conv_w = np.concatenate([a["ssm_conv_w_2"][l], a["dn_conv_w_2"][l]], 1)
        small_w = np.concatenate([dt, a_, b_], 1).reshape(KT, P, SMALL).transpose(1, 0, 2).reshape(P, KT * SMALL)
        packs.append(_pack(PACK2, PACK2_N, {
            "ffn1": _columns_of(a["ffn1_norm_2"][l]), "mix": _columns_of(a["mix_norm_2"][l]),
            "ffn2": _columns_of(a["ffn2_norm_2"][l]),
            "conv_w": conv_w.reshape(4, CONV_TILES, P).transpose(2, 1, 0).reshape(P, 4 * CONV_TILES),
            "conv_b": np.concatenate([_columns_of(a["ssm_conv_b_2"][l]), np.zeros((P, QKV_TILES), np.float32)], 1),
            "ssm_norm": _columns_of(a["ssm_norm_2"][l]), "ssm_d": _columns_of(np.repeat(a["ssm_d_2"][l], HD)),
            "dn_norm": _columns_of(a["dn_norm_2"][l]),
            "small_b": np.concatenate([a["ssm_dt_bias_2"][l], a["dn_dt_bias_2"][l], np.zeros(8, np.float32)]),
            "a_log": np.concatenate([a["ssm_a_log_2"][l], a["dn_a_log_2"][l]]), "small_w": small_w}))
    two = lambda g: np.concatenate([g, g])[:, None]
    pack1 = _pack(PACK1, PACK1_N, {
        "c": _columns_of(a["c"][0]), "b_ada": _columns_of(a["b_ada"][0]), "g1": _columns_of(a["g_norm1"][0]),
        "g2": _columns_of(a["g_norm2"][0]), "b_gate": _columns_of(a["b_gate"][0]),
        "final": _columns_of(a["final_norm_2"]), "g_qa": two(a["g_qa"][0]), "g_ka": two(a["g_ka"][0]),
        "g_qb": two(a["g_qb"][0]), "g_kb": two(a["g_kb"][0])})
    return {
        "w_stream": np.concatenate(stream), "ada_stream": _wide_panels(a["w_ada"][0]),
        "x_t": a["x"][0].T.reshape(KT, P, S).transpose(1, 0, 2),
        "pack1": pack1, "pack2": np.stack(packs), "consts": _constants(), "ropes": _rope_constants(),
        "na_bias": _na_bias(a["rpb"][0])}


def kernel(**inputs):
    import concourse.bacc as bacc
    from concourse.bass_utils import run_bass_kernel_spmd

    laid = {k: np.ascontiguousarray(v, np.float32) for k, v in _layout({k: np.asarray(v) for k, v in inputs.items()}).items()}
    nc = bacc.Bacc("TRN2", target_bir_lowering=False, num_devices=1)
    args = {k: nc.dram_tensor(f"in_{k}", v.shape, F32, kind="ExternalInput").ap() for k, v in laid.items()}
    args["out_t"] = nc.dram_tensor("out_t", (P, KT, S), F32, kind="ExternalOutput").ap()
    build_program(nc, **args)
    r = run_bass_kernel_spmd(nc, [{f"in_{k}": v for k, v in laid.items()}], core_ids=[0])
    out = r.results[0]["out_t"]
    return out.transpose(1, 0, 2).reshape(D, S).T[None]
```

```python
import concourse.bass as bass
from concourse import mybir
from contextlib import ExitStack
import numpy as np

F32 = mybir.dt.float32
F32R = mybir.dt.float32r
ACT = mybir.ActivationFunctionType
ALU = mybir.AluOpType
AX = mybir.AxisListType

P = 128
S = 256
D = 1024
KT = D // P
HD = 64
FF = 2816
HID_PAIRS = FF // (2 * P)
LAYERS = 2
EPS = 1e-6
NEG = -1e30

QA, KA, QB, KB, GATE = 0, 4, 8, 14, 20
HEAD_PAIRS, NA_PAIRS = 10, 4
V_COLS = 512 + 768
GRID_W, NA_KH, NA_KW = 64, 8, 16
NA_HEADS, DIL_SLOTS, DIL_GROUPS = 8, 4, 3
NA_UNITS, DIL_UNITS = 2 * NA_HEADS, 2 * DIL_SLOTS
UNITS = NA_UNITS + DIL_UNITS

XBC_TILES, QKV_TILES, ZS_TILES, ZD_TILES = 24, 24, 16, 8
CONV_TILES = XBC_TILES + QKV_TILES
B_TILE, C_TILE = 16, 20
GROUPS = 4
SSM_HEADS = 32
DN_HEADS = 8
SMALL = 48
SP_COLS = 40

PANEL = 2048
RING = 3
PARTS = 2
ROUND = 6
ADA_FIRST, ADA_PANELS = 8, 24
B1_WIDE, B1_V, B1_GATES, B1_PROJ, B1_WO = 12, 5, 6, 3, 4
FFN_PANELS = 3 * HID_PAIRS
Q_WIDE1 = 0
Q_V = Q_WIDE1 + B1_WIDE
Q_GATES1 = Q_V + B1_V
Q_PROJ1 = Q_GATES1 + B1_GATES
Q_WO = Q_PROJ1 + B1_PROJ
Q_FFN0 = Q_WO + B1_WO
Q_LAYERS = Q_FFN0 + FFN_PANELS
L_CONV = CONV_TILES // 2
L_ZS, L_ZD, L_GATES = ZS_TILES // 2, ZD_TILES // 2, KT
L_WIDE = L_CONV + L_ZS + L_ZD + L_GATES
L_PROJ, L_WOUT = 12, 4
LQ_FFN1 = 0
LQ_WIDE = LQ_FFN1 + FFN_PANELS
LQ_PROJ = LQ_WIDE + L_WIDE
LQ_WOUT = LQ_PROJ + L_PROJ
LQ_FFN2 = LQ_WOUT + L_WOUT
L_PANELS = LQ_FFN2 + FFN_PANELS
N_PANELS = Q_LAYERS + LAYERS * L_PANELS
assert L_PANELS % ROUND == 0 and Q_FFN0 % ROUND == 0 and B1_WIDE % ROUND == 0 and L_CONV % ROUND == 0
L_ROUNDS = L_PANELS // ROUND
assert N_PANELS % RING == 0
WIDE0 = B1_WIDE + B1_V + B1_GATES

def columns(sizes):
    at, out = 0, {}
    for name, n in sizes:
        out[name] = (at, at + n)
        at += n
    return out, at


PACK1, PACK1_N = columns([("c", 8), ("b_ada", 48), ("g1", 8), ("g2", 8), ("b_gate", 16), ("final", 8),
                          ("g_qa", 1), ("g_ka", 1), ("g_qb", 1), ("g_kb", 1)])
PACK2, PACK2_N = columns([("ffn1", 8), ("mix", 8), ("ffn2", 8), ("conv_w", 4 * CONV_TILES), ("conv_b", CONV_TILES),
                          ("ssm_norm", 16), ("ssm_d", 16), ("dn_norm", 1), ("small_b", SMALL), ("a_log", SP_COLS),
                          ("small_w", KT * SMALL)])
LEVELS = 6
GROUP_BANKS = (0, 1, 6, 7)
KK_BANKS = ((6, 7, 4, 5), (2, 3, 0, 1))
O_BANKS = (2, 3, 6, 7)
SCAN_CONV = 6
SCAN_SLOTS = (1, 3, 6, 8, 10)
assert len(SCAN_SLOTS) == SCAN_CONV - 1
LATE_GATES = 2
LATE_SLOTS = (("level1", "level3", "chunk0", "chunk1"), ("level1", "level2", "level3", "level4", "chunk0", "chunk1"))
assert len(LATE_SLOTS[0]) == L_ZD and len(LATE_SLOTS[1]) == L_GATES - LATE_GATES


def late_panel(t, slot):
    return LATE_SLOTS[t].index(slot) + t * L_ZD if slot in LATE_SLOTS[t] else None


CONSTS, CONSTS_N = columns([("ident", P), ("cum128", P), ("cum64", P), ("floor64", P), ("same64", P),
                            ("half0", P), ("half1", P), ("levels", LEVELS * P)])
ROPES, ROPES_N = columns([("swap", P), ("cos", S), ("sin", S), ("dil", DIL_GROUPS * 2 * S)])

DVE_B1, DVE_LAYER = 256, 512


def build_program(nc, w_stream, ada_stream, x_t, pack1, pack2, consts, ropes, na_bias, out_t):
    with ExitStack() as ctx:
        def sb(name, shape):
            return ctx.enter_context(nc.sbuf_tensor(name, shape, F32))

        def sem(name):
            return ctx.enter_context(nc.semaphore(name))

        ARENA_N = CONV_TILES * S + 10752
        ARENA = sb("ARENA", [P, ARENA_N])
        arena_at = nc.sbuf_base - 4 * ARENA_N

        def part_over(name, at, shape):
            return nc.alloc_sbuf_tensor_at(name, shape, F32R, offset=arena_at + 4 * at)

        ring = sb("ring", [P, RING, PANEL])
        H = sb("H", [P, KT, S])
        SQ = sb("SQ", [P, KT * S])
        U = SQ[:, :].rearrange("p (t n) -> p t n", t=KT)

        def sb_part(name, shape):
            return ctx.enter_context(nc.sbuf_tensor(name, shape, F32R))

        HI, LO = sb_part("HI", [P, PARTS, PANEL]), sb_part("LO", [P, PARTS, PANEL])
        UH, UL = sb_part("UH", [P, KT, S]), sb_part("UL", [P, KT, S])
        RMS = sb("RMS", [P, 512])
        RSTD = sb("RSTD", [P, 512])
        PK1 = sb("PK1", [P, PACK1_N])
        PK2 = sb("PK2", [P, PACK2_N])
        CON = sb("CON", [P, CONSTS_N])
        NROOT, NRSTD = sb("NROOT", [P, 2]), sb("NRSTD", [P, 2])
        ROOT0 = sb("ROOT0", [P, 1])
        MEAN_G = sb("MEAN_G", [P, P])
        ONES = sb("ONES", [P, P])
        EPST = sb("EPST", [P, 1])
        XPAD = sb("XPAD", [P, 2, 2, S + 3])
        taken = [0]

        def region(n):
            taken[0] += n
            assert taken[0] <= ARENA_N, taken
            return ARENA[:, taken[0] - n:taken[0]]

        FFN_AT = ARENA_N - 4096
        SG = ARENA[:, FFN_AT:FFN_AT + 1024].rearrange("p (b n) -> p b n", b=2)
        HID = ARENA[:, FFN_AT + 1024:FFN_AT + 2048].rearrange("p (b n) -> p b n", b=2)
        HIDH = part_over("HIDH", FFN_AT + 2048, [P, 2, 512])
        HIDL = part_over("HIDL", FFN_AT + 3072, [P, 2, 512])

        PROJ = region(36 * S).rearrange("p (t n) -> p t n", t=36)
        VT = region(2 * V_COLS).rearrange("p (t n) -> p t n", t=2)
        BIAS_AT = taken[0]
        BIAS = region(NA_UNITS * S).rearrange("p (u n) -> p u n", u=NA_UNITS)
        ROP = region(ROPES_N)
        SC_AT = taken[0]
        SC = region(2 * 768).rearrange("p (b n) -> p b n", b=2)
        PT = region(2 * 768).rearrange("p (b n) -> p b n", b=2)
        NMAX = region(2 * UNITS)
        DEN = region(UNITS)
        RDEN = region(UNITS)
        OTOK = region(2 * 768).rearrange("p (t n) -> p t n", t=2)
        MTMP = ARENA[:, SC_AT:SC_AT + 2048].rearrange("p (t n) -> p t n", t=4)
        HROOT, HRSTD = sb("HROOT", [P, 2, 4 * HEAD_PAIRS]), sb("HRSTD", [P, 2, 4 * HEAD_PAIRS])
        OTH, OTL = part_over("OTH", BIAS_AT, [P, 6, S]), part_over("OTL", BIAS_AT + 6 * S, [P, 6, S])
        ADA1 = ARENA[:, 0:ADA_FIRST * PANEL].rearrange("p (b n) -> p b n", b=ADA_FIRST)
        ADA2 = ARENA[:, BIAS_AT:BIAS_AT + 2 * PANEL].rearrange("p (b n) -> p b n", b=2)
        ADA_SUM = ARENA[:, SC_AT:SC_AT + 4096].rearrange("p (b n) -> p b n", b=16)
        assert ADA_FIRST * PANEL <= SC_AT
        MOD = sb("MOD", [P, 48])
        CACT = sb("CACT", [P, 8])
        GS = sb("GS", [P, 24])

        taken[0] = 0
        CONV = region(CONV_TILES * S).rearrange("p (t n) -> p t n", t=CONV_TILES)
        TMP_AT = taken[0]
        QKV = CONV[:, XBC_TILES:, :]
        ZD = CONV[:, B_TILE:B_TILE + ZD_TILES, :]
        GT = QKV[:, DN_HEADS:DN_HEADS + 2 * KT, :]
        SMX = sb("SMX", [P, 8, 2 * SMALL])
        SPL = sb("SPL", [P, 2, SP_COLS])
        LOGA = sb("LOGA", [P, 2, SP_COLS])
        BETA = sb("BETA", [P, 2, DN_HEADS])
        CUM = sb("CUM", [P, 160])
        CUM_A = CUM[:, 0:64].rearrange("p (t h) -> p t h", t=2)
        CUM_G = CUM[:, 64:80].rearrange("p (t h) -> p t h", t=2)
        LAST_G = CUM[:, 80:96].rearrange("p (t h) -> p t h", t=2)
        LAST_A = CUM[:, 96:128]
        LAST_C = CUM[:, 128:160].rearrange("p (c h) -> p c h", c=4)
        ECUM = sb("ECUM", [P, 128])
        END_A = ECUM[:, 0:32]
        END_G = ECUM[:, 32:48].rearrange("p (t h) -> p t h", t=2)
        BEG = ECUM[:, 48:64].rearrange("p (t h) -> p t h", t=2)
        EXP_C = ECUM[:, 64:96].rearrange("p (c h) -> p c h", c=4)
        XDT = region(2 * 2048).rearrange("p (t n) -> p t n", t=2)
        STATE = region(2048)
        CBM = region(2 * 512).rearrange("p (t n) -> p t n", t=2)
        BTOK = region(512)
        SEG = region(2 * 512).rearrange("p (b n) -> p b n", b=2)
        MIX = region(2 * 512).rearrange("p (b n) -> p b n", b=2)
        CDEC = region(2 * 512).rearrange("p (b n) -> p b n", b=2)
        XEND = SQ
        ZT = ARENA[:, TMP_AT:TMP_AT + 1024].rearrange("p (b n) -> p b n", b=2)
        QSQ = ARENA[:, TMP_AT + 1024:TMP_AT + 5120].rearrange("p (b t n) -> p b t n", b=8, t=2)
        GRMS = sb("GRMS", [P, GROUPS, S])
        QROOT, QR = sb("QROOT", [P, 2, 16]), sb("QR", [P, 2, 16])
        YSL, YDL = part_over("YSL", 0, [P, 16, S]), part_over("YDL", XBC_TILES * S, [P, 8, S])
        YSH, YDH = part_over("YSH", TMP_AT, [P, 16, S]), part_over("YDH", TMP_AT + 16 * S, [P, 8, S])
        taken[0] = TMP_AT
        KBG = region(1024)
        KDEC = region(1024)
        VB = region(1024)
        MT = region(1024)
        AQK = region(1024)
        TI = region(1024)
        TT = region(1024)
        UB = region(1024)
        DEC = region(1024)
        DCY = region(1024)
        ST = SQ[:, 0:1024]
        CS = SQ[:, 1024:2048]
        WT = UB
        GROW = (RSTD, RMS)

        VN = MT

        bank = [ctx.enter_context(nc.psum_tensor(f"bank{i}", [P, 512], F32)) for i in range(8)]

        panel_loaded = [sem(f"panel_loaded{i}") for i in range(RING)]
        hi_ready, lo_ready = sem("hi_ready"), sem("lo_ready")
        panel_used = sem("panel_used")
        uh_ready, ul_ready = sem("uh_ready"), sem("ul_ready")
        ada1_loaded = [sem(f"ada1_loaded{i}") for i in range(ADA_FIRST)]
        ada2_loaded = [sem(f"ada2_loaded{i}") for i in range(2)]
        ada1_step, ada2_step, ada_done, ada_copied = sem("ada1_step"), sem("ada2_step"), sem("ada_done"), sem("ada_copied")
        hid_product, hidh_ready = sem("hid_product"), sem("hidh_ready")
        down_done = sem("down_done")
        oth_ready, otl_ready = sem("oth_ready"), sem("otl_ready")
        branch_hi, branch_lo = sem("branch_hi"), sem("branch_lo")
        x_loaded, pack1_loaded, consts_loaded = sem("x_loaded"), sem("pack1_loaded"), sem("consts_loaded")
        bias_loaded = [sem(f"bias_loaded{i}") for i in range(2)]
        ropes_loaded, pack2_loaded = sem("ropes_loaded"), sem("pack2_loaded")
        fills_done = sem("fills_done")
        out_stored = sem("out_stored")
        dve_done = sem("dve_done")
        residual_ready, squares_ready, squares_added, sumsq_ready = (
            sem("residual_ready"), sem("squares_ready"), sem("squares_added"), sem("sumsq_ready"))
        rms_ready, nrstd_ready, nspread_done, u_ready, rstd_copied, xn_ready = (
            sem("rms_ready"), sem("nrstd_ready"), sem("nspread_done"), sem("u_ready"), sem("rstd_copied"), sem("xn_ready"))
        wide_free = sem("wide_free")
        conv_step, conv_ready = sem("conv_step"), sem("conv_ready")
        gate_act_ready, hidden_ready = sem("gate_act_ready"), sem("hidden_ready")
        c_ready = sem("c_ready")
        hsq_ready, hss_ready, hrms_ready = sem("hsq_ready"), sem("hss_ready"), sem("hrms_ready")
        hrstd_ready, hspread_done, hnorm_ready = sem("hrstd_ready"), sem("hspread_done"), sem("hnorm_ready")
        rope_done, heads_ready, gates_ready = (
            sem("rope_done"), sem("heads_ready"), sem("gates_ready"))
        scores_done, scored, nmax_ready, probs_ready = (
            sem("scores_done"), sem("scored"), sem("nmax_ready"), sem("probs_ready"))
        pt_done, pt_copied, pv_done, otok_ready = sem("pt_done"), sem("pt_copied"), sem("pv_done"), sem("otok_ready")
        ot_done = sem("ot_done")
        proj_done, gated_a, merged_ready = sem("proj_done"), sem("gated_a"), sem("merged_ready")
        small_done, small_x, small_abs, small_exp, small_w, small_ln = (
            sem("small_done"), sem("small_x"), sem("small_abs"), sem("small_exp"), sem("small_w"), sem("small_ln"))
        beta_ready, aneg_ready, loga_ready, cum_done, cum_copied, ecum_ready = (
            sem("beta_ready"), sem("aneg_ready"), sem("loga_ready"), sem("cum_done"), sem("cum_copied"),
            sem("ecum_ready"))
        xtok_done, xdt_ready, btok_done, btok_copied, xend_ready = (
            sem("xtok_done"), sem("xdt_ready"), sem("btok_done"), sem("btok_copied"), sem("xend_ready"))
        state_done, state_copied, cb_done, cbm_ready = (
            sem("state_done"), sem("state_copied"), sem("cb_done"), sem("cbm_ready"))
        seg_done, seg_taken, seg_ready, row_exp_ready, decay_ready, mix_ready, cdec_ready = (
            sem("seg_done"), sem("seg_taken"), sem("seg_ready"), sem("row_exp_ready"), sem("decay_ready"),
            sem("mix_ready"), sem("cdec_ready"))
        y_done, y_taken, yg_ready, ysq_ready, yss_done, yrms_ready, ys_ready = (
            sem("y_done"), sem("y_taken"), sem("yg_ready"), sem("ysq_ready"), sem("yss_done"), sem("yrms_ready"),
            sem("ys_ready"))
        qksq_ready, qkss_done, qkrms_ready, qk_ready = (
            sem("qksq_ready"), sem("qkss_done"), sem("qkrms_ready"), sem("qk_ready"))
        qkr_ready, qkb_done, or_ready, ob_done = sem("qkr_ready"), sem("qkb_done"), sem("or_ready"), sem("ob_done")
        kv_done, k_taken, vb_ready, kk_done, gseg_ready, grow_ready, gdec_ready = (
            sem("kv_done"), sem("k_taken"), sem("vb_ready"), sem("kk_done"), sem("gseg_ready"),
            sem("grow_ready"), sem("gdec_ready"))
        aqk_ready, qd_ready, c0_ready = sem("aqk_ready"), sem("qd_ready"), sem("c0_ready")
        cs_ready, inv_u_done, inv_u_copied, inv_v_done, inv_ready = (
            sem("cs_ready"), sem("inv_u_done"), sem("inv_u_copied"), sem("inv_v_done"), sem("inv_ready"))
        wt_done, wt_copied, vn_done, vn_copied, o_done, o_copied, st_done, st_ready = (
            sem("wt_done"), sem("wt_copied"), sem("vn_done"), sem("vn_copied"), sem("o_done"), sem("o_copied"),
            sem("st_done"), sem("st_ready"))
        osq_ready, oss_done, orms_ready, yd_ready = (
            sem("osq_ready"), sem("oss_done"), sem("orms_ready"), sem("yd_ready"))

        def con(name):
            return CON[:, CONSTS[name][0]:CONSTS[name][1]]

        def rop(name):
            return ROP[:, ROPES[name][0]:ROPES[name][1]]

        def pk1(name, i=0, n=1):
            return PK1[:, PACK1[name][0] + i:PACK1[name][0] + i + n]

        def pk2(name, i=0, n=1):
            return PK2[:, PACK2[name][0] + i:PACK2[name][0] + i + n]

        def tiles(x, t):
            return x.rearrange("p (t n) -> p t n", t=t)

        def spread(x, n):
            return x.unsqueeze(2).to_broadcast([P, x.shape[1], n])

        def each(x, h):
            return x.unsqueeze(1).to_broadcast([P, h, x.shape[1]])

        def norm_no(l, i):
            return 2 + 3 * l + i

        FILL_B1_NORM1, FILL_B1_MERGE, FILL_B1_NORM2, FILL_LAYER = 0, 1, 2, 3

        block = ctx.enter_context(nc.Block())

        @block.sync
        def _(sp):
            sp.dma_start(PK1[:, :], pack1).then_inc(pack1_loaded, 16)
            sp.dma_start(H[:, :, :], x_t).then_inc(x_loaded, 16)
            sp.dma_start(CON[:, :], consts).then_inc(consts_loaded, 16)
            for i in range(ADA_FIRST):
                sp.dma_start(ADA1[:, i, :], ada_stream[i]).then_inc(ada1_loaded[i], 16)

            def load(q, slot):
                sp.dma_start(ring[:, slot, :], w_stream[q]).then_inc(panel_loaded[slot], 16)

            for q in range(RING):
                load(q, q)
            with sp.Fori(1, N_PANELS // RING) as r:
                for s in range(RING):
                    sp.wait_ge(lo_ready, (r - 1) * RING + s + 1)
                    load(r * RING + s, s)
            sp.wait_ge(u_ready, KT * (norm_no(LAYERS, 0) + 1))
            sp.dma_start(out_t, U[:, :, :]).then_inc(out_stored, 16)
            sp.wait_ge(out_stored, 16)

        @block.gpsimd
        def _(pool):
            pool.wait_ge(rstd_copied, 1)
            for k in range(KT):
                ins = nc.gpsimd.tensor_tensor(U[:, k, :], H[:, k, :], RSTD[:, 0:S], ALU.mult)
            ins.then_inc(xn_ready, 1)
            pool.wait_ge(ada1_step, KT * ADA_FIRST)
            pool.wait_ge(ada_done, 1)
            for b in range(2):
                pool.dma_start(ADA2[:, b, :], ada_stream[ADA_FIRST + b]).then_inc(ada2_loaded[b], 16)
            pool.dma_start(ROP, ropes).then_inc(ropes_loaded, 16)
            pool.wait_ge(ada_copied, 1)
            sums4 = ADA_SUM.rearrange("p (r b) n -> p r b n", b=2)

            def ada_sum(r, b):
                pool.wait_ge(ada2_loaded[b], 16 * r + 16)
                src, done = tiles(ADA2[:, b, :], KT), 8 * r + 4 * b
                nc.gpsimd.tensor_tensor(src, src, spread(CACT[:, :], S), ALU.mult).then_inc(ada2_step, 1)
                for i, n in enumerate((4, 2)):
                    pool.wait_ge(ada2_step, done + i + 1)
                    nc.gpsimd.tensor_tensor(src[:, 0:n, :], src[:, 0:n, :], src[:, n:2 * n, :],
                                            ALU.add).then_inc(ada2_step, 1)
                pool.wait_ge(ada2_step, done + 3)
                nc.gpsimd.tensor_tensor(sums4[:, r, b, :], src[:, 0, :], src[:, 1, :], ALU.add).then_inc(ada2_step, 1)

            last = (ADA_PANELS - ADA_FIRST) // 2 - 1
            with pool.Fori(0, last) as r:
                for b in range(2):
                    ada_sum(r, b)
                    pool.wait_ge(ada2_step, 8 * r + 4 * b + 4)
                    pool.dma_start(ADA2[:, b, :], ada_stream[ADA_FIRST + 2 + 2 * r + b]).then_inc(ada2_loaded[b], 16)
            for b in range(2):
                ada_sum(last, b)
                pool.wait_ge(ada2_step, 8 * last + 4 * b + 4)
                units = slice(b * NA_UNITS // 2, (b + 1) * NA_UNITS // 2)
                pool.dma_start(BIAS[:, units, :], tiles(na_bias, NA_UNITS)[:, units, :]).then_inc(bias_loaded[b], 16)
            pool.wait_ge(consts_loaded, 16)

            def split(q, panels=0):
                pool.wait_ge(lo_ready, q + panels)
                pool.wait_ge(hi_ready, q + 1 + panels)
                nc.gpsimd.tensor_tensor(LO[:, q % PARTS, :], ring[:, q % RING, :], HI[:, q % PARTS, :].bitcast(F32),
                                        ALU.subtract).then_inc(lo_ready, 1)

            split(Q_FFN0 + 1)
            with pool.Fori(0, LAYERS) as l:
                pool.wait_ge(u_ready, KT * (2 + 3 * l))
                pool.dma_start(PK2[:, :], pack2[l]).then_inc(pack2_loaded, 16)
                split(Q_LAYERS + 1, L_PANELS * l)
                split(Q_LAYERS + LQ_WIDE + 1, L_PANELS * l)
                pool.wait_ge(ecum_ready, l + 1)
                for g in range(GROUPS):
                    pool.wait_ge(xdt_ready, 8 * l + g + 1)
                    nc.gpsimd.tensor_tensor(tiles(XEND[:, g * 512:(g + 1) * 512], 8),
                                            tiles(XDT[:, 0, g * 512:(g + 1) * 512], 8),
                                            spread(END_A[:, 8 * g:8 * g + 8], HD), ALU.mult).then_inc(xend_ready, 1)
                for j in range(L_CONV - SCAN_CONV, L_CONV):
                    split(Q_LAYERS + LQ_WIDE + j + PARTS, L_PANELS * l)
                for t in range(2):
                    for v in range(1, LEVELS):
                        for b in range(2):
                            k = (2 * l + t) * LEVELS + v
                            if v == 1:
                                pool.wait_ge(inv_ready, 2 * (k - 1) + b + 1)
                            else:
                                pool.wait_ge(inv_u_done, 2 * (k - 1) + b + 1)
                            lev = con("levels")[:, v * P:(v + 1) * P]
                            nc.gpsimd.tensor_tensor(tiles(CS[:, 512 * b:512 * b + 512], 4),
                                                    tiles(MT[:, 512 * b:512 * b + 512], 4), each(lev, 4),
                                                    ALU.mult).then_inc(cs_ready, 1)
                split(Q_LAYERS + LQ_FFN2 + 1, L_PANELS * l)

        @block.tensor
        def _(pe):
            def panel(q, rounds=0):
                pe.wait_ge(lo_ready, q + 1 + ROUND * rounds)
                return HI[:, q % PARTS, :], LO[:, q % PARTS, :]

            def product(out, left, right, start, stop, **kw):
                (lh, ll), (rh, rl) = left, right
                nc.tensor.matmul(out, lh, rh, start=start, stop=False, **kw)
                nc.tensor.matmul(out, lh, rl, start=False, stop=False, **kw)
                return nc.tensor.matmul(out, ll, rh, start=False, stop=stop, **kw)

            def both(parts, f):
                return f(parts[0]), f(parts[1])

            def u_parts(k):
                return UH[:, k, :], UL[:, k, :]

            def norm(n):
                first = isinstance(n, int) and n == 0
                pairs = KT // 2 if first else KT // 2 - 1
                for k in range(pairs):
                    if first or k < pairs - 1:
                        pe.wait_ge(squares_ready, KT // 2 * n + k + 1)
                    else:
                        pe.wait_ge(squares_added, n)
                    for e in range(2):
                        for t in range(2):
                            at = (2 * k + e) * S + t * P
                            mm = nc.tensor.matmul(bank[4 + t][:, 0:1], SQ[:, at:at + P], ONES[:, 0:1],
                                                  start=(k + e == 0), stop=(k == pairs - 1 and e == 1))
                mm.then_inc(sumsq_ready, 1)
                pe.wait_ge(nrstd_ready, n + 1)
                for t in range(2):
                    mm = spread_tokens(bank[6][:, t * P:(t + 1) * P], NRSTD[:, t:t + 1])
                mm.then_inc(nspread_done, 1)

            def both_tiles(outs, src, fill):
                one_bank = len(outs) == 1
                high, low = src
                for pair in range(KT // 2):
                    both_k = [(k, e) for k in (2 * pair, 2 * pair + 1) for e in range(2)]

                    def part(left, k, e, right, start, stop):
                        out = outs[0][:, e * S:(e + 1) * S] if one_bank else outs[e]
                        return nc.tensor.matmul(out, left[:, k, e * P:(e + 1) * P], right[:, k, :], start=start, stop=stop,
                                                skip_group_check=True)

                    pe.wait_ge(uh_ready, 4 * fill + pair + 1)
                    for k, e in both_k:
                        part(high, k, e, UH, start=(k == 0 and not (one_bank and e)), stop=False)
                        part(low, k, e, UH, start=False, stop=False)
                    pe.wait_ge(ul_ready, 4 * fill + pair + 1)
                    for k, e in both_k:
                        mm = part(high, k, e, UL, start=False, stop=(k == KT - 1))
                return mm

            def wide(w, q, rounds, par, fill=None):
                if fill is not None:
                    src = both(panel(q, rounds), lambda x: tiles(x, KT))
                    pe.wait_ge(wide_free, w + 1)
                    both_tiles((bank[4 + par],), src, fill).then_inc(panel_used, 1)
                    return
                for e in range(2):
                    wide_half(w, q, rounds, par, e)

            def wide_half(w, q, rounds, par, e):
                src = both(panel(q, rounds), lambda x: tiles(x, KT))
                if e == 0:
                    pe.wait_ge(wide_free, w + 1)
                for k in range(KT):
                    mm = product(bank[4 + par][:, e * S:(e + 1) * S], both(src, lambda x: x[:, k, e * P:(e + 1) * P]),
                                 u_parts(k), start=(k == 0), stop=(k == KT - 1))
                if e == 1:
                    mm.then_inc(panel_used, 1)

            def squares_summed(sq, tile, out):
                for t in range(2):
                    mm = nc.tensor.matmul(out(t, tile), sq[:, t * P:(t + 1) * P], ONES[:, 0:1], start=True, stop=True)
                return mm

            def spread_tokens(out, column):
                return nc.tensor.matmul(out, column.to_broadcast([P, P]), con("ident"), start=True, stop=True)

            def ffn(f, q0, rounds, fill):
                def gate_up(q, rr, par, fill=None):
                    for e in range(2):
                        src = both(panel(q + e, rr), lambda x: tiles(x, KT))
                        if fill is not None and e == 0:
                            mm = both_tiles([bank[4 + 2 * par + half][:, 0:S] for half in range(2)], src, fill)
                        else:
                            for half in range(2):
                                for k in range(KT):
                                    mm = product(bank[4 + 2 * par + half][:, e * S:(e + 1) * S],
                                                 both(src, lambda x: x[:, k, half * P:(half + 1) * P]), u_parts(k),
                                                 start=(k == 0), stop=(k == KT - 1))
                        mm.then_inc(panel_used, 1)

                def down(i, q, rr, par, first=False, last=False):
                    src = panel(q, rr)
                    pe.wait_ge(hidden_ready, f * HID_PAIRS + i + 1)
                    for e in range(2):
                        for j in range(KT):
                            mm = product(bank[j // 2][:, (j % 2) * S:(j % 2 + 1) * S],
                                         both(src, lambda x: x[:, e * D + j * P:e * D + (j + 1) * P]),
                                         both((HIDH, HIDL), lambda x: x[:, par, e * S:(e + 1) * S]),
                                         start=(first and e == 0 and j % 2 == 0),
                                         stop=(last and e == 1), skip_group_check=True)
                            if last and e == 1 and j % 2 == 1 and j < KT - 1:
                                mm.then_inc(down_done, 1)
                    mm.then_inc(panel_used, 1)

                gate_up(q0, rounds, 0, fill)
                gate_up(q0 + 2, rounds, 1)
                down(0, q0 + 4, rounds, 0, first=True)
                with pe.Fori(0, 4) as r:
                    for b in range(2):
                        gate_up(q0 + 5 + 3 * b, rounds + r, b)
                        down(r * 2 + 1 + b, q0 + 7 + 3 * b, rounds + r, 1 - b)
                gate_up(q0 + 29, rounds, 0)
                down(9, q0 + 31, rounds, 1)
                down(10, q0 + 32, rounds, 0, last=True)

            def ada_columns(to, n, done):
                for i in range(n):
                    pe.wait_ge(*done(i))
                    for e in range(2):
                        mm = nc.tensor.matmul(to[:, 2 * i + e:2 * i + e + 1], ADA_SUM[:, i, e * P:(e + 1) * P],
                                              ONES[:, 0:1], start=True, stop=True)
                return mm

            pe.wait_ge(fills_done, 1)
            pe.wait_ge(consts_loaded, 16)
            norm(0)
            ada_columns(bank[7], ADA_FIRST, lambda i: (ada1_step, KT * (i // 2 * 2 + 2))).then_inc(ada_done, 1)
            with pe.Fori(0, B1_WIDE // ROUND) as r:
                for s in range(ROUND):
                    wide(r * ROUND + s, Q_WIDE1 + s, r, s % 2, FILL_B1_NORM1 if s == 0 else None)
            pe.wait_ge(ropes_loaded, 16)

            def head_sums(pr):
                pe.wait_ge(hsq_ready, pr + 1)
                at = CONSTS["half0"][0]
                for e in range(2):
                    for t in range(2):
                        sq = pr % 4 * 512 + e * S + t * P
                        to = 2 * (2 * pr + e) + t * 4 * HEAD_PAIRS
                        mm = nc.tensor.matmul(bank[int(pr >= NA_PAIRS)][:, to:to + 2], SQ[:, sq:sq + P],
                                              CON[:, at:at + P + 1:P], start=True, stop=True)
                mm.then_inc(hss_ready, 1)

            def head_spread(pr):
                pe.wait_ge(hrstd_ready, 1 if pr < NA_PAIRS else 2)
                if pr >= 2:
                    pe.wait_ge(hnorm_ready, pr - 1)
                for e in range(2):
                    for t in range(2):
                        for half in range(2):
                            c = 2 * (2 * pr + e) + half
                            to = bank[2 + pr % 2][half * HD:(half + 1) * HD, e * S + t * P:e * S + (t + 1) * P]
                            mm = nc.tensor.matmul(to, HRSTD[:, t, c:c + 1].to_broadcast([P, HD]), con("ident"), start=True,
                                                  stop=True)
                mm.then_inc(hspread_done, 1)

            def rope(pr):
                pe.wait_ge(hnorm_ready, pr + 1)
                if pr >= NA_PAIRS + 2:
                    pe.wait_ge(heads_ready, pr - NA_PAIRS - 1)
                nc.tensor.matmul(bank[6 + pr % 2][:, :], rop("swap"), PROJ[:, 2 * pr:2 * pr + 2, :],
                                 start=True, stop=True).then_inc(rope_done, 1)

            for c in range(B1_V):
                src = both(panel(Q_V + c), lambda x: tiles(x, KT))
                pe.wait_ge(wide_free, B1_WIDE + c + 1)
                for t in range(2):
                    for k in range(KT):
                        mm = product(bank[4 + c % 2][:, t * S:(t + 1) * S], both(u_parts(k), lambda x: x[:, t * P:(t + 1) * P]),
                                     both(src, lambda x: x[:, k, :]), start=(k == 0), stop=(k == KT - 1))
                mm.then_inc(panel_used, 1)
                if c >= 1:
                    head_sums(2 * c - 2)
                    head_sums(2 * c - 1)
            for g in range(B1_GATES):
                wide(B1_WIDE + B1_V + g, Q_GATES1 + g, 0, (B1_V + g) % 2)
                if g == 0:
                    head_sums(8)
                    head_sums(9)
                if g <= 4:
                    head_spread(2 * g)
                    head_spread(2 * g + 1)
                if 3 <= g:
                    rope(2 * g - 2)
                    rope(2 * g - 1)

            def heads(u):
                if u < NA_UNITS:
                    return u % 2, [(QA, KA, u // 2, (u // 2) * HD)]
                j, t = (u - NA_UNITS) // 2, u % 2
                return t, [(QB, KB, g * DIL_SLOTS + j, 512 + (g * DIL_SLOTS + j) * HD) for g in range(DIL_GROUPS)]

            def scores(u):
                t, hs = heads(u)
                if u == NA_UNITS:
                    pe.wait_ge(ada_copied, 2)
                if u >= 2:
                    pe.wait_ge(scored, u - 1)
                for g, (q0, k0, h, _) in enumerate(hs):
                    at = h % 2 * HD
                    mm = nc.tensor.matmul(bank[u % 2 * 2 + g // 2][:, g % 2 * S:(g % 2 + 1) * S],
                                          PROJ[at:at + HD, q0 + h // 2, t * P:(t + 1) * P],
                                          PROJ[at:at + HD, k0 + h // 2, :], start=True, stop=True)
                mm.then_inc(scores_done, 1)

            def turn(u):
                pe.wait_ge(probs_ready, u + 1)
                if u >= 1:
                    pe.wait_ge(pt_copied, u)
                for k in range(2 * len(heads(u)[1])):
                    mm = nc.tensor.transpose(bank[4 + k // 4][:, k % 4 * P:(k % 4 + 1) * P],
                                             SC[:, u % 2, k * P:(k + 1) * P], con("ident"))
                mm.then_inc(pt_done, 1)

            def values(u):
                t, hs = heads(u)
                pe.wait_ge(pt_copied, u + 1)
                if u == NA_UNITS:
                    pe.wait_ge(otok_ready, 2)
                at = (u // 2 if u < NA_UNITS else (u - NA_UNITS) // 2) * HD
                for g, (_, _, _, v0) in enumerate(hs):
                    for k in range(2):
                        mm = nc.tensor.matmul(bank[6 + t][:, at:at + HD],
                                              PT[:, u % 2, (2 * g + k) * P:(2 * g + k + 1) * P],
                                              VT[:, k, v0:v0 + HD], start=(g + k == 0),
                                              stop=(g == len(hs) - 1 and k == 1))
                mm.then_inc(pv_done, 1)

            ada_columns(bank[3], ADA_PANELS - ADA_FIRST, lambda i: (ada2_step, 4 * (i + 1))).then_inc(ada_done, 1)
            pe.wait_ge(heads_ready, HEAD_PAIRS - NA_PAIRS)
            pe.wait_ge(wide_free, 2 + WIDE0)
            scores(0)
            for u in range(UNITS):
                if u + 1 < UNITS:
                    scores(u + 1)
                turn(u)
                if u >= 1:
                    values(u - 1)
            values(UNITS - 1)
            pe.wait_ge(otok_ready, 4)
            for k in range(6):
                for t in range(2):
                    mm = nc.tensor.transpose(bank[k // 2][:, k % 2 * S + t * P:k % 2 * S + (t + 1) * P],
                                             OTOK[:, t, k * P:(k + 1) * P], con("ident"))
            mm.then_inc(ot_done, 1)
            pe.wait_ge(otl_ready, 3)
            for i in range(2):
                src = both(panel(Q_PROJ1 + i), lambda x: tiles(x, 4))
                for c in (2 * i, 2 * i + 1):
                    for e in range(2):
                        for k in range(4):
                            at = c % 2 * S + e * P
                            mm = product(bank[c][:, e * S:(e + 1) * S], both(src, lambda x: x[:, k, at:at + P]),
                                         (OTH[:, k, :], OTL[:, k, :]), start=(k == 0), stop=(k == 3))
                mm.then_inc(panel_used, 1)
            src = both(panel(Q_PROJ1 + 2), lambda x: tiles(x, 2))
            for c in range(4):
                for e in range(2):
                    for k in range(2):
                        at = c * S + e * P
                        mm = product(bank[4 + c][:, e * S:(e + 1) * S], both(src, lambda x: x[:, k, at:at + P]),
                                     (OTH[:, 4 + k, :], OTL[:, 4 + k, :]), start=(k == 0), stop=(k == 1))
                mm.then_inc(proj_done if c < 3 else panel_used, 1)

            def to_residual(q, rounds, fill, v, first):
                for j in range(4):
                    src = both(panel(q + j, rounds), lambda x: tiles(x, KT))
                    if j >= 2:
                        pe.wait_ge(residual_ready, 4 * (v - 1) + j - 1)
                    for e in range(2 if j else 0):
                        for k in range(KT):
                            mm = product(bank[first + j % 2][:, e * S:(e + 1) * S],
                                         both(src, lambda x: x[:, k, e * P:(e + 1) * P]), u_parts(k),
                                         start=(k == 0), stop=(k == KT - 1))
                    if j == 0:
                        mm = both_tiles((bank[first],), src, fill)
                    mm.then_inc(panel_used, 1)

            to_residual(Q_WO, 0, FILL_B1_MERGE, 1, 0)
            norm(1)
            ffn(0, Q_FFN0, 0, FILL_B1_NORM2)

            with pe.Fori(0, LAYERS) as l:
                rounds = l * L_ROUNDS
                fill = FILL_LAYER + 4 * l
                w0 = WIDE0 + L_WIDE * l
                norm(2 + 3 * l)
                ffn(1 + 2 * l, Q_LAYERS + LQ_FFN1, rounds, fill)
                norm(3 + 3 * l)
                pe.wait_ge(pack2_loaded, 16 * l + 16)
                for k in range(KT):
                    pe.wait_ge(u_ready, KT * (3 + 3 * l) + k + 1)
                    for t in range(2):
                        mm = nc.tensor.matmul(bank[7][:, t * SMALL:(t + 1) * SMALL], U[:, k, t * P:(t + 1) * P],
                                              pk2("small_w", k * SMALL, SMALL), start=(k + t == 0), stop=(k == KT - 1),
                                              skip_group_check=True)
                mm.then_inc(small_done, 1)
                with pe.Fori(0, (L_CONV - SCAN_CONV) // ROUND) as r:
                    for s in range(ROUND):
                        wide(w0 + r * ROUND + s, Q_LAYERS + LQ_WIDE + s, rounds + r, s % 2,
                             fill + 1 if s == 0 else None)
                pe.wait_ge(loga_ready, l + 1)
                for t in range(2):
                    a, g = LOGA[:, t, 0:SSM_HEADS], LOGA[:, t, SSM_HEADS:SP_COLS]
                    nc.tensor.matmul(bank[6][:, 32 * t:32 * t + 32], con("cum128"), a, start=True, stop=True)
                    nc.tensor.matmul(bank[6][:, 64 + 8 * t:72 + 8 * t], con("cum64"), g, start=True, stop=True)
                    nc.tensor.matmul(bank[6][:, 80 + 8 * t:88 + 8 * t], con("same64"), g, start=True, stop=True)
                    for c in range(2):
                        at = 128 + 8 * (2 * t + c)
                        nc.tensor.matmul(bank[6][:, at:at + 8], con(f"half{c}"), g, start=True, stop=True)
                nc.tensor.matmul(bank[6][:, 96:128], ONES[:, :], LOGA[:, 0, 0:SSM_HEADS], start=True,
                                 stop=True).then_inc(cum_done, 1)
                pe.wait_ge(conv_ready, L_CONV * l + XBC_TILES // 2)
                for t in range(2):
                    for q in range(4):
                        i = 4 * t + q
                        if i >= 4:
                            pe.wait_ge(xdt_ready, 8 * l + i - 3)
                        for e in range(4):
                            mm = nc.tensor.transpose(bank[q][:, e * P:(e + 1) * P],
                                                     CONV[:, 4 * q + e, t * P:(t + 1) * P], con("ident"))
                        mm.then_inc(xtok_done, 1)
                    if t == 0:
                        j = L_CONV - SCAN_CONV
                        wide(w0 + j, Q_LAYERS + LQ_WIDE + j, rounds, j % 2)
                for g in range(GROUPS):
                    mm = nc.tensor.transpose(bank[7][:, g * P:(g + 1) * P], CONV[:, B_TILE + g, 0:P], con("ident"))
                mm.then_inc(btok_done, 1)
                pe.wait_ge(btok_copied, l + 1)
                for g in range(GROUPS):
                    pe.wait_ge(xend_ready, 4 * l + g + 1)
                    pe.wait_ge(xdt_ready, 8 * l + 4 + g + 1)
                    nc.tensor.matmul(bank[g][:, :], BTOK[:, g * P:(g + 1) * P], XEND[:, g * 512:(g + 1) * 512],
                                     start=True, stop=True).then_inc(state_done, 1)
                pe.wait_ge(cum_copied, l + 1)
                for t in range(2):
                    for g in range(GROUPS):
                        mm = nc.tensor.matmul(bank[6 + t][:, g * P:(g + 1) * P], CONV[:, B_TILE + g, t * P:(t + 1) * P],
                                              CONV[:, C_TILE + g, t * P:(t + 1) * P], start=True, stop=True)
                    mm.then_inc(cb_done, 1)
                pe.wait_ge(state_copied, 4 * l + 4)

                def decay_rows(i):
                    t, h0 = i // 8, i % 8 * 4
                    if i >= 2:
                        pe.wait_ge(seg_taken, 16 * l + i - 1)
                    if i >= 10:
                        pe.wait_ge(row_exp_ready, 8 * l + i - 9)
                    for e in range(4):
                        mm = nc.tensor.matmul(bank[i % 2][:, e * P:(e + 1) * P],
                                              LOGA[:, t, h0 + e:h0 + e + 1].to_broadcast([P, P]), con("cum128"),
                                              start=True, stop=True)
                    mm.then_inc(seg_done, 1)

                def scan_out(i):
                    t, h0, m = i // 8, i % 8 * 4, i // 2
                    pe.wait_ge(mix_ready, 16 * l + i + 1)
                    if t == 1:
                        pe.wait_ge(cdec_ready, 8 * l + i - 7)
                    if i % 2 == 0 and m >= 2:
                        pe.wait_ge(y_taken, 8 * l + m - 1)
                    for e in range(4):
                        h = h0 + e
                        dst = bank[2 + m % 2][h % 2 * HD:h % 2 * HD + HD, h % 8 // 2 * P:(h % 8 // 2 + 1) * P]
                        mm = nc.tensor.matmul(dst, XDT[:, t, h * HD:(h + 1) * HD], MIX[:, i % 2, e * P:(e + 1) * P],
                                              start=True, stop=(t == 0))
                        if t == 1:
                            mm = nc.tensor.matmul(dst, STATE[:, h * HD:(h + 1) * HD], CDEC[:, i % 2, e * P:(e + 1) * P],
                                                  start=False, stop=True)
                    mm.then_inc(y_done, 1)

                decay_rows(0)
                decay_rows(1)
                for i in range(16):
                    scan_out(i)
                    if i + 2 < 16:
                        decay_rows(i + 2)
                    for p, at in enumerate(SCAN_SLOTS):
                        if at <= i <= at + 1:
                            j = L_CONV - SCAN_CONV + 1 + p
                            wide_half(w0 + j, Q_LAYERS + LQ_WIDE + j, rounds, j % 2, i - at)
                qss = lambda t, i: bank[6 + i // 8][:, 8 * t + i % 8:8 * t + i % 8 + 1]

                def group_sum(g):
                    if g >= 2:
                        pe.wait_ge(qkrms_ready, 2 * l + g - 1)
                    pe.wait_ge(ysq_ready, 4 * l + g + 1)
                    for e in range(4):
                        at = g % 2 * 1024 + e * S
                        mm = nc.tensor.matmul(bank[GROUP_BANKS[g]][:, 0:S], MEAN_G[:, :], SQ[:, at:at + S], start=(e == 0),
                                              stop=(e == 3))
                    mm.then_inc(yss_done, 1)

                def qk_spread(pr):
                    pe.wait_ge(qkr_ready, 2 * l + pr // 4 + 1)
                    if pr >= 2:
                        pe.wait_ge(qk_ready, 8 * l + pr - 1)
                    for e in range(2):
                        for t in range(2):
                            mm = spread_tokens(bank[2 + pr % 2][:, e * S + t * P:e * S + (t + 1) * P],
                                               QR[:, t, 2 * pr + e:2 * pr + e + 1])
                    mm.then_inc(qkb_done, 1)

                for j in range(L_ZS):
                    wide(w0 + L_CONV + j, Q_LAYERS + LQ_WIDE + L_CONV + j, rounds, j % 2)
                    if 1 <= j <= 4:
                        for pr in (2 * j - 2, 2 * j - 1):
                            pe.wait_ge(qksq_ready, 8 * l + pr + 1)
                            for e in range(2):
                                mm = squares_summed(QSQ[:, pr, e, :], 2 * pr + e, qss)
                        if j % 2 == 0:
                            mm.then_inc(qkss_done, 1)
                    if j % 2 == 1 and j >= 3:
                        group_sum((j - 3) // 2)
                    if 4 <= j:
                        qk_spread(2 * j - 8)
                        qk_spread(2 * j - 7)
                group_sum(3)

                pe.wait_ge(yrms_ready, 4 * l + 2)
                pe.wait_ge(qk_ready, 8 * l + 8)

                def late_wide(j, e):
                    wide_half(w0 + L_CONV + L_ZS + j, Q_LAYERS + LQ_WIDE + L_CONV + L_ZS + j, rounds, j % 2, e)

                for t in range(2):
                    tok = slice(t * P, (t + 1) * P)
                    if t == 1:
                        pe.wait_ge(o_copied, 4 * l + 2)
                        pe.wait_ge(wide_free, 2 + w0 + L_CONV + L_ZS + L_ZD)
                    def tokens_first():
                        if t == 1:
                            pe.wait_ge(st_ready, 6 * l + 4)
                        for m in range(4):
                            for e in range(4):
                                mm = nc.tensor.transpose(bank[m][:, e * P:(e + 1) * P], QKV[:, 8 + 4 * m + e, tok],
                                                         con("ident"))
                            mm.then_inc(kv_done, 1)

                    def head_products(b):
                        if b == 1:
                            pe.wait_ge(k_taken, 4 * l + 2 * t + 2)
                            pe.wait_ge(vb_ready, 4 * l + 2 * t + 2)
                        elif t == 0:
                            pe.wait_ge(yrms_ready, 4 * l + 4)
                            pe.wait_ge(wide_free, 2 + w0 + L_CONV + L_ZS)
                        rows_g, rows_b, kk, kq = [bank[i] for i in KK_BANKS[b]]
                        for e in range(4):
                            h, at = 4 * b + e, slice(e * P, (e + 1) * P)
                            q, k = QKV[:, h, tok], QKV[:, DN_HEADS + h, tok]
                            along = lambda column: column.to_broadcast([P, P])
                            nc.tensor.matmul(rows_g[:, at], along(LOGA[:, t, 32 + h:33 + h]), con("cum64"),
                                             start=True, stop=True)
                            nc.tensor.matmul(kk[:, at], k, k, start=True, stop=True)
                            nc.tensor.matmul(kq[:, at], k, q, start=True, stop=True)
                            mm = nc.tensor.matmul(rows_b[:, at], along(BETA[:, t, h:h + 1]), con("ident"), start=True,
                                                  stop=True)
                        mm.then_inc(kk_done, 1)

                    if t == 0:
                        tokens_first()
                        head_products(0)
                    else:
                        head_products(0)
                        tokens_first()
                    head_products(1)
                    for v in range(LEVELS):
                        k = (2 * l + t) * LEVELS + v
                        kc = (2 * l + t) * (LEVELS - 1) + v - 1
                        for b in range(2):
                            if v == 0:
                                pe.wait_ge(c0_ready, 4 * l + 2 * t + b + 1)
                                pe.wait_ge(grow_ready, 4 * l + 2 * t + 1)
                            else:
                                pe.wait_ge(cs_ready, 2 * kc + b + 1)
                                pe.wait_ge(inv_ready, 2 * k + b - 1)
                            if v == 1 and b == 1:
                                pe.wait_ge(aqk_ready, 4 * l + 2 * t + 1)
                            for e in range(4):
                                at = slice(512 * b + e * P, 512 * b + (e + 1) * P)
                                mm = nc.tensor.matmul(bank[b if v else 6 + b][:, e * P:(e + 1) * P], CS[:, at],
                                                      TI[:, at] if v else con("ident"), start=True, stop=True)
                            mm.then_inc(inv_u_done, 1)
                        late = late_panel(t, f"level{v}")
                        if late is not None:
                            if v == 1:
                                pe.wait_ge(aqk_ready, 4 * l + 2 * t + 2)
                            late_wide(late, 0)
                        if v == 1:
                            pe.wait_ge(grow_ready, 4 * l + 2 * t + 2)
                        for b in range(2 if v else 0):
                            pe.wait_ge(inv_u_copied, 2 * kc + b + 1)
                            for e in range(4):
                                at, to = slice(512 * b + e * P, 512 * b + (e + 1) * P), slice(e * P, (e + 1) * P)
                                if v < LEVELS - 1:
                                    nc.tensor.matmul(bank[2 + b][:, to], TT[:, at], UB[:, at], start=True, stop=True)
                                mm = nc.tensor.matmul(bank[6 + b][:, to], UB[:, at], TT[:, at], start=True, stop=True)
                            mm.then_inc(inv_v_done, 1)
                        if late is not None:
                            late_wide(late, 1)
                    for b in range(2):
                        pe.wait_ge(inv_ready, 2 * ((2 * l + t) * LEVELS + LEVELS - 1) + b + 1)
                        for e in range(4):
                            at = slice(512 * b + e * P, 512 * b + (e + 1) * P)
                            mm = nc.tensor.matmul(bank[b][:, e * P:(e + 1) * P], KBG[:, at], TT[:, at],
                                                  start=True, stop=True)
                        mm.then_inc(wt_done, 1)
                    pe.wait_ge(wt_copied, 4 * l + 2 * t + 2)
                    pe.wait_ge(qd_ready, 4 * l + 2 * t + 2)
                    for c in range(2):
                        cg, r = 2 * t + c, c * 64
                        rows = slice(r, r + 64)
                        if cg >= 1:
                            pe.wait_ge(st_ready, 6 * l + 2 * cg)
                        for b in range(2):
                            for e in range(4):
                                h = 4 * b + e
                                to = bank[2 + b][rows, e * P:(e + 1) * P]
                                at = slice(h * P, (h + 1) * P)
                                mm = nc.tensor.matmul(to, TT[:, h * P + r:h * P + r + 64], VB[:, at], start=True,
                                                      stop=(cg == 0))
                                if cg >= 1:
                                    mm = nc.tensor.matmul(to, WT[:, h * P + r:h * P + r + 64], ST[:, at], start=False,
                                                          stop=True)
                            mm.then_inc(vn_done, 1)
                        late = late_panel(t, f"chunk{c}")
                        if late is not None:
                            late_wide(late, 0)
                        pe.wait_ge(vn_copied, 8 * l + 2 * cg + 2)
                        if cg >= 1:
                            pe.wait_ge(o_copied, 4 * l + cg)
                        for h in range(DN_HEADS):
                            to = bank[6][:, h * 64:(h + 1) * 64]
                            if cg >= 1:
                                nc.tensor.matmul(to, ST[:, h * P:(h + 1) * P], QKV[:, h, t * P + r:t * P + r + 64],
                                                 start=True, stop=False)
                            mm = nc.tensor.matmul(to, VN[rows, h * P:(h + 1) * P],
                                                  AQK[rows, h * P + r:h * P + r + 64], start=(cg == 0), stop=True)
                        mm.then_inc(o_done, 1)
                        for b in range(2 if cg < 3 else 0):
                            for e in range(4):
                                at = slice(512 * b + e * P, 512 * b + (e + 1) * P)
                                mm = nc.tensor.matmul(bank[b][:, e * P:(e + 1) * P], KDEC[rows, at], VN[rows, at],
                                                      start=True, stop=True)
                            mm.then_inc(st_done, 1)
                        if late is not None:
                            late_wide(late, 1)
                oss = lambda t, i: bank[6][:, 8 * t + i:8 * t + i + 1]
                for j in range(LATE_GATES):
                    for e in range(2):
                        late_wide(L_ZD + L_GATES - LATE_GATES + j, e)
                    if j == 0:
                        for h in range(DN_HEADS):
                            pe.wait_ge(osq_ready, 4 * l + h // 2 + 1)
                            mm = squares_summed(SQ[:, h * S:(h + 1) * S], h, oss)
                        mm.then_inc(oss_done, 1)
                    if j == 1:
                        pe.wait_ge(or_ready, l + 1)
                        for h in range(DN_HEADS):
                            for t in range(2):
                                mm = spread_tokens(bank[O_BANKS[h // 2]][:, h % 2 * S + t * P:h % 2 * S + (t + 1) * P],
                                                   QR[:, t, h:h + 1])
                            if h % 2:
                                mm.then_inc(ob_done, 1)
                pe.wait_ge(branch_lo, 12 * l + 8)
                for c in range(4):
                    if c == 1:
                        pe.wait_ge(yd_ready, 4 * l + 4)
                    if c >= 2:
                        pe.wait_ge(merged_ready, 4 + 4 * l + c - 1)
                    for half in range(2):
                        src = both(panel(Q_LAYERS + LQ_PROJ + 3 * c + half, rounds), lambda x: tiles(x, KT))
                        for e in range(2):
                            for k in range(KT):
                                mm = product(bank[c % 2 * 2][:, e * S:(e + 1) * S],
                                             both(src, lambda x: x[:, k, e * P:(e + 1) * P]),
                                             both((YSH, YSL), lambda x: x[:, half * KT + k, :]),
                                             start=(half + e + k == 0), stop=(half == 1 and k == KT - 1),
                                             skip_group_check=True)
                        mm.then_inc(panel_used, 1)
                    if c == 0:
                        pe.wait_ge(branch_lo, 12 * l + 12)
                    src = both(panel(Q_LAYERS + LQ_PROJ + 3 * c + 2, rounds), lambda x: tiles(x, KT))
                    for e in range(2):
                        for k in range(KT):
                            mm = product(bank[c % 2 * 2 + 1][:, e * S:(e + 1) * S],
                                         both(src, lambda x: x[:, k, e * P:(e + 1) * P]),
                                         (YDH[:, k, :], YDL[:, k, :]), start=(k == 0), stop=(k == KT - 1))
                    mm.then_inc(panel_used, 1)
                to_residual(Q_LAYERS + LQ_WOUT, rounds, fill + 2, 4 + 3 * l, 6)
                norm(4 + 3 * l)
                ffn(2 + 2 * l, Q_LAYERS + LQ_FFN2, rounds, fill + 3)
            norm(2 + 3 * LAYERS)

        @block.scalar
        def _(act):
            act.sem_inc(wide_free, 2)
            act.wait_ge(pack1_loaded, 16)
            nc.scalar.activation(CACT[:, :], pk1("c", 0, 8), ACT.Silu).then_inc(c_ready, 1)

            def split(q, rounds=0):
                act.wait_ge(panel_loaded[q % RING], 16 * (q // RING + 1) + 16 * (ROUND // RING) * rounds)
                if q >= PARTS:
                    act.wait_ge(panel_used, q - PARTS + 1 + ROUND * rounds)
                nc.scalar.activation(HI[:, q % PARTS, :], ring[:, q % RING, :], ACT.Copy).then_inc(hi_ready, 1)

            def fill_high(f, counter, before):
                for k in range(KT // 2):
                    act.wait_ge(counter, before(k))
                    nc.scalar.activation(UH[:, 2 * k:2 * k + 2, :], U[:, 2 * k:2 * k + 2, :],
                                         ACT.Copy).then_inc(uh_ready, 1)

            def norm(n, fill, loaded=False, before=(), after=None):
                nc.scalar.activation(ROOT0[:, :], EPST[:, :], ACT.Sqrt)
                for k in range(KT // 2):
                    if k < len(before):
                        split(*before[k])
                    if loaded:
                        act.wait_ge(x_loaded, 16)
                    else:
                        act.wait_ge(residual_ready, KT // 2 * (n - 1) + k + 1)
                    nc.scalar.activation(tiles(SQ[:, k * 512:(k + 1) * 512], 2), H[:, 2 * k:2 * k + 2, :],
                                         ACT.Square).then_inc(squares_ready, 1)
                if after is not None:
                    split(*after)
                act.wait_ge(sumsq_ready, n + 1)
                for t in range(2):
                    root = nc.scalar.activation(NROOT[:, t:t + 1], bank[4 + t][:, 0:1], ACT.Sqrt, bias=EPST[:, :],
                                                scale=1.0 / D)
                root.then_inc(rms_ready, 1)
                if fill is not None:
                    fill_high(fill, u_ready, lambda k: KT * n + 2 * k + 2)

            def ffn(q0, rounds):
                def silu(q, rr, par):
                    act.wait_ge(panel_used, q + 1 + ROUND * rr)
                    nc.scalar.activation(SG[:, par, :], bank[4 + 2 * par][:, :], ACT.Silu).then_inc(gate_act_ready, 1)

                split(q0 + 2, rounds)
                split(q0 + 3, rounds)
                silu(q0 + 1, rounds, 0)
                split(q0 + 4, rounds)
                split(q0 + 5, rounds)
                silu(q0 + 3, rounds, 1)
                split(q0 + 6, rounds)
                with act.Fori(0, 4) as r:
                    for b in range(2):
                        split(q0 + 7 + 3 * b, rounds + r)
                        split(q0 + 8 + 3 * b, rounds + r)
                        silu(q0 + 6 + 3 * b, rounds + r, b)
                        split(q0 + 9 + 3 * b, rounds + r)
                split(q0 + 31, rounds)
                split(q0 + 32, rounds)
                silu(q0 + 30, rounds, 0)

            act.wait_ge(fills_done, 1)
            norm(0, None, loaded=True)
            act.wait_ge(nspread_done, 1)
            nc.scalar.activation(RSTD[:, 0:S], bank[6][:, 0:S], ACT.Copy).then_inc(rstd_copied, 1)
            split(0)
            split(1)
            fill_high(FILL_B1_NORM1, u_ready, lambda k: 2 * k + 2)
            proj2 = ARENA[:, 0:36 * S].rearrange("p (w n) -> p w n", w=B1_WIDE + B1_GATES)
            with act.Fori(0, B1_WIDE // ROUND) as r:
                for i in range(ROUND):
                    split(Q_WIDE1 + i + PARTS, r)
                    act.wait_ge(panel_used, Q_WIDE1 + ROUND * r + i + 1)
                    nc.scalar.activation(proj2[:, ROUND * r + i, :], bank[4 + i % 2][:, :], ACT.Copy).then_inc(wide_free, 1)
            def head_root(i):
                act.wait_ge(hss_ready, (NA_PAIRS, HEAD_PAIRS)[i])
                cols = slice(0, 4 * NA_PAIRS) if i == 0 else slice(4 * NA_PAIRS, 4 * HEAD_PAIRS)
                nc.scalar.activation(HROOT[:, :, cols], tiles(bank[i][:, 0:8 * HEAD_PAIRS], 2)[:, :, cols], ACT.Sqrt,
                                     bias=EPST[:, :], scale=1.0 / HD).then_inc(hrms_ready, 1)

            def head_squares(pr):
                if pr >= 4:
                    act.wait_ge(hss_ready, pr - 3)
                nc.scalar.activation(tiles(SQ[:, pr % 4 * 512:pr % 4 * 512 + 512], 2), PROJ[:, 2 * pr:2 * pr + 2, :],
                                     ACT.Square).then_inc(hsq_ready, 1)

            act.wait_ge(wide_free, 2 + B1_WIDE)
            for c in range(B1_V):
                split(Q_V + c + PARTS)
                act.wait_ge(panel_used, Q_V + c + 1)
                nc.scalar.activation(VT[:, :, c * S:(c + 1) * S], tiles(bank[4 + c % 2][:, :], 2),
                                     ACT.Copy).then_inc(wide_free, 1)
                head_squares(2 * c)
                head_squares(2 * c + 1)
                if c == 3:
                    head_root(0)
            for g in range(B1_GATES):
                split(Q_GATES1 + g + PARTS)
                act.wait_ge(panel_used, Q_GATES1 + g + 1)
                for e in range(2):
                    i = 2 * (B1_WIDE - HEAD_PAIRS + g) + e
                    gate = nc.scalar.activation(PROJ[:, GATE + i, :], bank[4 + (B1_V + g) % 2][:, e * S:(e + 1) * S],
                                                ACT.Sigmoid, bias=pk1("b_gate", i))
                gate.then_inc(wide_free, 1)
                if g == 1:
                    head_root(1)
            for i in range(2 * (B1_WIDE - HEAD_PAIRS)):
                gate = nc.scalar.activation(PROJ[:, GATE + i, :], PROJ[:, GATE + i, :], ACT.Sigmoid, bias=pk1("b_gate", i))
            gate.then_inc(gates_ready, 1)

            def keys(u):
                return S if u < NA_UNITS else DIL_GROUPS * S

            def softmax_exp(u):
                act.wait_ge(nmax_ready, u + 1)
                nc.scalar.activation(SC[:, u % 2, 0:keys(u)], SC[:, u % 2, 0:keys(u)], ACT.Exp,
                                     bias=NMAX[:, UNITS + u:UNITS + u + 1],
                                     accum_out=DEN[:, u:u + 1]).then_inc(probs_ready, 1)

            def turned(u):
                act.wait_ge(pt_done, u + 1)
                if u >= 2:
                    act.wait_ge(pv_done, u - 1)
                copy = nc.scalar.activation(PT[:, u % 2, 0:min(512, keys(u))], bank[4][:, 0:min(512, keys(u))], ACT.Copy)
                if keys(u) > 512:
                    copy = nc.scalar.activation(PT[:, u % 2, 512:keys(u)], bank[5][:, 0:keys(u) - 512], ACT.Copy)
                copy.then_inc(pt_copied, 1)

            softmax_exp(0)
            for u in range(UNITS):
                if u + 1 < UNITS:
                    softmax_exp(u + 1)
                turned(u)
            act.wait_ge(ot_done, 1)
            for i in range(3):
                nc.scalar.activation(OTH[:, 2 * i:2 * i + 2, :], tiles(bank[i][:, :], 2), ACT.Copy).then_inc(oth_ready, 1)
            for i in range(B1_PROJ - 1):
                split(Q_PROJ1 + i + PARTS)
            fill_high(FILL_B1_MERGE, merged_ready, lambda k: k + 1)
            split(Q_PROJ1 + B1_PROJ - 1 + PARTS)
            norm(1, FILL_B1_NORM2, before=[(Q_WO + i + PARTS,) for i in range(B1_WO - 1)], after=(Q_FFN0 + 1,))
            ffn(Q_FFN0, 0)

            conv2 = ARENA[:, 0:CONV_TILES * S].rearrange("p (w n) -> p w n", w=L_CONV)
            with act.Fori(0, LAYERS) as l:
                used0 = Q_LAYERS + L_PANELS * l
                rounds = L_ROUNDS * l
                fill = FILL_LAYER + 4 * l

                def ahead(q):
                    split(Q_LAYERS + q + PARTS, rounds)

                norm(2 + 3 * l, fill, before=[(Q_LAYERS, rounds)], after=(Q_LAYERS + 1, rounds))
                ffn(Q_LAYERS + LQ_FFN1, rounds)
                norm(3 + 3 * l, fill + 1, before=[(Q_LAYERS + LQ_WIDE, rounds)], after=(Q_LAYERS + LQ_WIDE + 1, rounds))
                act.wait_ge(small_abs, l + 1)
                nc.scalar.activation(SMX[:, 2, :], SMX[:, 1, :], ACT.Exp).then_inc(small_exp, 1)
                nc.scalar.activation(SMX[:, 7, 0:SP_COLS], pk2("a_log", 0, SP_COLS), ACT.Exp).then_inc(aneg_ready, 1)
                act.wait_ge(small_w, l + 1)
                nc.scalar.activation(SMX[:, 4, :], SMX[:, 3, :], ACT.Ln).then_inc(small_ln, 1)
                nc.scalar.activation(BETA[:, :, :], tiles(SMX[:, 0, :], 2)[:, :, SP_COLS:SMALL],
                                     ACT.Sigmoid).then_inc(beta_ready, 1)
                def conv_silu(j):
                    act.wait_ge(conv_step, 192 * l + 8 * j + 24)
                    nc.scalar.activation(conv2[:, j, :], conv2[:, j, :], ACT.Silu).then_inc(conv_ready, 1)

                def conv_in(j, b):
                    act.wait_ge(panel_used, used0 + LQ_WIDE + j + 1)
                    act.wait_ge(conv_step, 192 * l + 8 * j + 8)
                    nc.scalar.activation(XPAD[:, b, :, 3:S + 3], tiles(bank[4 + b][:, :], 2),
                                         ACT.Copy).then_inc(wide_free, 1)

                for i in range(ROUND):
                    ahead(LQ_WIDE + i)
                    conv_in(i, i % 2)
                    if i >= 1:
                        conv_silu(i - 1)
                with act.Fori(1, (L_CONV - SCAN_CONV) // ROUND) as r:
                    for i in range(ROUND):
                        split(Q_LAYERS + LQ_WIDE + i + PARTS, rounds + r)
                        conv_in(ROUND * r + i, i % 2)
                        conv_silu(ROUND * r + i - 1)
                conv_silu(L_CONV - SCAN_CONV - 1)
                act.wait_ge(cum_copied, l + 1)
                nc.scalar.activation(ECUM[:, 0:96], ECUM[:, 0:96], ACT.Exp).then_inc(ecum_ready, 1)
                act.wait_ge(btok_done, l + 1)
                nc.scalar.activation(BTOK[:, :], bank[7][:, :], ACT.Copy).then_inc(btok_copied, 1)
                ahead(LQ_WIDE + L_CONV - SCAN_CONV)
                conv_in(L_CONV - SCAN_CONV, 0)
                for g in range(GROUPS):
                    act.wait_ge(state_done, 4 * l + g + 1)
                    nc.scalar.activation(STATE[:, g * 512:(g + 1) * 512], bank[g][:, :], ACT.Copy).then_inc(state_copied, 1)
                for i in range(16):
                    if i >= 8:
                        act.wait_ge(seg_taken, 16 * l + i + 1)
                        if i >= 10:
                            act.wait_ge(y_done, 16 * l + i - 1)
                        nc.scalar.activation(CDEC[:, i % 2, :], bank[i % 2][:, :], ACT.Exp).then_inc(row_exp_ready, 1)
                    act.wait_ge(seg_ready, 16 * l + i + 1)
                    nc.scalar.activation(SEG[:, i % 2, :], SEG[:, i % 2, :], ACT.Exp).then_inc(decay_ready, 1)
                    if i - 2 in SCAN_SLOTS:
                        j = L_CONV - SCAN_CONV + 1 + SCAN_SLOTS.index(i - 2)
                        ahead(LQ_WIDE + j)
                        conv_in(j, j % 2)
                def group_rms(g):
                    act.wait_ge(yss_done, 4 * l + g + 1)
                    nc.scalar.activation(GRMS[:, g, :], bank[GROUP_BANKS[g]][:, 0:S], ACT.Sqrt,
                                         bias=EPST[:, :]).then_inc(yrms_ready, 1)

                def group_squares(g):
                    act.wait_ge(yg_ready, 8 * l + 2 * g + 2)
                    if g >= 2:
                        act.wait_ge(yss_done, 4 * l + g - 1)
                    nc.scalar.activation(tiles(SQ[:, g % 2 * 1024:g % 2 * 1024 + 1024], 4),
                                         CONV[:, 4 * g:4 * g + 4, :], ACT.Square).then_inc(ysq_ready, 1)

                def qk_root(i):
                    act.wait_ge(qkss_done, 2 * l + i + 1)
                    nc.scalar.activation(QROOT[:, :, 8 * i:8 * i + 8], tiles(bank[6 + i][:, 0:16], 2),
                                         ACT.Sqrt, bias=EPST[:, :]).then_inc(qkrms_ready, 1)

                act.wait_ge(y_taken, 8 * l + 8)
                for j in range(L_ZS):
                    ahead(LQ_WIDE + L_CONV + j)
                    act.wait_ge(panel_used, used0 + LQ_WIDE + L_CONV + j + 1)
                    if j >= 2:
                        act.wait_ge(yg_ready, 8 * l + j - 1)
                    nc.scalar.activation(tiles(ZT[:, j % 2, :], 2), tiles(bank[4 + j % 2][:, :], 2),
                                         ACT.Silu).then_inc(wide_free, 1)
                    if j < SCAN_CONV // 2:
                        for i in range(2):
                            conv_silu(L_CONV - SCAN_CONV + 2 * j + i)
                    if j < 4:
                        for pr in (2 * j, 2 * j + 1):
                            nc.scalar.activation(QSQ[:, pr, :, :], QKV[:, 2 * pr:2 * pr + 2, :],
                                                 ACT.Square).then_inc(qksq_ready, 1)
                    if j % 2 == 0 and j >= 2:
                        group_squares(j // 2 - 1)
                    if j in (3, 5):
                        qk_root((j - 3) // 2)
                    if j in (5, 7):
                        group_rms((j - 5) // 2)
                group_squares(3)
                group_rms(2)
                group_rms(3)

                def late_gate(j):
                    q = LQ_WIDE + L_CONV + L_ZS + j
                    ahead(q)
                    act.wait_ge(panel_used, used0 + q + 1)
                    to, func = (ZD[:, 2 * j:2 * j + 2, :], ACT.Silu) if j < L_ZD else \
                        (GT[:, 2 * (j - L_ZD):2 * (j - L_ZD) + 2, :], ACT.Sigmoid)
                    nc.scalar.activation(to, tiles(bank[4 + j % 2][:, :], 2), func).then_inc(wide_free, 1)

                for t in range(2):
                    nc.scalar.activation(ROOT0[:, :], EPST[:, :], ACT.Exp)

                    def values_first():
                        for b in range(2):
                            act.wait_ge(kv_done, 8 * l + 4 * t + 3 + b)
                            for e in range(4):
                                h = 4 * b + e
                                ins = nc.scalar.activation(VB[:, h * P:(h + 1) * P], bank[2 + b][:, e * P:(e + 1) * P],
                                                           ACT.Copy, scale=BETA[:, t, h:h + 1])
                            ins.then_inc(vb_ready, 1)

                    for b in range(2):
                        n = 4 * l + 2 * t + b
                        if b == t:
                            values_first()
                        act.wait_ge(gseg_ready, n + 1)
                        nc.scalar.activation(DEC[:, 512 * b:512 * b + 512], DCY[:, 512 * b:512 * b + 512],
                                             ACT.Exp).then_inc(gdec_ready, 1)
                        nc.scalar.activation(GROW[b][:, :], bank[KK_BANKS[b][0]][:, :], ACT.Exp).then_inc(grow_ready, 1)
                    for v in range(1, LEVELS):
                        k = (2 * l + t) * LEVELS + v
                        for b in range(2):
                            act.wait_ge(inv_u_done, 2 * k + b + 1)
                            nc.scalar.activation(UB[:, 512 * b:512 * b + 512], bank[b][:, :],
                                                 ACT.Copy).then_inc(inv_u_copied, 1)
                        late = late_panel(t, f"level{v - 1}")
                        if late is not None:
                            late_gate(late)
                    for b in range(2):
                        act.wait_ge(wt_done, 4 * l + 2 * t + b + 1)
                        nc.scalar.activation(WT[:, 512 * b:512 * b + 512], bank[b][:, :], ACT.Copy,
                                             scale=-1.0).then_inc(wt_copied, 1)
                    for c in range(2):
                        cg, rows = 2 * t + c, slice(64 * c, 64 * c + 64)
                        for b in range(2):
                            act.wait_ge(vn_done, 8 * l + 2 * cg + b + 1)
                            nc.scalar.activation(VN[rows, 512 * b:512 * b + 512], bank[2 + b][rows, :],
                                                 ACT.Copy).then_inc(vn_copied, 1)
                        if c == 1:
                            late_gate(late_panel(t, "chunk0"))
                    late_gate(late_panel(t, "chunk1"))
                act.wait_ge(o_copied, 4 * l + 4)
                for pr in range(4):
                    nc.scalar.activation(tiles(SQ[:, pr * 512:pr * 512 + 512], 2), QKV[:, 2 * pr:2 * pr + 2, :],
                                         ACT.Square).then_inc(osq_ready, 1)
                for j in range(8):
                    act.wait_ge(ys_ready, 4 * l + j // 2 + 1)
                    nc.scalar.activation(YSH[:, 2 * j:2 * j + 2, :], CONV[:, 2 * j:2 * j + 2, :],
                                         ACT.Copy).then_inc(branch_hi, 1)
                    if j == 3:
                        late_gate(L_ZD + L_GATES - LATE_GATES)
                        act.wait_ge(oss_done, l + 1)
                        nc.scalar.activation(QROOT[:, :, 0:8], tiles(bank[6][:, 0:16], 2), ACT.Sqrt, bias=EPST[:, :],
                                             scale=1.0 / P).then_inc(orms_ready, 1)
                for j in range(1, LATE_GATES):
                    late_gate(L_ZD + L_GATES - LATE_GATES + j)
                for j in range(4):
                    act.wait_ge(yd_ready, 4 * l + j + 1)
                    nc.scalar.activation(YDH[:, 2 * j:2 * j + 2, :], QKV[:, 2 * j:2 * j + 2, :],
                                         ACT.Copy).then_inc(branch_hi, 1)
                def merged_high(c):
                    act.wait_ge(merged_ready, 4 + 4 * l + c + 1)
                    nc.scalar.activation(UH[:, 2 * c:2 * c + 2, :], U[:, 2 * c:2 * c + 2, :],
                                         ACT.Copy).then_inc(uh_ready, 1)

                for j in range(L_PROJ - 1):
                    ahead(LQ_PROJ + j)
                    if j % 3 == 2 and j >= 5:
                        merged_high((j - 5) // 3)
                merged_high(2)
                merged_high(3)
                ahead(LQ_PROJ + L_PROJ - 1)
                norm(4 + 3 * l, fill + 3, before=[(Q_LAYERS + LQ_WOUT + j + PARTS, rounds) for j in range(L_WOUT - 1)],
                     after=(Q_LAYERS + LQ_FFN2 + 1, rounds))
                ffn(Q_LAYERS + LQ_FFN2, rounds)
            norm(2 + 3 * LAYERS, None)

        @block.vector
        def _(dve):
            base, count = [0], [0]

            def step(ins):
                ins.then_inc(dve_done, 1)
                count[0] += 1
                return count[0]

            def need(number):
                dve.wait_ge(dve_done, base[0] + number)

            def pad(total):
                assert count[0] <= total, count
                need(count[0])
                dve.sem_inc(dve_done, total - count[0])
                count[0] = 0

            nc.vector.memset(MEAN_G[:, :], 1.0 / 512)
            nc.vector.memset(ONES[:, :], 1.0)
            nc.vector.memset(XPAD[:, :, :, :], 0.0)
            nc.vector.memset(EPST[:, :], EPS).then_inc(fills_done, 1)
            dve.sem_inc(conv_step, 16)

            def split(q, rounds=0):
                dve.wait_ge(hi_ready, q + 1 + ROUND * rounds)
                nc.vector.tensor_tensor(LO[:, q % PARTS, :], ring[:, q % RING, :], HI[:, q % PARTS, :].bitcast(F32),
                                        ALU.subtract).then_inc(lo_ready, 1)

            def fill_low(f, k):
                dve.wait_ge(uh_ready, 4 * f + k + 1)
                at = slice(2 * k, 2 * k + 2)
                nc.vector.tensor_tensor(UL[:, at, :], U[:, at, :], UH[:, at, :].bitcast(F32),
                                        ALU.subtract).then_inc(ul_ready, 1)

            def reciprocal_rms(n):
                dve.wait_ge(rms_ready, n + 1)
                nc.vector.reciprocal(NRSTD[:, :], NROOT[:, :]).then_inc(nrstd_ready, 1)

            def norm(n, fill, gain, shift=None, panel=None):
                first = shift is not None and n == 0
                if first:
                    dve.wait_ge(xn_ready, 1)
                else:
                    dve.wait_ge(squares_ready, KT // 2 * n + 4)
                    nc.vector.tensor_tensor(SQ[:, 1024:1536], SQ[:, 1024:1536], SQ[:, 1536:2048],
                                            ALU.add).then_inc(squares_added, 1)
                    if panel is not None:
                        split(*panel)
                    reciprocal_rms(n)
                    dve.wait_ge(nspread_done, n + 1)
                for k in range(KT):
                    if shift is None:
                        nc.vector.scalar_tensor_tensor(U[:, k, :], H[:, k, :], gain[:, k:k + 1], bank[6][:, 0:S],
                                                       ALU.mult, ALU.mult).then_inc(u_ready, 1)
                    else:
                        if not first:
                            need(step(nc.vector.tensor_tensor(U[:, k, :], H[:, k, :], bank[6][:, 0:S], ALU.mult)))
                        nc.vector.tensor_scalar(U[:, k, :], U[:, k, :], gain[:, k:k + 1], shift[:, k:k + 1], ALU.mult,
                                                ALU.add).then_inc(u_ready, 1)
                    if fill is not None and k % 2 and k > 1:
                        fill_low(fill, k // 2 - 1)
                if fill is not None:
                    fill_low(fill, KT // 2 - 1)

            def pool_split(q, rounds=0):
                dve.wait_ge(lo_ready, q + 1 + ROUND * rounds)

            def ffn_hidden(f, q0, rounds):
                def hidden(i, par):
                    dve.wait_ge(gate_act_ready, f * HID_PAIRS + i + 1)
                    n = f * HID_PAIRS + i + 1
                    nc.vector.tensor_tensor(HID[:, par, :], SG[:, par, :], bank[5 + 2 * par][:, :],
                                            ALU.mult).then_inc(hid_product, 1)
                    dve.wait_ge(hid_product, n)
                    nc.vector.tensor_copy(HIDH[:, par, :], HID[:, par, :]).then_inc(hidh_ready, 1)
                    dve.wait_ge(hidh_ready, n)
                    nc.vector.tensor_tensor(HIDL[:, par, :], HID[:, par, :], HIDH[:, par, :].bitcast(F32),
                                            ALU.subtract).then_inc(hidden_ready, 1)

                split(q0 + 2, rounds)
                split(q0 + 3, rounds)
                hidden(0, 0)
                split(q0 + 4, rounds)
                split(q0 + 5, rounds)
                hidden(1, 1)
                split(q0 + 6, rounds)
                with dve.Fori(0, 4) as r:
                    for b in range(2):
                        split(q0 + 7 + 3 * b, rounds + r)
                        split(q0 + 8 + 3 * b, rounds + r)
                        hidden(2 + 2 * r + b, b)
                        split(q0 + 9 + 3 * b, rounds + r)
                split(q0 + 31, rounds)
                split(q0 + 32, rounds)
                hidden(10, 0)

            def ffn_out(j, f, panels):
                return (down_done, 3 * f + j + 1) if j < 3 else (panel_used, panels)

            def residual(j, src, scale):
                if isinstance(scale, float):
                    nc.vector.scalar_tensor_tensor(H[:, 2 * j:2 * j + 2, :], tiles(src, 2), scale, H[:, 2 * j:2 * j + 2, :],
                                                   ALU.mult, ALU.add).then_inc(residual_ready, 1)
                    return
                for e in range(2):
                    ins = nc.vector.scalar_tensor_tensor(H[:, 2 * j + e, :], src[:, e * S:(e + 1) * S],
                                                         scale[:, 2 * j + e:2 * j + e + 1], H[:, 2 * j + e, :],
                                                         ALU.mult, ALU.add)
                ins.then_inc(residual_ready, 1)

            dve.wait_ge(pack1_loaded, 16)
            dve.wait_ge(c_ready, 1)
            for i in range(0, ADA_FIRST, 2):
                if i == 4:
                    reciprocal_rms(0)
                for e in range(2):
                    dve.wait_ge(ada1_loaded[i + e], 16)
                for k in range(KT):
                    for e in range(2):
                        out, src, c = ADA_SUM[:, i + e, :], tiles(ADA1[:, i + e, :], KT), CACT[:, k:k + 1]
                        if k == 0:
                            ins = nc.vector.tensor_scalar(out, src[:, k, :], c, None, ALU.mult)
                        else:
                            dve.wait_ge(ada1_step, KT * i + 2 * k + e - 1)
                            ins = nc.vector.scalar_tensor_tensor(out, src[:, k, :], c, out, ALU.mult, ALU.add)
                        ins.then_inc(ada1_step, 1)
            split(0)
            shift1, scale1, gate1, shift2, scale2, gate2 = [MOD[:, 8 * i:8 * i + 8] for i in range(6)]
            dve.wait_ge(ada_done, 1)
            nc.vector.tensor_tensor(MOD[:, 0:2 * ADA_FIRST], bank[7][:, 0:2 * ADA_FIRST], pk1("b_ada", 0, 2 * ADA_FIRST),
                                    ALU.add).then_inc(ada_copied, 1)
            dve.wait_ge(ada_copied, 1)
            step(nc.vector.scalar_tensor_tensor(GS[:, 0:8], scale1, 1.0, pk1("g1", 0, 8), ALU.add, ALU.mult))
            step(nc.vector.tensor_scalar(GS[:, 16:17], pk1("g_qa"), HD ** -0.5, None, ALU.mult))
            need(step(nc.vector.tensor_scalar(GS[:, 17:18], pk1("g_qb"), HD ** -0.5, None, ALU.mult)))
            norm(0, FILL_B1_NORM1, GS[:, 0:8], shift1)
            split(1)
            with dve.Fori(0, B1_WIDE // ROUND) as r:
                for i in range(ROUND):
                    split(Q_WIDE1 + i + PARTS, r)
            def head_reciprocal(i):
                dve.wait_ge(hrms_ready, i + 1)
                cols = slice(0, 4 * NA_PAIRS) if i == 0 else slice(4 * NA_PAIRS, 4 * HEAD_PAIRS)
                nc.vector.reciprocal(HRSTD[:, :, cols], HROOT[:, :, cols]).then_inc(hrstd_ready, 1)

            gains = [GS[:, 16:17]] * 2 + [pk1("g_ka")] * 2 + [GS[:, 17:18]] * 3 + [pk1("g_kb")] * 3

            def head_norm(pr):
                dve.wait_ge(hspread_done, pr + 1)
                x = PROJ[:, 2 * pr:2 * pr + 2, :]
                nc.vector.scalar_tensor_tensor(x, x, gains[pr], tiles(bank[2 + pr % 2][:, :], 2), ALU.mult,
                                               ALU.mult).then_inc(hnorm_ready, 1)

            def rotate(pr):
                x = PROJ[:, 2 * pr:2 * pr + 2, :]
                dve.wait_ge(rope_done, pr - NA_PAIRS + 1)
                need(step(nc.vector.tensor_tensor(tiles(SQ[:, pr % 4 * 512:pr % 4 * 512 + 512], 2), tiles(bank[6 + pr % 2][:, :], 2),
                                                  each(rop("sin"), 2), ALU.mult)))
                need(step(nc.vector.tensor_tensor(x, x, each(rop("cos"), 2), ALU.mult)))
                nc.vector.tensor_tensor(x, x, tiles(SQ[:, pr % 4 * 512:pr % 4 * 512 + 512], 2), ALU.add).then_inc(heads_ready, 1)

            for c in range(B1_V):
                split(Q_V + c + PARTS)
            head_reciprocal(0)

            dve.wait_ge(ropes_loaded, 16)
            for g in range(B1_GATES):
                split(Q_GATES1 + g + PARTS)
                if g <= 4:
                    head_norm(2 * g)
                    head_norm(2 * g + 1)
                if g == 1:
                    head_reciprocal(1)
                if 3 <= g:
                    rotate(2 * g - 2)
                    rotate(2 * g - 1)

            rest = slice(2 * ADA_FIRST, 2 * ADA_PANELS)
            dve.wait_ge(ada_done, 2)
            nc.vector.tensor_tensor(MOD[:, rest], bank[3][:, 0:2 * (ADA_PANELS - ADA_FIRST)],
                                    pk1("b_ada", 2 * ADA_FIRST, 2 * (ADA_PANELS - ADA_FIRST)), ALU.add).then_inc(ada_copied, 1)
            dve.wait_ge(ada_copied, 2)
            step(nc.vector.scalar_tensor_tensor(GS[:, 8:16], scale2, 1.0, pk1("g2", 0, 8), ALU.add, ALU.mult))
            def score(u):
                t = u % 2
                dve.wait_ge(scores_done, u + 1)
                if u in (0, NA_UNITS // 2):
                    dve.wait_ge(bias_loaded[2 * u // NA_UNITS], 16)
                if u >= 2:
                    dve.wait_ge(pt_done, u - 1)
                if u < NA_UNITS:
                    nc.vector.tensor_tensor(SC[:, u % 2, 0:S], bank[u % 2 * 2][:, 0:S], BIAS[:, u, :],
                                            ALU.add).then_inc(scored, 1)
                    n = S
                else:
                    masks = tiles(rop("dil"), 2 * DIL_GROUPS)
                    nc.vector.tensor_tensor(tiles(SC[:, u % 2, 0:512], 2), tiles(bank[u % 2 * 2][:, :], 2),
                                            masks[:, 3 * t:3 * t + 2, :], ALU.add)
                    nc.vector.tensor_tensor(SC[:, u % 2, 512:768], bank[u % 2 * 2 + 1][:, 0:S], masks[:, 3 * t + 2, :],
                                            ALU.add).then_inc(scored, 1)
                    n = 768
                dve.wait_ge(scored, u + 1)
                need(step(nc.vector.tensor_reduce(NMAX[:, u:u + 1], SC[:, u % 2, 0:n], AX.X, ALU.max)))
                nc.vector.tensor_scalar(NMAX[:, UNITS + u:UNITS + u + 1], NMAX[:, u:u + 1], -1.0, None,
                                        ALU.mult).then_inc(nmax_ready, 1)

            def outputs(u0, units, at):
                dve.wait_ge(pv_done, u0 + units)
                need(step(nc.vector.reciprocal(RDEN[:, u0:u0 + units], DEN[:, u0:u0 + units])))
                heads = units // 2
                for t in range(2):
                    nc.vector.tensor_tensor(OTOK[:, t, at:at + heads * HD].rearrange("p (h n) -> p h n", h=heads),
                                            bank[6 + t][:, 0:heads * HD].rearrange("p (h n) -> p h n", h=heads),
                                            spread(RDEN[:, u0 + t:u0 + units:2], HD), ALU.mult).then_inc(otok_ready, 1)

            for u in range(UNITS):
                score(u)
                if u == NA_UNITS + 1:
                    outputs(0, NA_UNITS, 0)
            outputs(NA_UNITS, DIL_UNITS, 512)

            def merge_first(c, bank_a, gate_a, ta):
                nc.vector.tensor_tensor(tiles(ta, 2), tiles(bank_a[:, :], 2), gate_a[:, 2 * c:2 * c + 2, :],
                                        ALU.mult).then_inc(gated_a, 1)

            def merge(c, m0, bank_b, gate_b, ta):
                u = U[:, 2 * c:2 * c + 2, :]
                need(step(nc.vector.tensor_tensor(u, tiles(bank_b[:, :], 2), gate_b[:, 2 * c:2 * c + 2, :], ALU.mult)))
                dve.wait_ge(gated_a, m0 + c + 1)
                nc.vector.tensor_tensor(u, u, tiles(ta, 2), ALU.add).then_inc(merged_ready, 1)

            for i in range(3):
                dve.wait_ge(oth_ready, i + 1)
                nc.vector.tensor_tensor(OTL[:, 2 * i:2 * i + 2, :], tiles(bank[i][:, :], 2),
                                        OTH[:, 2 * i:2 * i + 2, :].bitcast(F32), ALU.subtract).then_inc(otl_ready, 1)
            dve.wait_ge(gates_ready, 1)
            split(Q_PROJ1 + PARTS)
            gate_a, gate_b = PROJ[:, GATE:GATE + 8, :], PROJ[:, GATE + 8:GATE + 16, :]
            for c in range(4):
                dve.wait_ge(panel_used, Q_PROJ1 + c // 2 + 1)
                merge_first(c, bank[c], gate_a, MTMP[:, c, :])
            split(Q_PROJ1 + 1 + PARTS)
            for c in range(4):
                if c < 3:
                    dve.wait_ge(proj_done, c + 1)
                else:
                    dve.wait_ge(panel_used, Q_PROJ1 + B1_PROJ)
                merge(c, 0, bank[4 + c], gate_b, MTMP[:, c, :])
                if c:
                    fill_low(FILL_B1_MERGE, c - 1)
            fill_low(FILL_B1_MERGE, 3)
            split(Q_PROJ1 + 2 + PARTS)
            for j in range(B1_WO):
                dve.wait_ge(panel_used, Q_WO + j + 1)
                residual(j, bank[j % 2][:, :], gate1)
                if j < B1_WO - 1:
                    split(Q_WO + j + PARTS)
            dve.wait_ge(residual_ready, 4)
            norm(1, FILL_B1_NORM2, GS[:, 8:16], shift2)
            pool_split(Q_FFN0 + 1)
            ffn_hidden(0, Q_FFN0, 0)
            for j in range(4):
                dve.wait_ge(*ffn_out(j, 0, Q_LAYERS))
                residual(j, bank[j][:, :], gate2)
            dve.wait_ge(residual_ready, 8)
            pad(DVE_B1)

            with dve.Fori(0, LAYERS) as l:
                base[0] = DVE_B1 + DVE_LAYER * l
                used0 = Q_LAYERS + L_PANELS * l
                dve.wait_ge(pack2_loaded, 16 * l + 16)
                rounds = L_ROUNDS * l
                fill = FILL_LAYER + 4 * l

                def ahead(q):
                    split(Q_LAYERS + q + PARTS, rounds)

                norm(2 + 3 * l, fill, pk2("ffn1", 0, 8), panel=(Q_LAYERS, rounds))
                pool_split(Q_LAYERS + 1, rounds)
                ffn_hidden(1 + 2 * l, Q_LAYERS + LQ_FFN1, rounds)
                for j in range(4):
                    dve.wait_ge(*ffn_out(j, 1 + 2 * l, used0 + LQ_WIDE))
                    residual(j, bank[j][:, :], 0.5)
                dve.wait_ge(residual_ready, 4 * (3 + 3 * l))
                norm(3 + 3 * l, fill + 1, pk2("mix", 0, 8), panel=(Q_LAYERS + LQ_WIDE, rounds))
                pool_split(Q_LAYERS + LQ_WIDE + 1, rounds)

                x, e, w, ln, d, m, r_ = [SMX[:, i, :] for i in (0, 2, 3, 4, 5, 6, 1)]
                dve.wait_ge(small_done, l + 1)
                nc.vector.tensor_tensor(tiles(x, 2), tiles(bank[7][:, 0:2 * SMALL], 2), each(pk2("small_b", 0, SMALL), 2),
                                        ALU.add).then_inc(small_x, 1)
                dve.wait_ge(small_x, l + 1)
                nc.vector.scalar_tensor_tensor(SMX[:, 1, :], x, -1.0, x, ALU.mult, ALU.min).then_inc(small_abs, 1)
                dve.wait_ge(small_exp, l + 1)
                nc.vector.tensor_scalar(w, e, 1.0, None, ALU.add).then_inc(small_w, 1)
                dve.wait_ge(small_w, l + 1)
                need(step(nc.vector.tensor_scalar(d, w, -1.0, None, ALU.add)))
                need(step(nc.vector.tensor_scalar(m, d, 0.0, None, ALU.is_equal)))
                need(step(nc.vector.tensor_tensor(d, d, m, ALU.add)))
                need(step(nc.vector.reciprocal(r_, d)))
                need(step(nc.vector.tensor_tensor(r_, r_, e, ALU.mult)))
                dve.wait_ge(small_ln, l + 1)
                need(step(nc.vector.tensor_tensor(ln, ln, m, ALU.add)))
                need(step(nc.vector.tensor_tensor(ln, ln, r_, ALU.mult)))
                need(step(nc.vector.scalar_tensor_tensor(SPL[:, :, :], tiles(x, 2)[:, :, 0:SP_COLS], 0.0,
                                                         tiles(ln, 2)[:, :, 0:SP_COLS], ALU.max, ALU.add)))
                dve.wait_ge(aneg_ready, l + 1)
                nc.vector.scalar_tensor_tensor(LOGA[:, :, :], SPL[:, :, :], -1.0, each(SMX[:, 7, 0:SP_COLS], 2),
                                               ALU.mult, ALU.mult).then_inc(loga_ready, 1)

                w3 = pk2("conv_w", 0, 4 * CONV_TILES).rearrange("p (j n) -> p j n", n=8)
                b3 = pk2("conv_b", 0, CONV_TILES).rearrange("p (j n) -> p j n", n=2)
                conv_out = ARENA[:, 0:CONV_TILES * S].rearrange("p (w n) -> p w n", w=L_CONV)

                def convolve(j, b):
                    steps = 16 + 192 * l + 8 * j
                    dve.wait_ge(wide_free, WIDE0 + L_WIDE * l + j + 3)
                    for tap in (3, 2, 1, 0):
                        for e2 in range(2):
                            acc, src = conv_out[:, j, e2 * S:(e2 + 1) * S], XPAD[:, b, e2, tap:tap + S]
                            wt = w3[:, j, 4 * e2 + tap:4 * e2 + tap + 1]
                            if tap == 3:
                                ins = nc.vector.tensor_scalar(acc, src, wt, b3[:, j, e2:e2 + 1], ALU.mult, ALU.add)
                            else:
                                dve.wait_ge(conv_step, steps + 2 * (3 - tap) + e2 - 1)
                                ins = nc.vector.scalar_tensor_tensor(acc, src, wt, acc, ALU.mult, ALU.add)
                            ins.then_inc(conv_step, 1)

                def convolve_tile(j, b, e2):
                    steps = 16 + 192 * l + 8 * j + 4 * e2
                    dve.wait_ge(wide_free, WIDE0 + L_WIDE * l + j + 3)
                    acc = conv_out[:, j, e2 * S:(e2 + 1) * S]
                    for n, tap in enumerate((3, 2, 1, 0)):
                        src, wt = XPAD[:, b, e2, tap:tap + S], w3[:, j, 4 * e2 + tap:4 * e2 + tap + 1]
                        if n == 0:
                            ins = nc.vector.tensor_scalar(acc, src, wt, b3[:, j, e2:e2 + 1], ALU.mult, ALU.add)
                        else:
                            dve.wait_ge(conv_step, steps + n)
                            ins = nc.vector.scalar_tensor_tensor(acc, src, wt, acc, ALU.mult, ALU.add)
                        ins.then_inc(conv_step, 1)

                with dve.Fori(0, (L_CONV - SCAN_CONV) // ROUND) as r:
                    for i in range(ROUND):
                        split(Q_LAYERS + LQ_WIDE + i + PARTS, rounds + r)
                        convolve(ROUND * r + i, i % 2)

                dve.wait_ge(cum_done, l + 1)
                need(step(nc.vector.tensor_copy(CUM[:, :], bank[6][:, 0:160])))
                nc.vector.tensor_tensor(END_A, LAST_A, CUM_A[:, 0, :], ALU.subtract)
                nc.vector.tensor_tensor(END_G, LAST_G, CUM_G, ALU.subtract)
                nc.vector.tensor_copy(BEG, CUM_G)
                nc.vector.tensor_copy(EXP_C, LAST_C).then_inc(cum_copied, 1)
                dve.wait_ge(ecum_ready, l + 1)
                dve.wait_ge(beta_ready, l + 1)
                step(nc.vector.tensor_tensor(BEG, BEG, BETA[:, :, :], ALU.mult))

                for t in range(2):
                    for q in range(4):
                        dve.wait_ge(xtok_done, 8 * l + 4 * t + q + 1)
                        nc.vector.tensor_tensor(tiles(XDT[:, t, q * 512:(q + 1) * 512], 8), tiles(bank[q][:, :], 8),
                                                spread(SPL[:, t, 8 * q:8 * q + 8], HD), ALU.mult).then_inc(xdt_ready, 1)
                for t in range(2):
                    dve.wait_ge(cb_done, 2 * l + t + 1)
                    nc.vector.tensor_tensor(tiles(CBM[:, t, :], 4), tiles(bank[6 + t][:, :], 4), each(con("cum128"), 4),
                                            ALU.mult).then_inc(cbm_ready, 1)
                dve.wait_ge(cbm_ready, 2 * l + 2)

                def segment(i):
                    t, h0 = i // 8, i % 8 * 4
                    dve.wait_ge(seg_done, 16 * l + i + 1)
                    seg = tiles(SEG[:, i % 2, :], 4)
                    nc.vector.tensor_tensor(seg, tiles(bank[i % 2][:, :], 4), spread(CUM_A[:, t, h0:h0 + 4], P),
                                            ALU.subtract).then_inc(seg_taken, 1)
                    dve.wait_ge(seg_taken, 16 * l + i + 1)
                    nc.vector.tensor_scalar(SEG[:, i % 2, :], SEG[:, i % 2, :], 0.0, None, ALU.min).then_inc(seg_ready, 1)

                def mix(i):
                    t, g = i // 8, i % 8 // 2
                    dve.wait_ge(decay_ready, 16 * l + i + 1)
                    if i >= 2:
                        dve.wait_ge(y_done, 16 * l + i - 1)
                    nc.vector.tensor_tensor(tiles(MIX[:, i % 2, :], 4), tiles(SEG[:, i % 2, :], 4),
                                            each(CBM[:, t, g * P:(g + 1) * P], 4), ALU.mult).then_inc(mix_ready, 1)
                    if t == 1:
                        dve.wait_ge(row_exp_ready, 8 * l + i - 7)
                        nc.vector.tensor_tensor(tiles(CDEC[:, i % 2, :], 4), tiles(CDEC[:, i % 2, :], 4),
                                                each(CONV[:, C_TILE + g, P:2 * P], 4), ALU.mult).then_inc(cdec_ready, 1)

                def scan_out(m):
                    t, g = m // 4, m % 4
                    tok = slice(t * P, (t + 1) * P)
                    dve.wait_ge(y_done, 16 * l + 2 * m + 2)
                    for e2 in range(4):
                        x_ = CONV[:, 4 * g + e2, tok]
                        ins = nc.vector.scalar_tensor_tensor(x_, x_, pk2("ssm_d", 4 * g + e2),
                                                             bank[2 + m % 2][:, e2 * P:(e2 + 1) * P], ALU.mult, ALU.add)
                    ins.then_inc(y_taken, 1)

                segment(0)
                for i in range(16):
                    if i + 1 < 16:
                        segment(i + 1)
                    mix(i)
                    if i % 2 == 0 and i >= 2:
                        scan_out(i // 2 - 1)
                    for p, at in enumerate((-2,) + SCAN_SLOTS):
                        if 3 <= i - at <= 4:
                            convolve_tile(L_CONV - SCAN_CONV + p, p % 2, i - at - 3)
                scan_out(7)
                def group_norm(g):
                    dve.wait_ge(yrms_ready, 4 * l + g + 1)
                    need(step(nc.vector.reciprocal(GRMS[:, g, :], GRMS[:, g, :])))
                    for e2 in range(4):
                        x_ = CONV[:, 4 * g + e2, :]
                        ins = nc.vector.scalar_tensor_tensor(x_, x_, pk2("ssm_norm", 4 * g + e2), GRMS[:, g, :],
                                                             ALU.mult, ALU.mult)
                    ins.then_inc(ys_ready, 1)

                def qk_reciprocal(i):
                    dve.wait_ge(qkrms_ready, 2 * l + i + 1)
                    cols = slice(8 * i, 8 * i + 8)
                    r_ = nc.vector.reciprocal(QR[:, :, cols], QROOT[:, :, cols])
                    if i == 1:
                        r_.then_inc(qkr_ready, 1)
                        return
                    need(step(r_))
                    nc.vector.tensor_scalar(QR[:, :, cols], QR[:, :, cols], P ** -0.5, None, ALU.mult).then_inc(qkr_ready, 1)

                def qk_norm(pr):
                    dve.wait_ge(qkb_done, 8 * l + pr + 1)
                    x_ = QKV[:, 2 * pr:2 * pr + 2, :]
                    nc.vector.tensor_tensor(x_, x_, tiles(bank[2 + pr % 2][:, :], 2), ALU.mult).then_inc(qk_ready, 1)

                dve.wait_ge(lo_ready, Q_LAYERS + LQ_WIDE + L_CONV + PARTS + L_PANELS * l)
                for j in range(L_ZS):
                    ahead(LQ_WIDE + L_CONV + j)
                    dve.wait_ge(wide_free, 2 + WIDE0 + L_WIDE * l + L_CONV + j + 1)
                    x_ = CONV[:, 2 * j:2 * j + 2, :]
                    nc.vector.tensor_tensor(x_, x_, tiles(ZT[:, j % 2, :], 2), ALU.mult).then_inc(yg_ready, 1)
                    if j in (3, 5):
                        qk_reciprocal((j - 3) // 2)
                    if j >= 4:
                        qk_norm(2 * j - 8)
                        qk_norm(2 * j - 7)

                def late_low(j):
                    ahead(LQ_WIDE + L_CONV + L_ZS + j)

                for t in range(2):
                    tok = slice(t * P, (t + 1) * P)
                    def keys_first():
                        for b in range(2):
                            at, hs = slice(512 * b, 512 * b + 512), slice(4 * b, 4 * b + 4)
                            dve.wait_ge(kv_done, 8 * l + 4 * t + b + 1)
                            src = tiles(bank[b][:, :], 4)
                            nc.vector.tensor_tensor(tiles(KBG[:, at], 4), src, spread(BEG[:, t, hs], P), ALU.mult)
                            nc.vector.tensor_tensor(tiles(KDEC[:, at], 4), src, spread(END_G[:, t, hs], P),
                                                    ALU.mult).then_inc(k_taken, 1)

                    def gseg(b):
                        n, at, hs = 4 * l + 2 * t + b, slice(512 * b, 512 * b + 512), slice(4 * b, 4 * b + 4)
                        dve.wait_ge(kk_done, n + 1)
                        need(step(nc.vector.tensor_tensor(tiles(DCY[:, at], 4), tiles(bank[KK_BANKS[b][0]][:, :], 4),
                                                          spread(CUM_G[:, t, hs], P), ALU.subtract)))
                        nc.vector.tensor_tensor(tiles(DCY[:, at], 4), tiles(DCY[:, at], 4), each(con("floor64"), 4),
                                                ALU.min).then_inc(gseg_ready, 1)

                    def weights(b):
                        n, at, hs = 4 * l + 2 * t + b, slice(512 * b, 512 * b + 512), slice(4 * b, 4 * b + 4)
                        _, rows_b, kk, _ = [bank[i] for i in KK_BANKS[b]]
                        dve.wait_ge(gdec_ready, n + 1)
                        need(step(nc.vector.tensor_tensor(MT[:, at], kk[:, :], DEC[:, at], ALU.mult)))
                        need(step(nc.vector.tensor_tensor(MT[:, at], MT[:, at], rows_b[:, :], ALU.mult)))
                        nc.vector.tensor_tensor(tiles(CS[:, at], 4), tiles(MT[:, at], 4), each(con("levels")[:, 0:P], 4),
                                                ALU.mult).then_inc(c0_ready, 1)

                    def first_inverse():
                        dve.wait_ge(c0_ready, 4 * l + 2 * t + 2)
                        nc.vector.tensor_tensor(tiles(TT[:, :], 8), each(con("ident"), 8), tiles(CS[:, :], 8), ALU.subtract)
                        for b in range(2):
                            at = slice(512 * b, 512 * b + 512)
                            dve.wait_ge(inv_u_done, 2 * (2 * l + t) * LEVELS + b + 1)
                            nc.vector.tensor_tensor(tiles(TI[:, at], 4), each(con("ident"), 4),
                                                    tiles(bank[6 + b][:, :], 4), ALU.subtract).then_inc(inv_ready, 1)

                    def query_weights(b):
                        at = slice(512 * b, 512 * b + 512)
                        nc.vector.tensor_tensor(AQK[:, at], bank[KK_BANKS[b][3]][:, :], DEC[:, at],
                                                ALU.mult).then_inc(aqk_ready, 1)

                    def decayed_queries(b):
                        n, hs = 4 * l + 2 * t + b, slice(4 * b, 4 * b + 4)
                        dve.wait_ge(grow_ready, n + 1)
                        nc.vector.tensor_tensor(QKV[:, hs, tok], QKV[:, hs, tok], tiles(GROW[b][:, :], 4),
                                                ALU.mult).then_inc(qd_ready, 1)

                    if t == 0:
                        keys_first()
                        gseg(0)
                    else:
                        gseg(0)
                        keys_first()
                    weights(0)
                    gseg(1)
                    weights(1)
                    first_inverse()
                    query_weights(1)
                    query_weights(0)
                    decayed_queries(0)
                    decayed_queries(1)
                    for v in range(1, LEVELS):
                        k = (2 * l + t) * LEVELS + v
                        kc = (2 * l + t) * (LEVELS - 1) + v - 1
                        for b in range(2):
                            at = slice(512 * b, 512 * b + 512)
                            dve.wait_ge(inv_ready, 2 * k + b - 1)
                            dve.wait_ge(inv_v_done, 2 * kc + b + 1)
                            if v < LEVELS - 1:
                                nc.vector.tensor_tensor(TI[:, at], TI[:, at], bank[2 + b][:, :], ALU.subtract)
                            nc.vector.tensor_tensor(TT[:, at], TT[:, at], bank[6 + b][:, :],
                                                    ALU.subtract).then_inc(inv_ready, 1)
                        late = late_panel(t, f"level{v - 1}")
                        if late is not None:
                            late_low(late)
                        if t == 0 and 1 <= v <= GROUPS:
                            group_norm(v - 1)
                    for c in range(2):
                        cg, r0 = 2 * t + c, t * P + 64 * c
                        dve.wait_ge(o_done, 4 * l + cg + 1)
                        nc.vector.tensor_copy(QKV[:, 0:DN_HEADS, r0:r0 + 64],
                                              tiles(bank[6][:, :], 8)).then_inc(o_copied, 1)
                        for b in range(2 if cg < 3 else 0):
                            at = slice(512 * b, 512 * b + 512)
                            if cg >= 1:
                                need(step(nc.vector.tensor_tensor(tiles(ST[:, at], 4), tiles(ST[:, at], 4),
                                                                  spread(EXP_C[:, cg, 4 * b:4 * b + 4], P), ALU.mult)))
                            dve.wait_ge(st_done, 6 * l + 2 * cg + b + 1)
                            if cg >= 1:
                                nc.vector.tensor_tensor(ST[:, at], ST[:, at], bank[b][:, :],
                                                        ALU.add).then_inc(st_ready, 1)
                            else:
                                nc.vector.tensor_copy(ST[:, at], bank[b][:, :]).then_inc(st_ready, 1)
                        if c == 1:
                            late_low(late_panel(t, "chunk0"))
                    late_low(late_panel(t, "chunk1"))
                def branch_low(i, low, high, x_):
                    dve.wait_ge(branch_hi, 12 * l + i + 1)
                    nc.vector.tensor_tensor(low, x_, high.bitcast(F32), ALU.subtract).then_inc(branch_lo, 1)

                for j in range(8):
                    at = slice(2 * j, 2 * j + 2)
                    branch_low(j, YSL[:, at, :], YSH[:, at, :], CONV[:, at, :])
                    if j == 3:
                        late_low(L_ZD + L_GATES - LATE_GATES)
                dve.wait_ge(orms_ready, l + 1)
                nc.vector.reciprocal(QR[:, :, 0:8], QROOT[:, :, 0:8]).then_inc(or_ready, 1)
                late_low(L_ZD + L_GATES - LATE_GATES + 1)
                for j in range(4):
                    dve.wait_ge(ob_done, 4 * l + j + 1)
                    x_ = QKV[:, 2 * j:2 * j + 2, :]
                    need(step(nc.vector.scalar_tensor_tensor(x_, x_, pk2("dn_norm"), tiles(bank[O_BANKS[j]][:, :], 2), ALU.mult,
                                                             ALU.mult)))
                    nc.vector.tensor_tensor(x_, x_, ZD[:, 2 * j:2 * j + 2, :], ALU.mult).then_inc(yd_ready, 1)
                for j in range(2, LATE_GATES):
                    late_low(L_ZD + L_GATES - LATE_GATES + j)
                for j in range(4):
                    at = slice(2 * j, 2 * j + 2)
                    branch_low(8 + j, YDL[:, at, :], YDH[:, at, :], QKV[:, at, :])

                dve.wait_ge(wide_free, 2 + WIDE0 + L_WIDE * l + L_WIDE)
                for j in range(3):
                    ahead(LQ_PROJ + j)
                for c in range(4):
                    dve.wait_ge(panel_used, used0 + LQ_PROJ + 3 * c + 2)
                    merge_first(c, bank[c % 2 * 2], GT[:, 0:8, :], SG[:, c % 2, :])
                    dve.wait_ge(panel_used, used0 + LQ_PROJ + 3 * (c + 1))
                    merge(c, 4 + 4 * l, bank[c % 2 * 2 + 1], GT[:, 8:16, :], SG[:, c % 2, :])
                    for j in range(3 * c + 3, min(3 * c + 6, L_PROJ - 1)):
                        ahead(LQ_PROJ + j)
                    fill_low(fill + 2, c)
                ahead(LQ_PROJ + L_PROJ - 1)
                for j in range(L_WOUT):
                    dve.wait_ge(panel_used, used0 + LQ_WOUT + j + 1)
                    residual(j, bank[6 + j % 2][:, :], 1.0)
                    if j < L_WOUT - 1:
                        ahead(LQ_WOUT + j)
                dve.wait_ge(residual_ready, 4 * (4 + 3 * l))
                norm(4 + 3 * l, fill + 3, pk2("ffn2", 0, 8))
                pool_split(Q_LAYERS + LQ_FFN2 + 1, rounds)
                ffn_hidden(2 + 2 * l, Q_LAYERS + LQ_FFN2, rounds)
                for j in range(4):
                    dve.wait_ge(*ffn_out(j, 2 + 2 * l, used0 + L_PANELS))
                    residual(j, bank[j][:, :], 0.5)
                dve.wait_ge(residual_ready, 4 * (5 + 3 * l))
                pad(DVE_LAYER)
            base[0] = DVE_B1 + DVE_LAYER * LAYERS
            norm(2 + 3 * LAYERS, None, pk1("final", 0, 8))


def _wide_panels(w):
    n = w.shape[1] // 256
    return w.reshape(KT, P, n, 256).transpose(2, 1, 0, 3).reshape(n, P, PANEL)


def _ffn_panels(w_in, w_out):
    gu = w_in.reshape(KT, P, 2, 2 * HID_PAIRS, P).transpose(3, 1, 0, 2, 4).reshape(2 * HID_PAIRS, P, PANEL)
    dn = w_out.reshape(HID_PAIRS, 2, P, D).transpose(0, 2, 1, 3).reshape(HID_PAIRS, P, PANEL)
    order = [gu[0], gu[1]]
    for i in range(HID_PAIRS):
        if i + 1 < HID_PAIRS:
            order += [gu[2 * i + 2], gu[2 * i + 3]]
        order.append(dn[i])
    return np.stack(order)


def _columns_of(v):
    return v.reshape(-1, P).T


def _pack(layout, width, parts):
    out = np.zeros((P, width), np.float32)
    for name, part in parts.items():
        a, b = layout[name]
        out[:, a:b] = part
    return out


def _constants():
    i = np.arange(P)
    s, l = i[:, None], i[None, :]
    same = s // 64 == l // 64
    parts = {
        "ident": s == l, "cum128": s <= l, "cum64": same & (s <= l), "floor64": np.where(same & (s <= l), 0.0, NEG), "same64": same,
        "half0": (s < 64) & (l >= 0), "half1": (s >= 64) & (l >= 0),
    }
    levels = []
    for v in range(LEVELS):
        n = 1 << v
        levels.append((s // (2 * n) == l // (2 * n)) & (s // n % 2 == 0) & (l // n % 2 == 1))
    parts["levels"] = np.concatenate(levels, 1)
    return _pack(CONSTS, CONSTS_N, parts)


def _rope_constants():
    i = np.arange(P)
    half = HD // 8
    inv = np.float32(500000.0) ** (-(np.arange(half, dtype=np.float32) * np.float32(2.0)) / np.float32(2 * half))
    ang = np.arange(S, dtype=np.float32)[:, None] * inv[None, :]
    cos, sin = np.ones((P, S), np.float32), np.zeros((P, S), np.float32)
    swap = np.zeros((P, P), np.float32)
    for at in (0, HD):
        for d in range(half):
            cos[at + d] = cos[at + half + d] = np.cos(ang[:, d])
            sin[at + d] = sin[at + half + d] = np.sin(ang[:, d])
            swap[at + half + d, at + d] = -1.0
            swap[at + d, at + half + d] = 1.0
    q, k = np.arange(S)[:, None], np.arange(S)[None, :]
    masks = []
    for window, dil in ((128, 1), (512, 4), (2048, 16)):
        seen = (np.abs(q - k) % dil == 0) & (np.abs(q - k) // dil <= window // 2 // dil)
        masks.append(np.where(seen, 0.0, NEG))
    dil_masks = np.stack(masks).reshape(DIL_GROUPS, 2, P, S).transpose(2, 1, 0, 3).reshape(P, -1)
    return _pack(ROPES, ROPES_N, {"swap": swap, "cos": cos,
                                  "sin": sin, "dil": dil_masks})


def _na_bias(rpb):
    rows = S // GRID_W
    kh = min(NA_KH, rows)
    pos = np.arange(S)
    r, c = pos // GRID_W, pos % GRID_W
    assert kh == rows
    row_off = r[None, :] - r[:, None] + NA_KH - 1
    start = np.clip(c - NA_KW // 2, 0, GRID_W - NA_KW)
    seen = (c[None, :] >= start[:, None]) & (c[None, :] < start[:, None] + NA_KW)
    col_off = np.clip(c[None, :] - c[:, None] + NA_KW - 1, 0, 2 * NA_KW - 2)
    flat = np.concatenate([rpb.reshape(NA_HEADS, -1), np.full((NA_HEADS, 1), NEG, np.float32)], 1)
    at = np.where(seen, row_off * (2 * NA_KW - 1) + col_off, flat.shape[1] - 1)
    return flat[:, at].reshape(NA_HEADS, 2, P, S).transpose(2, 0, 1, 3).reshape(P, NA_UNITS * S)


def _layout(a):
    w_in = a["w_in"][0]
    wa, wb = 512, 768
    qa, ka, va, qb, kb, vb, gates = np.split(w_in, np.cumsum([wa, wa, wa, wb, wb, wb]), axis=1)
    wpa = a["w_proj_a"][0].reshape(4, P, 2, 512).transpose(2, 1, 0, 3).reshape(2, P, PANEL)
    wpb = a["w_proj_b"][0].reshape(2, P, D).transpose(1, 0, 2).reshape(1, P, PANEL)
    qk_gates = _wide_panels(np.concatenate([qa, ka, qb, kb, gates], 1))
    stream = [qk_gates[:B1_WIDE], _wide_panels(np.concatenate([va, vb], 1)), qk_gates[B1_WIDE:], wpa, wpb, _wide_panels(a["w_o"][0]),
              _ffn_panels(a["w_ffn_in"][0], a["w_ffn_out"][0])]
    packs = []
    for l in range(LAYERS):
        stream.append(_ffn_panels(a["ffn1_w_in_2"][l], a["ffn1_w_out_2"][l]))
        z, xbc, dt, qkv, zd, b_, a_, gs, gd = np.split(
            a["w_in_2"][l], np.cumsum([2048, 3072, 32, 3072, 1024, 8, 8, 1024]), axis=1)
        stream.append(_wide_panels(np.concatenate([xbc, qkv, z, zd, gs, gd], 1)))
        ssm = _wide_panels(a["ssm_w_branch_2"][l][:D]), _wide_panels(a["ssm_w_branch_2"][l][D:])
        dn = _wide_panels(a["dn_w_branch_2"][l])
        stream.append(np.stack([x for c in range(4) for x in (ssm[0][c], ssm[1][c], dn[c])]))
        stream.append(_wide_panels(a["w_out_2"][l]))
        stream.append(_ffn_panels(a["ffn2_w_in_2"][l], a["ffn2_w_out_2"][l]))
        conv_w = np.concatenate([a["ssm_conv_w_2"][l], a["dn_conv_w_2"][l]], 1)
        small_w = np.concatenate([dt, a_, b_], 1).reshape(KT, P, SMALL).transpose(1, 0, 2).reshape(P, KT * SMALL)
        packs.append(_pack(PACK2, PACK2_N, {
            "ffn1": _columns_of(a["ffn1_norm_2"][l]), "mix": _columns_of(a["mix_norm_2"][l]),
            "ffn2": _columns_of(a["ffn2_norm_2"][l]),
            "conv_w": conv_w.reshape(4, CONV_TILES, P).transpose(2, 1, 0).reshape(P, 4 * CONV_TILES),
            "conv_b": np.concatenate([_columns_of(a["ssm_conv_b_2"][l]), np.zeros((P, QKV_TILES), np.float32)], 1),
            "ssm_norm": _columns_of(a["ssm_norm_2"][l]), "ssm_d": _columns_of(np.repeat(a["ssm_d_2"][l], HD)),
            "dn_norm": _columns_of(a["dn_norm_2"][l]),
            "small_b": np.concatenate([a["ssm_dt_bias_2"][l], a["dn_dt_bias_2"][l], np.zeros(8, np.float32)]),
            "a_log": np.concatenate([a["ssm_a_log_2"][l], a["dn_a_log_2"][l]]), "small_w": small_w}))
    two = lambda g: np.concatenate([g, g])[:, None]
    pack1 = _pack(PACK1, PACK1_N, {
        "c": _columns_of(a["c"][0]), "b_ada": _columns_of(a["b_ada"][0]), "g1": _columns_of(a["g_norm1"][0]),
        "g2": _columns_of(a["g_norm2"][0]), "b_gate": _columns_of(a["b_gate"][0]),
        "final": _columns_of(a["final_norm_2"]), "g_qa": two(a["g_qa"][0]), "g_ka": two(a["g_ka"][0]),
        "g_qb": two(a["g_qb"][0]), "g_kb": two(a["g_kb"][0])})
    return {
        "w_stream": np.concatenate(stream), "ada_stream": _wide_panels(a["w_ada"][0]),
        "x_t": a["x"][0].T.reshape(KT, P, S).transpose(1, 0, 2),
        "pack1": pack1, "pack2": np.stack(packs), "consts": _constants(), "ropes": _rope_constants(),
        "na_bias": _na_bias(a["rpb"][0])}


def kernel(**inputs):
    import concourse.bacc as bacc
    from concourse.bass_utils import run_bass_kernel_spmd

    laid = {k: np.ascontiguousarray(v, np.float32) for k, v in _layout({k: np.asarray(v) for k, v in inputs.items()}).items()}
    nc = bacc.Bacc("TRN2", target_bir_lowering=False, num_devices=1)
    args = {k: nc.dram_tensor(f"in_{k}", v.shape, F32, kind="ExternalInput").ap() for k, v in laid.items()}
    args["out_t"] = nc.dram_tensor("out_t", (P, KT, S), F32, kind="ExternalOutput").ap()
    build_program(nc, **args)
    r = run_bass_kernel_spmd(nc, [{f"in_{k}": v for k, v in laid.items()}], core_ids=[0])
    out = r.results[0]["out_t"]
    return out.transpose(1, 0, 2).reshape(D, S).T[None]
```
